# Optimizing a Trainium2 kernel written in Bass

```python
import math
import jax, jax.numpy as jnp
from jax import lax
import numpy as np

D_MODEL = 1024
BATCH = 1
SEQ = 256
DEPTH = 2

N_BRANCH = 4
BRANCH_W = 512
NORM_EPS = 1e-6
LRU_HEADS = 8
LRU_HD = BRANCH_W // LRU_HEADS
CONV_W = 4
LRU_C = 8.0
S5_GROUP = 16
S5_GROUPS = BRANCH_W // S5_GROUP
S5_STATE = 64
RET_HEADS = 4
RET_HD = BRANCH_W // RET_HEADS
RET_CHUNK = 128
RET_ROPE_BASE = 10000.0
NSA_HEADS = 8
NSA_KV_HEADS = 2
NSA_HD = BRANCH_W // NSA_HEADS
NSA_GQA = NSA_HEADS // NSA_KV_HEADS
CMP_LEN = 32
CMP_STRIDE = 16
CMP_HIDDEN = 256
SLC_BLOCK = 64
SLC_TOPK = 16
WIN = 512
Q_BLOCK = 128
ROPE_THETA = 500000.0
ROPE_DIM = NSA_HD // 4
FORCE_SCORE = 1e4
NEG = -1e30
NSA_KV_W = 6 * NSA_KV_HEADS * NSA_HD
IN_SIZES = (BRANCH_W, BRANCH_W, 3 * BRANCH_W, NSA_HEADS * NSA_HD, NSA_KV_W, 3 * NSA_HEADS,
            N_BRANCH * BRANCH_W, N_BRANCH * D_MODEL)
D_IN = sum(IN_SIZES)

kernel_name = 'hybrid_lru_s5_retention_nsa_block'

def rms_norm(x, g):
    xf = x.astype(jnp.float32)
    y = xf * lax.rsqrt(jnp.mean(xf * xf, axis=-1, keepdims=True) + NORM_EPS)
    return (y * g.astype(jnp.float32)).astype(x.dtype)

def split_columns(p, sizes):
    outs, off = [], 0
    for n in sizes:
        outs.append(p[..., off:off + n])
        off += n
    return outs

def rope_half(x, pos, base, rot_dim):
    half = rot_dim // 2
    inv = base ** (-jnp.arange(half, dtype=jnp.float32) * 2.0 / rot_dim)
    ang = pos.astype(jnp.float32)[:, None] * inv[None, :]
    cos = jnp.cos(ang)[:, None, :]
    sin = jnp.sin(ang)[:, None, :]
    xf = x.astype(jnp.float32)
    x1 = xf[..., :half]
    x2 = xf[..., half:rot_dim]
    out = jnp.concatenate([x1 * cos - x2 * sin, x2 * cos + x1 * sin, xf[..., rot_dim:]], axis=-1)
    return out.astype(x.dtype)

def masked_softmax(s, mask):
    s = jnp.where(mask, s, NEG)
    p = jax.nn.softmax(s, axis=-1)
    return jnp.where(mask, p, 0.0)

def causal_depthwise_conv(x, w, b):
    c = x.shape[-1]
    y = lax.conv_general_dilated(x, w[:, None, :].astype(x.dtype), window_strides=(1,),
                                 padding=((CONV_W - 1, 0),), dimension_numbers=('NWC', 'WIO', 'NWC'),
                                 feature_group_count=c)
    return y + b

def rg_lru_mixer(u, conv_w, conv_b, wa, ba, wx, bx, lam):
    bsz, s, w = u.shape
    xc = causal_depthwise_conv(u, conv_w, conv_b)
    xh = xc.reshape(bsz, s, LRU_HEADS, LRU_HD)
    r = jax.nn.sigmoid((jnp.einsum('bshi,hij->bshj', xh, wa).reshape(bsz, s, w) + ba).astype(jnp.float32))
    i = jax.nn.sigmoid((jnp.einsum('bshi,hij->bshj', xh, wx).reshape(bsz, s, w) + bx).astype(jnp.float32))
    log_a = -LRU_C * r * jax.nn.softplus(-lam.astype(jnp.float32))
    a = jnp.exp(log_a)
    mult = jnp.sqrt(-jnp.expm1(2.0 * log_a))
    bterm = mult * i * xc.astype(jnp.float32)

    def op(l, r_):
        a1, b1 = l
        a2, b2 = r_
        return a1 * a2, a2 * b1 + b2

    _, h = lax.associative_scan(op, (a, bterm), axis=1)
    return h.astype(u.dtype)

def s5_mixer(u, lam_re, lam_im, b_re, b_im, c_re, c_im, log_dt, d_skip, w_glu, b_glu):
    bsz, s, w = u.shape
    f32 = jnp.float32
    uf = u.astype(f32).reshape(bsz, s, S5_GROUPS, S5_GROUP)
    dt = jnp.exp(log_dt.astype(f32))[:, None]
    lr = jnp.minimum(lam_re.astype(f32), -1e-4)
    li = lam_im.astype(f32)
    mag = jnp.exp(lr * dt)
    ab_re = mag * jnp.cos(li * dt)
    ab_im = mag * jnp.sin(li * dt)
    den = lr * lr + li * li
    nr = ab_re - 1.0
    ni = ab_im
    f_re = (nr * lr + ni * li) / den
    f_im = (ni * lr - nr * li) / den
    br = b_re.astype(f32)
    bi = b_im.astype(f32)
    bb_re = f_re[..., None] * br - f_im[..., None] * bi
    bb_im = f_re[..., None] * bi + f_im[..., None] * br
    x_re = jnp.einsum('bsgc,gpc->bsgp', uf, bb_re)
    x_im = jnp.einsum('bsgc,gpc->bsgp', uf, bb_im)
    a_re = jnp.broadcast_to(ab_re, x_re.shape)
    a_im = jnp.broadcast_to(ab_im, x_im.shape)

    def op(l, r_):
        ar1, ai1, br1, bi1 = l
        ar2, ai2, br2, bi2 = r_
        return (ar2 * ar1 - ai2 * ai1, ar2 * ai1 + ai2 * ar1,
                ar2 * br1 - ai2 * bi1 + br2, ar2 * bi1 + ai2 * br1 + bi2)

    _, _, h_re, h_im = lax.associative_scan(op, (a_re, a_im, x_re, x_im), axis=1)
    y = (jnp.einsum('bsgp,gcp->bsgc', h_re, c_re.astype(f32))
         - jnp.einsum('bsgp,gcp->bsgc', h_im, c_im.astype(f32)))
    y = y.reshape(bsz, s, w) + d_skip.astype(f32) * u.astype(f32)
    z = jax.nn.gelu(y).astype(u.dtype)
    g = jnp.einsum('bsw,wv->bsv', z, w_glu) + b_glu
    return (g[..., :w] * jax.nn.sigmoid(g[..., w:])).astype(u.dtype)

def retention_mixer(q, k, v):
    bsz, s, nh, dh = q.shape
    f32 = jnp.float32
    pos = jnp.arange(s)
    q = rope_half(q, pos, RET_ROPE_BASE, dh).astype(f32)
    k = rope_half(k, pos, RET_ROPE_BASE, dh).astype(f32) * (dh ** -0.5)
    v = v.astype(f32)
    gamma = 1.0 - jnp.exp(jnp.linspace(math.log(1.0 / 32.0), math.log(1.0 / 512.0), nh, dtype=f32))
    log_g = jnp.log(gamma)
    c = RET_CHUNK
    nc = s // c
    n = jnp.arange(c, dtype=f32)
    diff = n[:, None] - n[None, :]
    dmask = jnp.where(diff[None] >= 0, jnp.exp(jnp.maximum(diff, 0.0)[None] * log_g[:, None, None]), 0.0)
    xi = jnp.exp((n[None, :] + 1.0) * log_g[:, None])
    zeta = jnp.exp((c - 1.0 - n)[None, :] * log_g[:, None])
    chunk_decay = jnp.exp(c * log_g)
    qc = q.reshape(bsz, nc, c, nh, dh)
    kc = k.reshape(bsz, nc, c, nh, dh)
    vc = v.reshape(bsz, nc, c, nh, dh)
    scores = jnp.einsum('bcihd,bcjhd->bchij', qc, kc) * dmask[None, None]
    inner = jnp.einsum('bchij,bcjhe->bcihe', scores, vc)
    kv = jnp.einsum('bcjhd,hj,bcjhe->bchde', kc, zeta, vc)

    def step(r_state, kv_c):
        return chunk_decay[None, :, None, None] * r_state + kv_c, r_state

    _, r_prev = lax.scan(step, jnp.zeros((bsz, nh, dh, dh), f32), jnp.moveaxis(kv, 1, 0))
    r_prev = jnp.moveaxis(r_prev, 0, 1)
    cross = jnp.einsum('bcihd,hi,bchde->bcihe', qc, xi, r_prev)
    o = (inner + cross).reshape(bsz, s, nh, dh)
    mu = jnp.mean(o, axis=-1, keepdims=True)
    var = jnp.mean(jnp.square(o - mu), axis=-1, keepdims=True)
    o = (o - mu) * lax.rsqrt(var + 1e-5)
    return o.reshape(bsz, s, nh * dh)

def compress_blocks(kraw, pos_emb, w1, w2):
    bsz, s, hkv, dh = kraw.shape
    ncmp = (s - CMP_LEN) // CMP_STRIDE + 1
    idx = jnp.arange(ncmp)[:, None] * CMP_STRIDE + jnp.arange(CMP_LEN)[None, :]
    blocks = kraw[:, idx] + pos_emb[None, None, :, None, :]
    flat = jnp.moveaxis(blocks, 3, 2).reshape(bsz, ncmp, hkv, CMP_LEN * dh)
    hid = jax.nn.gelu(jnp.einsum('bnhf,fk->bnhk', flat, w1))
    return jnp.einsum('bnhk,kd->bnhd', hid, w2)

def nsa_mixer(q, k_cr, v_cr, k_slc, v_slc, k_win, v_win, bgate, pos_k, pos_v, ck_w1, ck_w2, cv_w1, cv_w2):
    bsz, s, hq, dh = q.shape
    hkv = NSA_KV_HEADS
    f32 = jnp.float32
    pos = jnp.arange(s)
    q = rope_half(q, pos, ROPE_THETA, ROPE_DIM)
    k_slc = rope_half(k_slc, pos, ROPE_THETA, ROPE_DIM)
    k_win = rope_half(k_win, pos, ROPE_THETA, ROPE_DIM)
    k_cmp = compress_blocks(k_cr, pos_k, ck_w1, ck_w2)
    v_cmp = compress_blocks(v_cr, pos_v, cv_w1, cv_w2)
    ncmp = k_cmp.shape[1]
    cmp_end = jnp.arange(ncmp) * CMP_STRIDE + CMP_LEN - 1
    k_cmp = rope_half(k_cmp, cmp_end, ROPE_THETA, ROPE_DIM)
    nsel = s // SLC_BLOCK
    topk = min(SLC_TOPK, nsel)
    cmp_tok_blk = (jnp.arange(ncmp)[:, None] * CMP_STRIDE + jnp.arange(CMP_LEN)[None, :]) // SLC_BLOCK
    overlap = jnp.mean((cmp_tok_blk[..., None] == jnp.arange(nsel)).astype(f32), axis=1)
    k_blk = jnp.transpose(k_slc.reshape(bsz, nsel, SLC_BLOCK, hkv, dh), (0, 3, 1, 2, 4))
    v_blk = jnp.transpose(v_slc.reshape(bsz, nsel, SLC_BLOCK, hkv, dh), (0, 3, 1, 2, 4))
    k_win_p = jnp.pad(k_win, ((0, 0), (WIN, 0), (0, 0), (0, 0)))
    v_win_p = jnp.pad(v_win, ((0, 0), (WIN, 0), (0, 0), (0, 0)))
    nqb = s // Q_BLOCK
    qg = q.reshape(bsz, nqb, Q_BLOCK, hkv, NSA_GQA, dh)
    gates = jax.nn.sigmoid(bgate.astype(f32)).reshape(bsz, nqb, Q_BLOCK, 3, hkv, NSA_GQA)
    scale = dh ** -0.5
    b_ix = jnp.arange(bsz)[:, None, None, None]
    h_ix = jnp.arange(hkv)[None, :, None, None]
    blk_id = jnp.arange(nsel)
    wlen = WIN + Q_BLOCK

    def block_fn(args):
        qb, gb, blk = args
        t = blk * Q_BLOCK + jnp.arange(Q_BLOCK)
        s_c = jnp.einsum('bqhgd,bnhd->bhgqn', qb, k_cmp).astype(f32) * scale
        p_c = masked_softmax(s_c, cmp_end[None, :] <= t[:, None])
        o_c = jnp.einsum('bhgqn,bnhd->bqhgd', p_c.astype(v_cmp.dtype), v_cmp)
        imp = jnp.einsum('bhgqn,nj->bhqj', p_c, overlap)
        cur = t // SLC_BLOCK
        valid = blk_id[None, :] <= cur[:, None]
        forced = (blk_id[None, :] == 0) | (blk_id[None, :] == cur[:, None]) | (blk_id[None, :] == cur[:, None] - 1)
        score = jnp.where(valid, jnp.where(forced, FORCE_SCORE, imp), -1.0)
        top_val, top_idx = lax.top_k(score, topk)
        sel_ok = top_val >= 0.0
        kg = k_blk[b_ix, h_ix, top_idx].reshape(bsz, hkv, Q_BLOCK, topk * SLC_BLOCK, dh)
        vg = v_blk[b_ix, h_ix, top_idx].reshape(bsz, hkv, Q_BLOCK, topk * SLC_BLOCK, dh)
        kpos = (top_idx[..., None] * SLC_BLOCK + jnp.arange(SLC_BLOCK)).reshape(bsz, hkv, Q_BLOCK, topk * SLC_BLOCK)
        m_s = jnp.repeat(sel_ok, SLC_BLOCK, axis=-1) & (kpos <= t[None, None, :, None])
        s_s = jnp.einsum('bqhgd,bhqkd->bhgqk', qb, kg).astype(f32) * scale
        p_s = masked_softmax(s_s, m_s[:, :, None])
        o_s = jnp.einsum('bhgqk,bhqkd->bqhgd', p_s.astype(vg.dtype), vg)
        start = blk * Q_BLOCK
        kw = lax.dynamic_slice_in_dim(k_win_p, start, wlen, axis=1)
        vw = lax.dynamic_slice_in_dim(v_win_p, start, wlen, axis=1)
        wpos = start - WIN + jnp.arange(wlen)
        m_w = (wpos[None, :] <= t[:, None]) & (wpos[None, :] > t[:, None] - WIN) & (wpos[None, :] >= 0)
        s_w = jnp.einsum('bqhgd,bkhd->bhgqk', qb, kw).astype(f32) * scale
        p_w = masked_softmax(s_w, m_w)
        o_w = jnp.einsum('bhgqk,bkhd->bqhgd', p_w.astype(vw.dtype), vw)
        out = (gb[:, :, 0][..., None] * o_c + gb[:, :, 1][..., None] * o_s + gb[:, :, 2][..., None] * o_w)
        return out.astype(q.dtype)

    outs = lax.map(block_fn, (jnp.moveaxis(qg, 1, 0), jnp.moveaxis(gates, 1, 0), jnp.arange(nqb)))
    return jnp.moveaxis(outs, 0, 1).reshape(bsz, s, hq * dh)

def hybrid_layer(x, norm_g, w_in, lru_conv_w, lru_conv_b, lru_wa, lru_ba, lru_wx, lru_bx, lru_lambda,
                 s5_lambda_re, s5_lambda_im, s5_b_re, s5_b_im, s5_c_re, s5_c_im, s5_log_dt, s5_d,
                 s5_w_glu, s5_b_glu, nsa_pos_k, nsa_pos_v, nsa_ck_w1, nsa_ck_w2, nsa_cv_w1, nsa_cv_w2,
                 w_branch, w_out):
    bsz, s, d = x.shape
    h = rms_norm(x, norm_g)
    proj = jnp.einsum('bsd,de->bse', h, w_in)
    u_lru, u_s5, qkv_ret, q_nsa, kv_nsa, bg_nsa, gate_paths, merge = split_columns(proj, IN_SIZES)
    y_lru = rg_lru_mixer(u_lru, lru_conv_w, lru_conv_b, lru_wa, lru_ba, lru_wx, lru_bx, lru_lambda)
    y_s5 = s5_mixer(u_s5, s5_lambda_re, s5_lambda_im, s5_b_re, s5_b_im, s5_c_re, s5_c_im,
                    s5_log_dt, s5_d, s5_w_glu, s5_b_glu)
    qkv = qkv_ret.reshape(bsz, s, 3, RET_HEADS, RET_HD)
    y_ret = retention_mixer(qkv[:, :, 0], qkv[:, :, 1], qkv[:, :, 2]).astype(x.dtype)
    kvs = kv_nsa.reshape(bsz, s, 6, NSA_KV_HEADS, NSA_HD)
    y_nsa = nsa_mixer(q_nsa.reshape(bsz, s, NSA_HEADS, NSA_HD), kvs[:, :, 0], kvs[:, :, 1], kvs[:, :, 2],
                      kvs[:, :, 3], kvs[:, :, 4], kvs[:, :, 5], bg_nsa, nsa_pos_k, nsa_pos_v,
                      nsa_ck_w1, nsa_ck_w2, nsa_cv_w1, nsa_cv_w2)
    ys = jnp.stack([y_lru, y_s5, y_ret, y_nsa.astype(x.dtype)], axis=2)
    ys = ys * jax.nn.silu(gate_paths.reshape(bsz, s, N_BRANCH, BRANCH_W))
    branch = jnp.einsum('bsnw,nwd->bsnd', ys, w_branch)
    merged = jnp.sum(jax.nn.sigmoid(merge.reshape(bsz, s, N_BRANCH, d)) * branch, axis=2)
    return x + jnp.einsum('bsd,de->bse', merged, w_out)

def setup_inputs(seed: int = 0) -> dict:
    key = jax.random.key(seed)
    ks = iter(jax.random.split(key, 40))
    f32 = jnp.float32

    def nrm(shape, scale):
        return jax.random.normal(next(ks), shape, f32) * scale

    W = BRANCH_W
    x = nrm((BATCH, SEQ, D_MODEL), 1.0)
    norm_g = 1.0 + nrm((DEPTH, D_MODEL), 0.01)
    w_in = nrm((DEPTH, D_MODEL, D_IN), D_MODEL ** -0.5)
    lru_conv_w = nrm((DEPTH, CONV_W, W), CONV_W ** -0.5)
    lru_conv_b = nrm((DEPTH, W), 0.01)
    lru_wa = nrm((DEPTH, LRU_HEADS, LRU_HD, LRU_HD), LRU_HD ** -0.5)
    lru_ba = nrm((DEPTH, W), 0.01)
    lru_wx = nrm((DEPTH, LRU_HEADS, LRU_HD, LRU_HD), LRU_HD ** -0.5)
    lru_bx = nrm((DEPTH, W), 0.01)
    a_c = jax.random.uniform(next(ks), (DEPTH, W), f32, minval=0.9, maxval=0.999)
    a0 = a_c ** (1.0 / LRU_C)
    lru_lambda = jnp.log(a0) - jnp.log1p(-a0)
    s5_lambda_re = -0.5 + nrm((DEPTH, S5_GROUPS, S5_STATE), 0.01)
    s5_lambda_im = (jnp.pi * jnp.arange(S5_STATE, dtype=f32))[None, None, :] + nrm((DEPTH, S5_GROUPS, S5_STATE), 0.01)
    s5_b_re = nrm((DEPTH, S5_GROUPS, S5_STATE, S5_GROUP), (2.0 * S5_GROUP) ** -0.5)
    s5_b_im = nrm((DEPTH, S5_GROUPS, S5_STATE, S5_GROUP), (2.0 * S5_GROUP) ** -0.5)
    s5_c_re = nrm((DEPTH, S5_GROUPS, S5_GROUP, S5_STATE), (2.0 * S5_STATE) ** -0.5)
    s5_c_im = nrm((DEPTH, S5_GROUPS, S5_GROUP, S5_STATE), (2.0 * S5_STATE) ** -0.5)
    s5_log_dt = jax.random.uniform(next(ks), (DEPTH, S5_GROUPS), f32, minval=math.log(0.001), maxval=math.log(0.1))
    s5_d = nrm((DEPTH, W), 1.0)
    s5_w_glu = nrm((DEPTH, W, 2 * W), W ** -0.5)
    s5_b_glu = nrm((DEPTH, 2 * W), 0.01)
    nsa_pos_k = nrm((DEPTH, CMP_LEN, NSA_HD), 0.02)
    nsa_pos_v = nrm((DEPTH, CMP_LEN, NSA_HD), 0.02)
    nsa_ck_w1 = nrm((DEPTH, CMP_LEN * NSA_HD, CMP_HIDDEN), (CMP_LEN * NSA_HD) ** -0.5)
    nsa_ck_w2 = nrm((DEPTH, CMP_HIDDEN, NSA_HD), CMP_HIDDEN ** -0.5)
    nsa_cv_w1 = nrm((DEPTH, CMP_LEN * NSA_HD, CMP_HIDDEN), (CMP_LEN * NSA_HD) ** -0.5)
    nsa_cv_w2 = nrm((DEPTH, CMP_HIDDEN, NSA_HD), CMP_HIDDEN ** -0.5)
    w_branch = nrm((DEPTH, N_BRANCH, W, D_MODEL), W ** -0.5)
    w_out = nrm((DEPTH, D_MODEL, D_MODEL), D_MODEL ** -0.5)
    final_norm_g = 1.0 + nrm((D_MODEL,), 0.01)
    return {'x': x, 'norm_g': norm_g, 'w_in': w_in, 'lru_conv_w': lru_conv_w, 'lru_conv_b': lru_conv_b,
            'lru_wa': lru_wa, 'lru_ba': lru_ba, 'lru_wx': lru_wx, 'lru_bx': lru_bx, 'lru_lambda': lru_lambda,
            's5_lambda_re': s5_lambda_re, 's5_lambda_im': s5_lambda_im, 's5_b_re': s5_b_re, 's5_b_im': s5_b_im,
            's5_c_re': s5_c_re, 's5_c_im': s5_c_im, 's5_log_dt': s5_log_dt, 's5_d': s5_d,
            's5_w_glu': s5_w_glu, 's5_b_glu': s5_b_glu, 'nsa_pos_k': nsa_pos_k, 'nsa_pos_v': nsa_pos_v,
            'nsa_ck_w1': nsa_ck_w1, 'nsa_ck_w2': nsa_ck_w2, 'nsa_cv_w1': nsa_cv_w1, 'nsa_cv_w2': nsa_cv_w2,
            'w_branch': w_branch, 'w_out': w_out, 'final_norm_g': final_norm_g}

def reference(x, norm_g, w_in, lru_conv_w, lru_conv_b, lru_wa, lru_ba, lru_wx, lru_bx, lru_lambda,
              s5_lambda_re, s5_lambda_im, s5_b_re, s5_b_im, s5_c_re, s5_c_im, s5_log_dt, s5_d,
              s5_w_glu, s5_b_glu, nsa_pos_k, nsa_pos_v, nsa_ck_w1, nsa_ck_w2, nsa_cv_w1, nsa_cv_w2,
              w_branch, w_out, final_norm_g):
    for l in range(DEPTH):
        x = hybrid_layer(x, norm_g[l], w_in[l], lru_conv_w[l], lru_conv_b[l], lru_wa[l], lru_ba[l],
                         lru_wx[l], lru_bx[l], lru_lambda[l], s5_lambda_re[l], s5_lambda_im[l],
                         s5_b_re[l], s5_b_im[l], s5_c_re[l], s5_c_im[l], s5_log_dt[l], s5_d[l],
                         s5_w_glu[l], s5_b_glu[l], nsa_pos_k[l], nsa_pos_v[l], nsa_ck_w1[l], nsa_ck_w2[l],
                         nsa_cv_w1[l], nsa_cv_w2[l], w_branch[l], w_out[l])
    return rms_norm(x, final_norm_g)


_drawn_inputs = setup_inputs


def setup_inputs(seed=0):
    import zlib

    import numpy as np

    out = dict(_drawn_inputs(seed))
    spreads = {}
    factors = {'norm_g': 5.269,
     'lru_conv_b': 3.372,
     'lru_ba': 8.0,
     'lru_bx': 8.0,
     's5_lambda_re': 64.0,
     's5_lambda_im': 49.416,
     's5_b_re': 64.0,
     's5_b_im': 64.0,
     's5_c_re': 64.0,
     's5_c_im': 64.0,
     's5_log_dt': 52.216,
     's5_b_glu': 8.0,
     'nsa_pos_k': 8.0,
     'nsa_pos_v': 8.0,
     'final_norm_g': 30.032}
    for name, (base, spread) in spreads.items():
        noise = np.random.default_rng([zlib.crc32(name.encode()), seed]).standard_normal(out[name].shape)
        drawn = base * np.exp(spread * noise) if base else spread * noise
        out[name] = __import__('jax').numpy.asarray(drawn.astype(out[name].dtype))
    for name, factor in factors.items():
        out[name] = (out[name] * factor).astype(out[name].dtype)
    return out
```

```python
import math
from contextlib import ExitStack

import numpy as np
import concourse.bass as bass
from concourse import mybir

P = 128
D = 1024
T = 256
TT = T // P
DEPTH = 2
BW = 512
KD = D // P
KB = BW // P
NH_RET = 4
HD_RET = 128
NHQ = 8
NKV = 2
HD = 64
NCMP = (T - 32) // 16 + 1
NS5 = 32 * 64 // P
EPS = 1e-6
EPS_RET = 1e-5
CMP_W = 280

COL_LRU, COL_S5, COL_RET, COL_NQ, COL_CMP, COL_KV, COL_BG, COL_GATE, COL_MERGE = (
    0, 512, 1024, 2560, 3072, 3328, 3840, 3864, 5912)
GATE_OF = {"lru": 0, "s5": 1, "ret": 2, "nsa": 3}

CHUNKS = [("u_s5", 8, 512), ("u_lru", 8, 512), ("ret_v", 8, 512), ("nsa_kv", 8, 512), ("cmp", 8, CMP_W),
          ("ck", 16, 256), ("cv", 16, 256), ("gate_s5", 8, 512), ("gate_lru", 8, 512),
          ("merge_s5_0", 8, 512), ("merge_s5_1", 8, 512), ("ret_q", 8, 512), ("ret_k", 8, 512),
          ("nsa_q", 8, 512), ("glu_a", 4, 512), ("glu_b", 4, 512), ("branch_s5_0", 4, 512),
          ("branch_s5_1", 4, 512), ("merge_lru_0", 8, 512), ("merge_lru_1", 8, 512),
          ("branch_lru_0", 4, 512), ("branch_lru_1", 4, 512), ("gate_ret", 8, 512),
          ("merge_ret_0", 8, 512), ("merge_ret_1", 8, 512), ("branch_ret_0", 4, 512),
          ("branch_ret_1", 4, 512), ("gate_nsa", 8, 512), ("merge_nsa_0", 8, 512),
          ("merge_nsa_1", 8, 512), ("branch_nsa_0", 4, 512), ("branch_nsa_1", 4, 512),
          ("out_0", 8, 512), ("out_1", 8, 512)]
CHUNK = {name: c for c, (name, _, _) in enumerate(CHUNKS)}
BRANCHES = ["s5", "lru", "ret", "nsa"]

UNITS = []
for _c, (_name, _kt, _w) in enumerate(CHUNKS):
    _per = 4 if _w == 256 else 2
    UNITS += [(_c, k, _per, _w) for k in range(0, _kt, _per)]
NU = len(UNITS)
UNIT_END = [max(u for u, x in enumerate(UNITS) if x[0] == c) + 1 for c in range(len(CHUNKS))]
N_RAW = 4
N_SPLIT = 5

V_NORM, V_CONV, V_CONVB, V_BA, V_BX, V_LAM, V_D, V_BGLU, V_LR, V_LI, V_DT, V_ROWS = (
    0, 8, 24, 28, 32, 36, 40, 44, 52, 68, 96, 112)

TWO_PI = 2.0 * math.pi
PI2_A = 6.28125
PI2_B = 0.0019350051879882812
PI2_C = TWO_PI - PI2_A - PI2_B
TURN = 6.2831845
ROUND = 12582912.0
GELU_C = math.sqrt(2.0 / math.pi)

CONST = {}
_at = 0
for _n, _s in (("ident", P), ("ret_cos", TT * 64), ("ret_sin", TT * 64), ("nsa_cos", TT * 8), ("nsa_sin", TT * 8),
               ("cmp_cos", 8), ("cmp_sin", 8), ("decay", NH_RET * T), ("causal", 2 * P), ("cmp_add", TT * 16),
               ("cmp_keep", TT * 16), ("head", NHQ), ("group", 2), ("time", T)):
    CONST[_n] = (_at, _s)
    _at += _s
N_CONST = _at


def shape_constants():
    f32 = np.float32
    out = np.zeros((P, N_CONST), f32)

    def put(name, a):
        at, size = CONST[name]
        out[:a.shape[0], at:at + size] = a.reshape(a.shape[0], size)

    def rope(pos, base, rot):
        half = rot // 2
        inv = (f32(base) ** (-np.arange(half, dtype=f32) * f32(2.0) / f32(rot))).astype(f32)
        ang = (pos.astype(f32)[..., None] * inv).astype(f32).astype(np.float64)
        return np.cos(ang).astype(f32), np.sin(ang).astype(f32)

    p = np.arange(P)
    tok = p[:, None] + P * np.arange(TT)[None, :]
    put("ident", np.eye(P, dtype=f32))
    c, s = rope(tok, 10000.0, HD_RET)
    put("ret_cos", c), put("ret_sin", s)
    c, s = rope(tok, 500000.0, HD // 4)
    put("nsa_cos", c), put("nsa_sin", s)
    c, s = rope((np.arange(32) % 16) * 16 + 31, 500000.0, HD // 4)
    put("cmp_cos", c), put("cmp_sin", s)
    gamma = 1.0 - np.exp(np.linspace(math.log(1 / 32), math.log(1 / 512), NH_RET))
    diff = np.arange(T)[None, :] - p[:, None]
    put("decay", np.stack([np.where(diff >= 0, g ** np.maximum(diff, 0), 0) for g in gamma], 1) * HD_RET ** -0.5)
    m = np.zeros((P, 2, P), f32)
    m[:, 1] = np.where(p[None, :] <= p[:, None], 0, -1e30)
    put("causal", m)
    n = np.arange(16)
    keep = (n * 16 + 31 <= tok[:, :, None]) & (n < NCMP)
    put("cmp_add", np.where(keep, 0, -1e30)), put("cmp_keep", keep * 1.0)
    put("head", ((p[:, None] // 16 == np.arange(NHQ)[None, :]) & (p[:, None] % 16 < NCMP)) * 1.0)
    put("group", ((p[:, None] // 16) % 2 == np.arange(2)[None, :]) * 1.0)
    put("time", np.broadcast_to(np.arange(T), (P, T)))
    return out


def hybrid_trunk(nc, a, out):
    f32, f32r = mybir.dt.float32, mybir.dt.float32r
    ALU, ACT, AX = mybir.AluOpType, mybir.ActivationFunctionType, mybir.AxisListType.X
    ctx = ExitStack()
    with ctx:
        def sb(name, shape, dt=f32):
            return ctx.enter_context(nc.sbuf_tensor(name, shape, dt))

        sems = []

        def sem(name):
            sems.append(ctx.enter_context(nc.semaphore(name)))
            return sems[-1]

        const = sb("const", [P, N_CONST])
        x = sb("x", [P, TT, D])
        raw = sb("raw", [P, N_RAW, 1024])
        w_hi = sb("w_hi", [P, N_SPLIT, 1024], f32r)
        w_lo = sb("w_lo", [P, N_SPLIT, 1024], f32r)
        h_hi = sb("h_hi", [P, KD, T], f32r)
        h_lo = sb("h_lo", [P, KD, T], f32r)
        ys_hi = sb("ys_hi", [P, KB, T], f32r)
        ys_lo = sb("ys_lo", [P, KB, T], f32r)
        merged = sb("merged", [P, TT, D])
        mt = sb("mt", [P, 2, TT, 512])
        gate = sb("gate", [P, 2, KB, T])
        rows = sb("rows", [P, P])
        rows2 = sb("rows2", [32, P])
        dt_in = sb("dt_in", [P, 2])
        vec = sb("vec", [P, V_ROWS])
        pos = sb("pos", [P, 2, 16])
        small = sb("small", [P, 30, 16])
        wa = sb("wa", [P, KB, P])
        wx = sb("wx", [P, KB, P])
        cw2 = sb("cw2", [P, 2, 2, HD])
        bT = sb("bT", [P, 2, KB, P])
        cT = sb("cT", [P, 2, KB, P])
        u_s5 = sb("u_s5", [P, KB, T])
        u_lru = sb("u_lru", [P, KB, T + 3])
        ret_v = sb("ret_v", [P, TT, BW])
        kd = sb("kd", [P, TT, 2, NKV, 2, HD])
        nv = sb("nv", [P, TT, 4, HD])
        hid = sb("hid", [P, 2, 2, 32])
        hid8 = sb("hid8", [P, 2, NHQ, 16])
        vbd = sb("vbd", [P, NHQ, HD])
        kc = sb("kc", [32, 2, HD])
        kcT = sb("kcT", [P, 32])
        bgate = sb("bgate", [P, TT, 24])
        st = sb("st", [P, 96])
        qT = sb("qT", [P, NH_RET, T])
        kT = sb("kT", [P, NH_RET, T])
        nqT = sb("nqT", [P, 4, T])
        nkT = sb("nkT", [P, 4, T])
        sc = sb("sc", [P, 7936])
        zero = sb("zero", [P, 1])
        half_pi = sb("half_pi", [P, 1])
        m_half = sb("m_half", [P, 8])
        proj = [ctx.enter_context(nc.psum_tensor(f"proj{i}", [P, 1024], f32)) for i in range(2)]
        M = ctx.enter_context(nc.psum_tensor("M", [P, 4, 512], f32))

        def cst(name):
            at, size = CONST[name]
            return const[:, at:at + size]

        def S(i, n=1):
            return small[:, i, :] if n == 1 else small[:, i:i + n, :]

        def cols(at, n):
            return sc[:, at:at + n]

        ident = cst("ident")
        cos_sin = cols(0, 2048).rearrange("p (b f j t) -> p b f j t", b=2, f=2, j=2)
        ang_a = cols(2048, 512).rearrange("p (j t) -> p j t", j=2)
        ang_s = cols(2560, 512).rearrange("p (j t) -> p j t", j=2)
        s5_t = cols(3072, 2048).rearrange("p (f j t) -> p f j t", f=4, j=2)
        s5_h = cols(5120, 2048).rearrange("p (b f j t) -> p b f j t", b=2, f=2, j=2)
        b_exp = cols(3072, 1024).rearrange("p (f s g c) -> p f s g c", f=2, s=NS5, g=2)
        b_tmp = cols(4096, 512).rearrange("p (f s c) -> p f s c", f=2, s=NS5)
        b_nat = cols(6656, 512).rearrange("p (f s c) -> p f s c", f=2, s=NS5)
        c_nat = cols(5120, 1024).rearrange("p (f q g n) -> p f q g n", f=2, q=KB, g=2)
        gelu_t = cols(2048, 1024)
        y_s5 = qT
        x2 = kT[:, 0:2, :].rearrange("p m (h t) -> p m h t", h=NKV)
        blocks = nqT[:, :, :].rearrange("p a (b h n) -> p (a b) h n", b=8, h=2)
        hid_y = kT[:, 2, 0:128]
        hid_t = kT[:, 2, 128:256]
        hid_q = kT[:, 3, 0:128]
        xc = cols(0, 1024).rearrange("p (t n) -> p t n", t=KB)
        l_r = cols(1024, 1024).rearrange("p (t n) -> p t n", t=KB)
        l_i = cols(2048, 1024).rearrange("p (t n) -> p t n", t=KB)
        l_a = cols(3072, 1024).rearrange("p (t n) -> p t n", t=KB)
        l_m = cols(4096, 1024).rearrange("p (t n) -> p t n", t=KB)
        l_h = cols(5120, 1024).rearrange("p (t n) -> p t n", t=KB)
        ret_s = cols(6144, 768).rearrange("p (b n) -> p b n", b=2)
        rope_t = cols(6912, 1024).rearrange("p (f a h c) -> p f a h c", f=2, a=TT, h=NH_RET)
        rope_n = cols(6912, 512).rearrange("p (f a h c) -> p f a h c", f=4, a=TT, h=NHQ)
        ro = u_lru[:, :, :].rearrange("p a b -> p (a b)")[:, 0:1024]
        ro4 = ro.rearrange("p (a h c) -> p a h c", a=TT, h=NH_RET)
        nq = u_s5[:, :, :].rearrange("p a b -> p (a b)")
        nq4 = nq.rearrange("p (a h c) -> p a h c", a=TT, h=NHQ)
        no4 = nq4
        prob = cols(0, 1536)
        probT = cols(1536, 1536).rearrange("p (b n) -> p b n", b=12)
        cmp_s = cols(3072, 256).rearrange("p (e a h n) -> p e a h n", e=2, a=TT, h=4)
        cmp_pT = cols(3328, 256)
        cmp_p = cols(3584, 256)
        att_t = cols(4096, 512)
        glu_v = cols(6912, 1024)
        glu_t = cols(0, 1024)
        bn = cols(6912, 48).rearrange("p (i n) -> p i n", n=6)
        mv = cols(6960, 16).rearrange("p (i n) -> p i n", n=2)
        kc_t = cols(7040, 32)[0:32].rearrange("p (f n) -> p f n", f=4)
        MF = M[:, :, :].rearrange("p b n -> p (b n)")

        prologue = sem("prologue")
        vec_loaded, b_loaded, c_loaded, wl_loaded, cw_loaded = (sem(n) for n in (
            "vec_loaded", "b_loaded", "c_loaded", "wl_loaded", "cw_loaded"))
        raw_loaded = [sem(f"raw_loaded{i}") for i in range(N_RAW)]
        hi_done, lo_done, unit_used = sem("hi_done"), sem("lo_done"), sem("unit_used")
        chunk_done = sem("chunk_done")
        evacuated = [sem("evacuated0"), sem("evacuated1")]
        dve_order = sem("dve_order")
        x_sq, x_var, x_rstd, x_norm, xT_done = (sem(n) for n in ("x_sq", "x_var", "x_rstd", "x_norm", "xT_done"))
        hhi_done, hlo_done = sem("hhi_done"), sem("hlo_done")
        dt_rows, vecT_done, vec_ready = sem("dt_rows"), sem("vecT_done"), sem("vec_ready")
        lam_abs, lam_exp, dt_exp, mag_arg, mag_exp = (sem(n) for n in ("lam_abs", "lam_exp", "dt_exp", "mag_arg", "mag_exp"))
        th_ready, th_sin = sem("th_ready"), sem("th_sin")
        b_ready, c_ready, bT_done, cT_done, bcT_ready = (sem(n) for n in ("b_ready", "c_ready", "bT_done", "cT_done", "bcT_ready"))
        ang_ready, trig_done, bu_done, bu_used, h_done, y_done = (sem(n) for n in (
            "ang_ready", "trig_done", "bu_done", "bu_used", "h_done", "y_done"))
        y_used = sem("y_used")
        z_arg, z_tanh, z_ready, z_hi, z_lo = (sem(n) for n in ("z_arg", "z_tanh", "z_ready", "z_hi", "z_lo"))
        blk_ready, blk_hi, blk_lo = (sem(n) for n in ("blk_ready", "blk_hi", "blk_lo"))
        hid_arg, hid_tanh, hid_ready = (sem(n) for n in ("hid_arg", "hid_tanh", "hid_ready"))
        gate_tanh, mt_free = (sem(n) for n in ("gate_tanh", "mt_free"))
        yg_ready, yg_hi, yg_lo = (sem(n) for n in ("yg_ready", "yg_hi", "yg_lo"))
        xc_ready, lru_mm, lru_act, lru_m2, lru_sqrt = (sem(n) for n in ("xc_ready", "lru_mm", "lru_act", "lru_m2", "lru_sqrt"))
        rope_ready, qkT_done, qkT_ready = sem("rope_ready"), sem("qkT_done"), sem("qkT_ready")
        rs_done, rs_ready, ro_done, rvar, rrstd, rn_ready, rnT_done, yr_ready = (sem(n) for n in (
            "rs_done", "rs_ready", "ro_done", "rvar", "rrstd", "rn_ready", "rnT_done", "yr_ready"))
        nrope_ready, nT_done, nT_ready = (sem(n) for n in (
            "nrope_ready", "nT_done", "nT_ready"))
        cw_done, kc_ready, vbd_ready, kcT_done, kcT_ready = (sem(n) for n in (
            "cw_done", "kc_ready", "vbd_ready", "kcT_done", "kcT_ready"))
        cs_done, cs_sub, cs_exp, cp_ready, cpT_done, cpT_ready, co_done, no_cmp = (sem(n) for n in (
            "cs_done", "cs_sub", "cs_exp", "cp_ready", "cpT_done", "cpT_ready", "co_done", "no_cmp"))
        at_even, at_s, at_max, at_exp, at_pT, at_pT_ready, at_o, at_no = (sem(n) for n in (
            "at_even", "at_s", "at_max", "at_exp", "at_pT", "at_pT_ready", "at_o", "at_no"))
        noT_done, yn_ready = sem("noT_done"), sem("yn_ready")
        mT_done, mhi_done, mlo_done = (sem(n) for n in ("mT_done", "mhi_done", "mlo_done"))
        fin = [ctx.enter_context(nc.semaphore(f"fin{i}")) for i in range(6)]

        raw_target = []
        _count = [0] * N_RAW
        for u, (c, _, _, _) in enumerate(UNITS):
            _count[u % N_RAW] += 32 if c == CHUNK["cmp"] else 16
            raw_target.append(_count[u % N_RAW])

        def ch(name):
            return CHUNK[name] + 1

        def wait_unit_read(eng, u):
            c = UNITS[u][0]
            if u + 1 == UNIT_END[c]:
                eng.wait_ge(chunk_done, c + 1)
            else:
                eng.wait_ge(unit_used, u + 1 - c)

        def pr(name):
            return proj[CHUNK[name] % 2]

        def evac(name):
            return evacuated[CHUNK[name] % 2]

        def ev(name):
            return CHUNK[name] // 2 + 1

        def flat(t):
            return t.rearrange("p a b -> p (a b)")

        def bc(ap, shape):
            return ap.to_broadcast(shape)

        with nc.Block() as block:
            @block.sync
            def _(sp):
                sp.dma_start(x[:, :, :], a["x"][0].rearrange("(t p) d -> p t d", p=P)).then_inc(prologue, 16)
                sp.dma_start(const[:, :], a["constants"]).then_inc(prologue, 16)
                sp.wait_ge(prologue, 32)

            @block.gpsimd
            def _(gp):
                for tile in (rows, wa, wx):
                    gp.memset(tile[:], 0.0)
                gp.memset(zero[:, :], 0.0)
                gp.memset(half_pi[:, :], math.pi / 2)
                gp.memset(m_half[:, :], -0.5)

        with nc.Fori(0, DEPTH) as l:
            with nc.Block() as block:
                @block.sync
                def _(sp):
                    def vectors(name, at, n):
                        src = a[name][l]
                        if name == "lru_conv_w":
                            src = src.rearrange("k (t p) -> (k t) p", p=P)
                        elif len(src.shape) == 2:
                            src = src.rearrange("(s g) n -> s (g n)", g=2)
                        else:
                            src = src.rearrange("(t p) -> t p", p=P)
                        sp.dma_start(rows[at:at + n, :], src).then_inc(vec_loaded, 16)

                    def load_unit(u):
                        c, k, n, w = UNITS[u]
                        name = CHUNKS[c][0]
                        slot = u % N_RAW
                        if u >= N_RAW:
                            sp.wait_ge(lo_done, u - N_RAW + 1)
                        dst = raw[:, slot, 0:n * w].rearrange("p (k n) -> p k n", k=n)

                        def load(d, src):
                            sp.dma_start(d, src.rearrange("(k p) n -> p k n", p=P)).then_inc(raw_loaded[slot], 16)

                        def w_in(col, width, d=None):
                            load(dst if d is None else d, a["w_in"][l][k * P:(k + n) * P, col:col + width])

                        kind = name.split("_")[0]
                        half = 512 * int(name[-1]) if name[-1] in "01" else 0
                        if kind == "u":
                            w_in(COL_S5 if name == "u_s5" else COL_LRU, w)
                        elif kind == "ret":
                            w_in(COL_RET + BW * "qkv".index(name[-1]), w)
                        elif name == "nsa_q":
                            w_in(COL_NQ, w)
                        elif name == "nsa_kv":
                            w_in(COL_KV, w)
                        elif name == "cmp":
                            w_in(COL_CMP, 256, dst[:, :, 0:256])
                            w_in(COL_BG, 24, dst[:, :, 256:CMP_W])
                        elif name in ("ck", "cv"):
                            load(dst, a[f"nsa_{name}_w1"][l][k * P:(k + n) * P, :])
                        elif kind == "gate":
                            w_in(COL_GATE + BW * GATE_OF[name[5:]], w)
                        elif kind == "merge":
                            w_in(COL_MERGE + D * GATE_OF[name[6:-2]] + half, w)
                        elif kind == "glu":
                            at = 512 * "ab".index(name[-1])
                            load(dst, a["s5_w_glu"][l][k * P:(k + n) * P, at:at + w])
                        elif kind == "branch":
                            load(dst, a["w_branch"][l][GATE_OF[name[7:-2]]][k * P:(k + n) * P, half:half + w])
                        else:
                            load(dst, a["w_out"][l][k * P:(k + n) * P, half:half + w])

                    vectors("norm_g", V_NORM, 8)
                    vectors("lru_conv_w", V_CONV, 16)
                    vectors("lru_conv_b", V_CONVB, 4)
                    vectors("lru_ba", V_BA, 4)
                    vectors("lru_bx", V_BX, 4)
                    vectors("lru_lambda", V_LAM, 4)
                    vectors("s5_d", V_D, 4)
                    vectors("s5_b_glu", V_BGLU, 8)
                    vectors("s5_lambda_re", V_LR, 16)
                    vectors("s5_lambda_im", V_LI, 16)
                    sp.dma_start(dt_in[V_DT:V_ROWS, :], a["s5_log_dt"][l].rearrange("(s g) -> s g", g=2)).then_inc(vec_loaded, 16)
                    for m, name in enumerate(("nsa_pos_k", "nsa_pos_v")):
                        sp.dma_start(rows2[16 * m:16 * m + 16, :], a[name][l].rearrange("(r s) d -> r (s d)", s=2)).then_inc(vec_loaded, 16)
                    for u in range(2):
                        load_unit(u)
                    for f, name in enumerate(("s5_b_re", "s5_b_im")):
                        sp.dma_start(b_nat[:, f], a[name][l].rearrange("(s g) n c -> (g n) s c", g=2)).then_inc(b_loaded, 16)
                    for f, name in enumerate(("s5_c_re", "s5_c_im")):
                        for g in range(2):
                            sp.dma_start(c_nat[:, f, :, g], a[name][l].rearrange("(q r) c n -> (r c) q n", q=KB)).then_inc(c_loaded, 16)
                    for u in range(2, N_RAW):
                        load_unit(u)
                    for tile, name in ((wa, "lru_wa"), (wx, "lru_wx")):
                        for g in range(2):
                            sp.dma_start(tile[64 * g:64 * g + 64, :, 64 * g:64 * g + 64],
                                         a[name][l].rearrange("(t g) i j -> g i t j", g=2)[g]).then_inc(wl_loaded, 16)
                    for m, name in enumerate(("nsa_ck_w2", "nsa_cv_w2")):
                        sp.dma_start(cw2[:, m], a[name][l].rearrange("(k p) d -> p k d", p=P)).then_inc(cw_loaded, 16)
                    for u in range(N_RAW, NU):
                        load_unit(u)

                @block.gpsimd
                def _(gp):
                    done = [0]

                    def split_lo(upto):
                        for u in range(done[0], upto):
                            c, _, n, w = UNITS[u]
                            gp.wait_ge(hi_done, u + 1)
                            if u >= N_SPLIT:
                                wait_unit_read(gp, u - N_SPLIT)
                            nc.gpsimd.tensor_tensor(w_lo[:, u % N_SPLIT, 0:n * w], raw[:, u % N_RAW, 0:n * w],
                                                    w_hi[:, u % N_SPLIT, 0:n * w].bitcast(f32), ALU.subtract).then_inc(lo_done, 1)
                        done[0] = max(done[0], upto)

                    split_lo(1)
                    gp.wait_ge(x_var, 1)
                    nc.gpsimd.tensor_tensor(st[:, 2:4], st[:, 0:2], m_half[:, 0:2], ALU.pow).then_inc(x_rstd, 1)
                    split_lo(UNIT_END[CHUNK["merge_lru_0"]] + 1)
                    gp.wait_ge(rvar, 1)
                    nc.gpsimd.tensor_tensor(st[:, 88:96], st[:, 80:88], m_half[:, :], ALU.pow).then_inc(rrstd, 1)
                    split_lo(NU)

                @block.scalar
                def _(act):
                    done = [0]

                    def run(out_, in_, func, signal=None, **kw):
                        i = nc.scalar.activation(out_, in_, func, **kw)
                        if signal is not None:
                            i.then_inc(signal, 1)

                    def cast_units(upto):
                        for u in range(done[0], upto):
                            c, _, n, w = UNITS[u]
                            act.wait_ge(raw_loaded[u % N_RAW], raw_target[u])
                            if u >= N_SPLIT:
                                wait_unit_read(act, u - N_SPLIT)
                            run(w_hi[:, u % N_SPLIT, 0:n * w], raw[:, u % N_RAW, 0:n * w], ACT.Copy, hi_done)
                        done[0] = max(done[0], upto)

                    def next_cast(name):
                        cast_units(UNIT_END[min(CHUNK[name] + 1, len(CHUNKS) - 1)])
                        act.wait_ge(chunk_done, ch(name))

                    for t in range(TT):
                        run(merged[:, t, :], x[:, t, :], ACT.Square, x_sq, accum_out=st[:, 4 + t:5 + t])
                    cast_units(2)
                    act.wait_ge(lam_abs, 1)
                    run(S(1)[:, 0:4], S(0)[:, 0:4], ACT.Exp, lam_exp, scale=-1.0)
                    run(S(8), vec[:, V_DT:V_ROWS], ACT.Exp, dt_exp)
                    for k in range(KD):
                        if k % 2 == 0:
                            act.wait_ge(xT_done, k // 2 + 1)
                        run(h_hi[:, k, :], M[:, k // 2, (k % 2) * T:(k % 2 + 1) * T], ACT.Copy, hhi_done,
                            scale=vec[:, V_NORM + k:V_NORM + k + 1])
                    cast_units(N_SPLIT)
                    act.wait_ge(mag_arg, 1)
                    run(S(10), S(9), ACT.Exp, mag_exp)
                    nc.scalar.preload_act_table_set("silu_and_others")
                    act.wait_ge(th_ready, 1)
                    run(S(13), S(12), ACT.Abs, th_sin)
                    act.wait_ge(th_sin, 1)
                    run(S(14), S(13), ACT.Sin, th_sin, bias=half_pi[:, 0:1], scale=-1.0)
                    run(S(15), S(12), ACT.Sin, th_sin)

                    def trig(p):
                        act.wait_ge(ang_ready, p + 1)
                        run(ang_s, ang_a, ACT.Abs, trig_done)
                        run(cos_sin[:, p % 2, 1], ang_a, ACT.Sin, trig_done, scale=TURN)
                        act.wait_ge(trig_done, 3 * p + 1)
                        run(cos_sin[:, p % 2, 0], ang_s, ACT.Sin, trig_done, scale=-TURN, bias=half_pi[:, 0:1])

                    next_cast("u_s5")
                    run(flat(u_s5[:, :, :]), pr("u_s5")[:, :], ACT.Copy, evac("u_s5"))
                    act.wait_ge(bT_done, 1)
                    run(bT[:, :, :, :].rearrange("p f q n -> p (f q n)"), MF[:, 1024:2048], ACT.Copy, bcT_ready)
                    act.wait_ge(cT_done, 1)
                    run(cT[:, :, :, :].rearrange("p f q n -> p (f q n)"), MF[:, 0:1024], ACT.Copy, bcT_ready)
                    trig(0)
                    next_cast("u_lru")
                    run(u_lru[:, :, 3:T + 3], pr("u_lru")[:, :].rearrange("p (t n) -> p t n", t=KB), ACT.Copy, evac("u_lru"))
                    trig(1)
                    next_cast("ret_v")
                    run(flat(ret_v[:, :, :]), pr("ret_v")[:, :], ACT.Copy, evac("ret_v"))
                    trig(2)
                    next_cast("nsa_kv")
                    kv = pr("nsa_kv")[:, :].rearrange("p (a y o h d) -> p a y o h d", a=TT, y=2, o=2, h=NKV)
                    for t in range(TT):
                        for dup in range(2):
                            run(kd[:, t, :, :, dup, :], kv[:, t, :, 0], ACT.Copy)
                        run(nv[:, t].rearrange("p (y h) d -> p y h d", y=2), kv[:, t, :, 1], ACT.Copy,
                            evac("nsa_kv") if t else None)
                    trig(3)
                    next_cast("cmp")
                    for h in range(NKV):
                        for s in range(2):
                            run(x2[64 * s:64 * s + 64, :, h, :],
                                pr("cmp")[64 * h:64 * h + 64, 0:512].rearrange("p (m t s) -> p m t s", m=2, s=2)[:, :, :, s],
                                ACT.Copy)
                    run(bgate[:, :, :], pr("cmp")[:, 512:560].rearrange("p (a n) -> p a n", a=TT), ACT.Tanh,
                        evac("cmp"), scale=0.5)
                    act.wait_ge(blk_ready, 1)
                    run(flat(ys_hi[:, :, :]), flat(nqT[:, :, :]), ACT.Copy, blk_hi)
                    trig(4)
                    for m, name in enumerate(("ck", "cv")):
                        next_cast(name)
                        run(hid_y[:, 64 * m:64 * m + 64].rearrange("p (k n) -> p k n", k=2),
                            pr(name)[:, :].rearrange("p (k n) -> p k n", k=2)[:, :, 0:32], ACT.Copy, evac(name))
                    act.wait_ge(hid_arg, 1)
                    run(hid_q, hid_q, ACT.Tanh, hid_tanh, scale=GELU_C)
                    trig(5)

                    def gate_chunk(name):
                        i = BRANCHES.index(name)
                        next_cast("gate_" + name)
                        if i >= 2:
                            act.wait_ge(yg_lo, i - 1)
                        run(flat(gate[:, i % 2]), pr("gate_" + name)[:, :], ACT.Tanh, gate_tanh, scale=0.5)

                    def merge_chunk(name, half):
                        i = BRANCHES.index(name)
                        full = f"merge_{name}_{half}"
                        next_cast(full)
                        if i == 1:
                            act.wait_ge(evac(f"branch_s5_{half}"), ev(f"branch_s5_{half}"))
                        if i > 1:
                            act.wait_ge(mt_free, 2 * (i - 2) + half + 1)
                        run(flat(mt[:, half]), pr(full)[:, :], ACT.Tanh, evac(full), scale=0.5)

                    def hi_of_gated(name):
                        i = BRANCHES.index(name)
                        act.wait_ge(yg_ready, i + 1)
                        act.wait_ge(chunk_done, ch("glu_b" if i == 0 else f"branch_{BRANCHES[i - 1]}_1"))
                        run(flat(ys_hi[:, :, :]), flat(gate[:, i % 2]), ACT.Copy, yg_hi)

                    def attention_exp(i):
                        act.wait_ge(at_max, i + 1)
                        for b, g in enumerate((0, 2, 1, 3)):
                            run(prob[:, b * T:(b + 1) * T], prob[:, b * T:(b + 1) * T], ACT.Exp, at_exp,
                                bias=st[:, 40 + b:41 + b], accum_out=st[:, 52 + g:53 + g])
                            at = 1024 + b * P
                            run(prob[:, at:at + P], prob[:, at:at + P], ACT.Exp, at_exp,
                                bias=st[:, 44 + b:45 + b], accum_out=st[:, 48 + g:49 + g])

                    def attention_evac(i):
                        act.wait_ge(at_pT, i + 1)
                        if i:
                            act.wait_ge(at_o, i)
                        run(flat(probT), MF[:, 0:1536], ACT.Copy, at_pT_ready)

                    gate_chunk("s5")
                    trig(6)
                    gate_chunk("lru")
                    trig(7)
                    merge_chunk("s5", 0)
                    merge_chunk("s5", 1)
                    cast_units(UNIT_END[CHUNK["ret_k"]])
                    act.wait_ge(z_arg, 1)
                    run(gelu_t, gelu_t, ACT.Tanh, z_tanh, scale=GELU_C)
                    act.wait_ge(z_ready, 1)
                    run(flat(ys_hi[:, :, :]), flat(y_s5[:, :, :]), ACT.Copy, z_hi)
                    act.wait_ge(lru_mm, 1)
                    for t in range(KB):
                        run(l_r[:, t, :], MF[:, t * T:(t + 1) * T], ACT.Tanh, lru_act, scale=0.5, bias=S(3)[:, t:t + 1])
                    for t in range(KB):
                        run(l_i[:, t, :], MF[:, 1024 + t * T:1024 + (t + 1) * T], ACT.Tanh, lru_act, scale=0.5,
                            bias=S(3)[:, 4 + t:5 + t])
                    nc.scalar.preload_act_table_set("exp_and_others")
                    act.wait_ge(lru_act, KB)
                    for t in range(KB):
                        run(l_a[:, t, :], l_r[:, t, :], ACT.Exp, lru_act, scale=S(4)[:, t:t + 1], bias=S(4)[:, t:t + 1])
                        run(l_m[:, t, :], l_r[:, t, :], ACT.Tanh, lru_act, scale=S(4)[:, 4 + t:5 + t], bias=S(4)[:, 4 + t:5 + t])
                    next_cast("ret_k")
                    act.wait_ge(qkT_done, 1)
                    act.wait_ge(z_lo, 1)
                    run(flat(qT[:, :, :]), MF[:, 0:1024], ACT.Copy, qkT_ready)
                    next_cast("nsa_q")
                    run(nq, pr("nsa_q")[:, :], ACT.Copy, evac("nsa_q"), scale=HD ** -0.5)
                    act.wait_ge(qkT_done, 2)
                    run(flat(kT[:, :, :]), MF[:, 1024:2048], ACT.Copy, qkT_ready)
                    next_cast("glu_a")
                    act.wait_ge(nT_done, 1)
                    run(flat(nqT[:, :, :]), MF[:, 0:1024], ACT.Copy, nT_ready)
                    next_cast("glu_b")
                    act.wait_ge(lru_m2, 1)
                    for t in range(KB):
                        run(glu_t[:, t * T:(t + 1) * T], pr("glu_b")[:, t * T:(t + 1) * T], ACT.Tanh,
                            evac("glu_b") if t == KB - 1 else None, scale=0.5, bias=S(5)[:, t:t + 1])
                    act.wait_ge(nT_done, 2)
                    run(flat(nkT[:, :, :]), MF[:, 1024:2048], ACT.Copy, nT_ready)
                    hi_of_gated("s5")
                    cast_units(UNIT_END[CHUNK["branch_s5_1"]])
                    run(flat(l_m), flat(l_m), ACT.Sqrt, lru_sqrt, scale=0.25)
                    nc.scalar.preload_act_table_set("exp_and_others")
                    cast_units(UNIT_END[CHUNK["merge_lru_0"]])
                    hi_of_gated("lru")
                    merge_chunk("lru", 0)
                    act.wait_ge(kcT_done, 1)
                    run(kcT[:, :], M[:, 1, 0:32], ACT.Copy, kcT_ready)
                    cast_units(UNIT_END[CHUNK["merge_lru_1"]])
                    act.wait_ge(rnT_done, 1)
                    run(flat(qT[:, :, :]), MF[:, 1024:2048], ACT.Copy, yr_ready)
                    act.wait_ge(cs_sub, 1)
                    run(cols(3072, 256), cols(3072, 256), ACT.Exp, cs_exp)
                    merge_chunk("lru", 1)
                    act.wait_ge(cpT_done, 1)
                    run(cmp_pT, M[:, 3, 0:256], ACT.Copy, cpT_ready)
                    cast_units(UNIT_END[CHUNK["branch_lru_1"]])
                    attention_exp(0)
                    cast_units(UNIT_END[CHUNK["gate_ret"]])
                    attention_evac(0)
                    gate_chunk("ret")
                    hi_of_gated("ret")
                    attention_exp(1)
                    merge_chunk("ret", 0)
                    attention_evac(1)
                    cast_units(UNIT_END[CHUNK["merge_ret_1"]])
                    attention_exp(2)
                    merge_chunk("ret", 1)
                    next_cast("branch_ret_0")
                    attention_evac(2)
                    next_cast("branch_ret_1")
                    attention_exp(3)
                    gate_chunk("nsa")
                    attention_evac(3)
                    merge_chunk("nsa", 0)
                    act.wait_ge(noT_done, 1)
                    run(flat(nqT[:, :, :]), MF[:, 1024:2048], ACT.Copy, yn_ready)
                    hi_of_gated("nsa")
                    merge_chunk("nsa", 1)
                    cast_units(UNIT_END[CHUNK["branch_nsa_1"]] + N_SPLIT)
                    for b in range(4):
                        act.wait_ge(mT_done, b + 1)
                        run(flat(h_hi[:, 2 * b:2 * b + 2, :]), M[:, b, :], ACT.Copy, mhi_done)
                    cast_units(NU)

                @block.vector
                def _(dve):
                    v = nc.vector
                    links = [0]

                    def link(i):
                        links[0] += 1
                        i.then_inc(dve_order, 1)
                        dve.wait_ge(dve_order, links[0])

                    v.memset(u_lru[:, :, 0:3], 0.0)
                    dve.wait_ge(vec_loaded, 13 * 16)
                    v.tensor_copy(rows[V_DT:V_ROWS, :].rearrange("p (g n) -> p g n", g=2),
                                  bc(dt_in[V_DT:V_ROWS, :].unsqueeze(2), [16, 2, 64])).then_inc(dt_rows, 1)
                    dve.wait_ge(x_sq, TT)
                    v.tensor_scalar(st[:, 0:2], st[:, 4:6], 1.0 / D, EPS, ALU.mult, ALU.add).then_inc(x_var, 1)
                    dve.wait_ge(vecT_done, 2)
                    v.tensor_copy(vec[:, :], proj[1][:, 0:V_ROWS])
                    v.tensor_copy(flat(pos[:, :, :]), proj[1][:, P:P + 32]).then_inc(vec_ready, 1)
                    dve.wait_ge(vec_ready, 1)
                    lam, lam_i, lam_r = vec[:, V_LAM:V_LAM + 4], vec[:, V_LI:V_LI + 16], vec[:, V_LR:V_LR + 16]
                    v.scalar_tensor_tensor(S(0)[:, 0:4], lam, -1.0, lam, ALU.mult, ALU.max).then_inc(lam_abs, 1)
                    dve.wait_ge(x_rstd, 1)
                    for t in range(TT):
                        v.tensor_scalar(merged[:, t, :], x[:, t, :], st[:, 2 + t:3 + t], None, ALU.mult).then_inc(x_norm, 1)
                    v.tensor_scalar(S(3)[:, 0:8], vec[:, V_BA:V_BA + 8], 0.5, None, ALU.mult)
                    v.tensor_scalar(S(5)[:, 0:4], vec[:, V_BGLU + 4:V_BGLU + 8], 0.5, None, ALU.mult)
                    v.tensor_scalar(S(11), lam_r, -1e-4, None, ALU.min)
                    dve.wait_ge(dt_exp, 1)
                    link(v.tensor_tensor(S(19), lam_i, S(8), ALU.mult))
                    v.tensor_tensor(S(9), S(11), S(8), ALU.mult).then_inc(mag_arg, 1)
                    link(v.tensor_scalar(S(18), S(19), 1.0 / TWO_PI, None, ALU.mult))
                    link(v.tensor_scalar(S(18), S(18), ROUND, ROUND, ALU.add, ALU.subtract))
                    for part in (PI2_A, PI2_B, PI2_C):
                        link(v.scalar_tensor_tensor(S(19), S(18), -part, S(19), ALU.mult, ALU.add))
                    v.tensor_scalar(S(12), S(19), 3.1415925, -3.1415925, ALU.min, ALU.max).then_inc(th_ready, 1)
                    for k in range(KD):
                        dve.wait_ge(hhi_done, k // 2 * 2 + 2)
                        v.scalar_tensor_tensor(h_lo[:, k, :], M[:, k // 2, (k % 2) * T:(k % 2 + 1) * T],
                                               vec[:, V_NORM + k:V_NORM + k + 1], h_hi[:, k, :].bitcast(f32),
                                               ALU.mult, ALU.subtract).then_inc(hlo_done, 1)
                    dve.wait_ge(th_ready, 1)
                    link(v.tensor_scalar(S(19), S(12), 1.0 / TWO_PI, None, ALU.mult))
                    link(v.tensor_scalar(S(16), S(19), 4096.0, ROUND, ALU.mult, ALU.add))
                    link(v.tensor_scalar(S(16), S(16), ROUND, 1.0 / 4096.0, ALU.subtract, ALU.mult))
                    link(v.tensor_tensor(S(17), S(19), S(16), ALU.subtract))

                    def angles(p):
                        if p:
                            dve.wait_ge(trig_done, 3 * p)
                        for j in range(2):
                            i = v.tensor_scalar(ang_a[:, j, :], cst("time"), S(16)[:, 2 * p + j:2 * p + j + 1], None, ALU.mult)
                        link(i)
                        for j in range(2):
                            i = v.scalar_tensor_tensor(ang_s[:, j, :], cst("time"), S(17)[:, 2 * p + j:2 * p + j + 1],
                                                       ang_a[:, j, :], ALU.mult, ALU.add)
                        link(i)
                        link(v.tensor_scalar(ang_s, ang_s, ROUND, ROUND, ALU.add, ALU.subtract))
                        link(v.tensor_tensor(ang_a, ang_a, ang_s, ALU.subtract))
                        for j in range(2):
                            i = v.scalar_tensor_tensor(ang_a[:, j, :], cst("time"), S(17)[:, 2 * p + j:2 * p + j + 1],
                                                       ang_a[:, j, :], ALU.mult, ALU.add)
                        link(i)
                        v.tensor_scalar(ang_a, ang_a, 0.5, -0.5, ALU.min, ALU.max).then_inc(ang_ready, 1)

                    dve.wait_ge(th_sin, 3)
                    dve.wait_ge(mag_exp, 1)
                    v.memset(cols(3072, 1024), 0.0)
                    link(v.tensor_tensor(S(21), S(15), S(10), ALU.mult))
                    link(v.tensor_tensor(S(20), S(14), S(10), ALU.mult))
                    link(v.tensor_scalar(S(20), S(20), 1.0, None, ALU.subtract))
                    v.tensor_tensor(S(22), S(11), S(11), ALU.mult)
                    link(v.tensor_tensor(S(26), lam_i, lam_i, ALU.mult))
                    link(v.tensor_tensor(S(22), S(22), S(26), ALU.add))
                    link(v.reciprocal(S(23), S(22)))
                    v.tensor_tensor(S(24), S(20), S(11), ALU.mult)
                    v.tensor_tensor(S(25), S(21), S(11), ALU.mult)
                    v.tensor_tensor(S(26), S(21), lam_i, ALU.mult)
                    link(v.tensor_tensor(S(27), S(20), lam_i, ALU.mult))
                    v.tensor_tensor(S(24), S(24), S(26), ALU.add)
                    link(v.tensor_tensor(S(25), S(25), S(27), ALU.subtract))
                    v.tensor_tensor(S(24), S(24), S(23), ALU.mult)
                    link(v.tensor_tensor(S(25), S(25), S(23), ALU.mult))
                    dve.wait_ge(b_loaded, 32)
                    f_re = bc(S(24).unsqueeze(2), [P, NS5, 16])
                    f_im = bc(S(25).unsqueeze(2), [P, NS5, 16])
                    for f, (b0, b1, op) in enumerate(((0, 1, ALU.subtract), (1, 0, ALU.add))):
                        v.tensor_tensor(b_tmp[:, 0], b_nat[:, b0], f_re, ALU.mult)
                        link(v.tensor_tensor(b_tmp[:, 1], b_nat[:, b1], f_im, ALU.mult))
                        for g in range(2):
                            h = slice(64 * g, 64 * g + 64)
                            i = v.tensor_tensor(b_exp[h, f, :, g, :], b_tmp[h, 0], b_tmp[h, 1], op)
                        i.then_inc(b_ready, 1)
                        dve.wait_ge(b_ready, f + 1)
                    dve.wait_ge(c_loaded, 64)
                    for f in range(2):
                        v.tensor_tensor(c_nat[:, f], c_nat[:, f], bc(cst("group").unsqueeze(1).unsqueeze(3), [P, KB, 2, 64]),
                                        ALU.mult).then_inc(c_ready, 1)
                    angles(0)
                    e, s_, s2, q_, m_ = S(1)[:, 0:4], S(6)[:, 0:4], S(6)[:, 4:8], S(7)[:, 0:4], S(7)[:, 4:8]
                    dve.wait_ge(lam_exp, 1)
                    v.tensor_scalar(m_, lam, -1.0, 0.0, ALU.mult, ALU.max)
                    link(v.tensor_scalar(s_, e, 2.0, None, ALU.add))
                    link(v.reciprocal(s_, s_))
                    link(v.tensor_tensor(s_, s_, e, ALU.mult))
                    link(v.tensor_tensor(s2, s_, s_, ALU.mult))
                    link(v.tensor_scalar(q_, s2, 1.0 / 15.0, None, ALU.mult))
                    for n in (13, 11, 9, 7, 5, 3):
                        link(v.scalar_tensor_tensor(q_, q_, 1.0 / n, s2, ALU.add, ALU.mult))
                    link(v.scalar_tensor_tensor(q_, q_, 1.0, s_, ALU.add, ALU.mult))
                    link(v.scalar_tensor_tensor(q_, q_, 2.0, m_, ALU.mult, ALU.add))
                    v.tensor_scalar(S(4)[:, 0:4], q_, -0.5 * 8.0, None, ALU.mult)
                    link(v.tensor_scalar(S(4)[:, 4:8], q_, 0.5 * 8.0, None, ALU.mult))

                    def scan_pair(p):
                        b = p % 2
                        cos, sin = cos_sin[:, b, 0], cos_sin[:, b, 1]
                        t0, t1, t2, t3 = (s5_t[:, f] for f in range(4))
                        re, im = M[:, 0:2, 0:T], M[:, 0:2, T:2 * T]
                        if p:
                            dve.wait_ge(h_done, p)
                        dve.wait_ge(trig_done, 3 * p + 3)
                        dve.wait_ge(bu_done, p + 1)
                        v.tensor_tensor(t0, re, cos, ALU.mult)
                        v.tensor_tensor(t1, im, sin, ALU.mult)
                        v.tensor_tensor(t2, im, cos, ALU.mult)
                        v.tensor_tensor(t3, re, sin, ALU.mult).then_inc(bu_used, 1)
                        dve.wait_ge(bu_used, p + 1)
                        v.tensor_tensor(t0, t0, t1, ALU.add)
                        link(v.tensor_tensor(t2, t2, t3, ALU.subtract))
                        for j in range(2):
                            mag = bc(S(10)[:, 2 * p + j:2 * p + j + 1], [P, T])
                            v.tensor_tensor_scan(t1[:, j, :], mag, t0[:, j, :], 0.0, ALU.mult, ALU.add)
                            i = v.tensor_tensor_scan(t3[:, j, :], mag, t2[:, j, :], 0.0, ALU.mult, ALU.add)
                        link(i)
                        if p >= 2:
                            dve.wait_ge(y_done, p - 1)
                        h_re, h_im = s5_h[:, b, 0], s5_h[:, b, 1]
                        v.tensor_tensor(h_re, t1, cos, ALU.mult)
                        v.tensor_tensor(t0, t3, sin, ALU.mult)
                        v.tensor_tensor(h_im, t3, cos, ALU.mult)
                        link(v.tensor_tensor(t2, t1, sin, ALU.mult))
                        v.tensor_tensor(h_re, h_re, t0, ALU.subtract)
                        v.scalar_tensor_tensor(h_im, h_im, -1.0, t2, ALU.mult, ALU.subtract).then_inc(h_done, 1)

                    def s5_out(q):
                        dve.wait_ge(y_done, 2 * q + 2)
                        v.scalar_tensor_tensor(y_s5[:, q, :], u_s5[:, q, :], vec[:, V_D + q:V_D + q + 1],
                                               M[:, 2 + q % 2, 0:T], ALU.mult, ALU.add).then_inc(y_used, 1)

                    def gate_times(name):
                        i = BRANCHES.index(name)
                        g = flat(gate[:, i % 2])
                        dve.wait_ge(gate_tanh, i + 1)
                        v.scalar_tensor_tensor(g, g, 1.0, pr("gate_" + name)[:, :], ALU.add, ALU.mult).then_inc(evac("gate_" + name), 1)

                    def gated(name, y):
                        i = BRANCHES.index(name)
                        g = flat(gate[:, i % 2])
                        dve.wait_ge(evac("gate_" + name), ev("gate_" + name))
                        v.tensor_tensor(g, g, y, ALU.mult).then_inc(yg_ready, 1)

                    def lo_of_gated(name):
                        i = BRANCHES.index(name)
                        dve.wait_ge(yg_hi, i + 1)
                        v.tensor_tensor(flat(ys_lo[:, :, :]), flat(gate[:, i % 2]), flat(ys_hi[:, :, :]).bitcast(f32),
                                        ALU.subtract).then_inc(yg_lo, 1)

                    def branch(name, half):
                        i = BRANCHES.index(name)
                        full = f"branch_{name}_{half}"
                        dst = merged[:, :, 512 * half:512 * half + 512]
                        dve.wait_ge(chunk_done, ch(full))
                        src = pr(full)[:, :].rearrange("p (a n) -> p a n", a=TT)
                        if i == 0:
                            v.scalar_tensor_tensor(dst, mt[:, half], 1.0, src, ALU.add, ALU.mult).then_inc(evac(full), 1)
                        else:
                            v.scalar_tensor_tensor(mt[:, half], mt[:, half], 1.0, src, ALU.add, ALU.mult).then_inc(evac(full), 1)
                            dve.wait_ge(evac(full), ev(full))
                            v.tensor_tensor(dst, dst, mt[:, half], ALU.add).then_inc(mt_free, 1)

                    angles(1)
                    scan_pair(0)
                    angles(2)
                    scan_pair(1)
                    angles(3)
                    scan_pair(2)
                    s5_out(0)
                    dve.wait_ge(evac("cmp"), ev("cmp"))
                    v.memset(blocks[:, :, :, NCMP:16], 0.0)
                    for m in range(2):
                        for r8 in range(2):
                            src = x2[:, m].rearrange("p h (n r) -> p r h n", r=8)[:, :, :, r8:r8 + NCMP]
                            at = 16 * m + 8 * r8
                            i = v.tensor_tensor(blocks[:, at:at + 8, :, 0:NCMP], src,
                                                bc(pos[:, m, 8 * r8:8 * r8 + 8].unsqueeze(2).unsqueeze(3), [P, 8, 2, NCMP]), ALU.add)
                    i.then_inc(blk_ready, 1)
                    v.tensor_scalar(bgate[:, :, :], bgate[:, :, :], 1.0, 0.5, ALU.add, ALU.mult)
                    dve.wait_ge(blk_hi, 1)
                    v.tensor_tensor(flat(ys_lo[:, :, :]), flat(nqT[:, :, :]), flat(ys_hi[:, :, :]).bitcast(f32), ALU.subtract).then_inc(blk_lo, 1)
                    angles(4)
                    scan_pair(3)
                    dve.wait_ge(evac("ck"), ev("ck"))
                    dve.wait_ge(evac("cv"), ev("cv"))
                    link(v.tensor_tensor(hid_q, hid_y, hid_y, ALU.mult))
                    link(v.tensor_scalar(hid_q, hid_q, 0.044715, 1.0, ALU.mult, ALU.add))
                    v.tensor_tensor(hid_q, hid_q, hid_y, ALU.mult).then_inc(hid_arg, 1)
                    dve.wait_ge(hid_tanh, 1)
                    link(v.tensor_scalar(hid_q, hid_q, 0.5, 0.5, ALU.mult, ALU.add))
                    link(v.tensor_tensor(hid[:, :, :, :].rearrange("p m k n -> p (m k n)"), hid_q, hid_y, ALU.mult))
                    for k in range(2):
                        i = v.tensor_copy(hid8[:, k].rearrange("p (h g) n -> p h g n", h=NKV),
                                          bc(hid[:, 1, k].rearrange("p (h n) -> p h n", h=NKV).unsqueeze(2), [P, NKV, 4, 16]))
                    i.then_inc(hid_ready, 1)
                    angles(5)
                    scan_pair(4)
                    s5_out(1)
                    gate_times("s5")
                    angles(6)
                    scan_pair(5)
                    gate_times("lru")
                    angles(7)
                    scan_pair(6)
                    s5_out(2)
                    scan_pair(7)
                    s5_out(3)
                    dve.wait_ge(y_used, KB)
                    yf = flat(y_s5[:, :, :])
                    link(v.tensor_tensor(gelu_t, yf, yf, ALU.mult))
                    link(v.tensor_scalar(gelu_t, gelu_t, 0.044715, 1.0, ALU.mult, ALU.add))
                    v.tensor_tensor(gelu_t, gelu_t, yf, ALU.mult).then_inc(z_arg, 1)
                    dve.wait_ge(evac("u_lru"), ev("u_lru"))

                    def tap(k, t):
                        return vec[:, V_CONV + KB * k + t:V_CONV + KB * k + t + 1]

                    for t in range(KB):
                        i = v.tensor_scalar(xc[:, t, :], u_lru[:, t, 0:T], tap(0, t), vec[:, V_CONVB + t:V_CONVB + t + 1],
                                            ALU.mult, ALU.add)
                    link(i)
                    for k in range(1, 4):
                        for t in range(KB):
                            i = v.scalar_tensor_tensor(xc[:, t, :], u_lru[:, t, k:k + T], tap(k, t), xc[:, t, :], ALU.mult, ALU.add)
                        if k < 3:
                            link(i)
                    i.then_inc(xc_ready, 1)
                    dve.wait_ge(z_tanh, 1)
                    link(v.tensor_scalar(gelu_t, gelu_t, 0.5, 0.5, ALU.mult, ALU.add))
                    v.tensor_tensor(yf, yf, gelu_t, ALU.mult).then_inc(z_ready, 1)
                    dve.wait_ge(z_hi, 1)
                    v.tensor_tensor(flat(ys_lo[:, :, :]), yf, flat(ys_hi[:, :, :]).bitcast(f32), ALU.subtract).then_inc(z_lo, 1)

                    def rope_ret(n, name):
                        src = pr(name)[:, :].rearrange("p (a h c) -> p a h c", a=TT, h=NH_RET)
                        shape = [P, TT, NH_RET, 64]
                        cos = bc(cst("ret_cos").rearrange("p (a c) -> p a c", a=TT).unsqueeze(2), shape)
                        sin = bc(cst("ret_sin").rearrange("p (a c) -> p a c", a=TT).unsqueeze(2), shape)
                        lo, hi = slice(0, 64), slice(64, 128)
                        dve.wait_ge(chunk_done, ch(name))
                        if n:
                            dve.wait_ge(qkT_done, n)
                        v.tensor_tensor(ro4[:, :, :, lo], src[:, :, :, lo], cos, ALU.mult)
                        v.tensor_tensor(rope_t[:, 0], src[:, :, :, hi], sin, ALU.mult)
                        v.tensor_tensor(ro4[:, :, :, hi], src[:, :, :, hi], cos, ALU.mult)
                        v.tensor_tensor(rope_t[:, 1], src[:, :, :, lo], sin, ALU.mult).then_inc(evac(name), 1)
                        dve.wait_ge(evac(name), ev(name))
                        v.tensor_tensor(ro4[:, :, :, lo], ro4[:, :, :, lo], rope_t[:, 0], ALU.subtract)
                        v.tensor_tensor(ro4[:, :, :, hi], ro4[:, :, :, hi], rope_t[:, 1], ALU.add).then_inc(rope_ready, 1)

                    rope_ret(0, "ret_q")
                    rope_ret(1, "ret_k")
                    dve.wait_ge(lru_act, 4 * KB)
                    link(v.tensor_tensor(l_r, l_a, l_a, ALU.mult))
                    v.scalar_tensor_tensor(flat(l_i), flat(l_i), 1.0, flat(xc), ALU.add, ALU.mult)
                    v.scalar_tensor_tensor(flat(l_m), flat(l_r), 1.0, flat(l_m), ALU.add, ALU.mult).then_inc(lru_m2, 1)

                    def rope_nsa(x4):
                        shape = [P, TT, NHQ, 8]
                        cos = bc(cst("nsa_cos").rearrange("p (a c) -> p a c", a=TT).unsqueeze(2), shape)
                        sin = bc(cst("nsa_sin").rearrange("p (a c) -> p a c", a=TT).unsqueeze(2), shape)
                        x1, x2_ = x4[:, :, :, 0:8], x4[:, :, :, 8:16]
                        v.tensor_tensor(rope_n[:, 0], x1, cos, ALU.mult)
                        v.tensor_tensor(rope_n[:, 1], x2_, sin, ALU.mult)
                        v.tensor_tensor(rope_n[:, 2], x2_, cos, ALU.mult)
                        link(v.tensor_tensor(rope_n[:, 3], x1, sin, ALU.mult))
                        v.tensor_tensor(x1, rope_n[:, 0], rope_n[:, 1], ALU.subtract)
                        v.tensor_tensor(x2_, rope_n[:, 2], rope_n[:, 3], ALU.add).then_inc(nrope_ready, 1)

                    rope_nsa_kd = kd[:, :, :, :, :, :].rearrange("p a y h u d -> p a (y h u) d")
                    dve.wait_ge(evac("nsa_kv"), ev("nsa_kv"))
                    dve.wait_ge(evac("nsa_q"), ev("nsa_q"))
                    rope_nsa(nq4)
                    dve.wait_ge(nrope_ready, 1)
                    rope_nsa(rope_nsa_kd)
                    dve.wait_ge(nrope_ready, 2)
                    dve.wait_ge(chunk_done, ch("glu_a"))
                    for t in range(KB):
                        i = v.tensor_scalar(glu_v[:, t * T:(t + 1) * T], pr("glu_a")[:, t * T:(t + 1) * T],
                                            vec[:, V_BGLU + t:V_BGLU + t + 1], 0.5, ALU.add, ALU.mult)
                    i.then_inc(evac("glu_a"), 1)
                    dve.wait_ge(evac("glu_a"), ev("glu_a"))
                    dve.wait_ge(evac("glu_b"), ev("glu_b"))
                    link(v.scalar_tensor_tensor(glu_v, glu_t, 1.0, glu_v, ALU.add, ALU.mult))
                    gated("s5", glu_v)
                    lo_of_gated("s5")

                    def decay_scores(h):
                        dve.wait_ge(rs_done, h + 1)
                        if h >= 2:
                            dve.wait_ge(ro_done, h - 1)
                        dec = cst("decay").rearrange("p (h t) -> p h t", h=NH_RET)[:, h, :]
                        v.tensor_tensor(ret_s[:, h % 2, 0:T], M[:, h % 2, 0:T], dec, ALU.mult)
                        v.tensor_tensor(ret_s[:, h % 2, T:T + P], M[:, h % 2, T:T + P], dec[:, 0:P], ALU.mult).then_inc(rs_ready, 1)

                    decay_scores(0)
                    decay_scores(1)
                    branch("s5", 0)
                    dve.wait_ge(lru_sqrt, 1)
                    link(v.tensor_tensor(l_i, l_i, l_m, ALU.mult))
                    for t in range(KB):
                        i = v.tensor_tensor_scan(l_h[:, t, :], l_a[:, t, :], l_i[:, t, :], 0.0, ALU.mult, ALU.add)
                    link(i)
                    gated("lru", flat(l_h))
                    branch("s5", 1)
                    decay_scores(2)
                    decay_scores(3)
                    lo_of_gated("lru")
                    dve.wait_ge(ro_done, NH_RET)
                    o_ret = MF[:, 1024:2048].rearrange("p (i c) -> p i c", c=P)
                    for n in range(TT * NH_RET):
                        i = v.bn_stats(bn[:, n, :], o_ret[:, n, :])
                    link(i)
                    for n in range(TT * NH_RET):
                        i = v.bn_aggr(mv[:, n, :], bn[:, n, :])
                    link(i)
                    v.tensor_scalar(st[:, 80:88], mv[:, :, 1], EPS_RET, None, ALU.add).then_inc(rvar, 1)
                    dve.wait_ge(cw_done, 1)
                    kps = M[0:32, 0, 0:HD]
                    cc, ss = cst("cmp_cos")[0:32], cst("cmp_sin")[0:32]
                    v.tensor_copy(kc[:, :, :], bc(kps.unsqueeze(1), [32, 2, HD]))
                    v.tensor_tensor(kc_t[:, 0], kps[:, 0:8], cc, ALU.mult)
                    v.tensor_tensor(kc_t[:, 1], kps[:, 8:16], ss, ALU.mult)
                    v.tensor_tensor(kc_t[:, 2], kps[:, 8:16], cc, ALU.mult)
                    link(v.tensor_tensor(kc_t[:, 3], kps[:, 0:8], ss, ALU.mult))
                    v.tensor_tensor(kc[:, :, 0:8], bc(kc_t[:, 0].unsqueeze(1), [32, 2, 8]), bc(kc_t[:, 1].unsqueeze(1), [32, 2, 8]), ALU.subtract)
                    v.tensor_tensor(kc[:, :, 8:16], bc(kc_t[:, 2].unsqueeze(1), [32, 2, 8]), bc(kc_t[:, 3].unsqueeze(1), [32, 2, 8]), ALU.add).then_inc(kc_ready, 1)
                    v.tensor_tensor(vbd[:, :, :], bc(M[:, 0, HD:2 * HD].unsqueeze(1), [P, NHQ, HD]),
                                    bc(cst("head").unsqueeze(2), [P, NHQ, HD]), ALU.mult).then_inc(vbd_ready, 1)
                    dve.wait_ge(rrstd, 1)
                    for n in range(TT * NH_RET):
                        i = v.tensor_scalar(ro[:, n * P:(n + 1) * P], o_ret[:, n, :], mv[:, n, 0:1], st[:, 88 + n:89 + n],
                                            ALU.subtract, ALU.mult)
                    i.then_inc(rn_ready, 1)
                    dve.wait_ge(cs_done, 1)
                    shape = [P, TT, 4, 16]
                    add = bc(cst("cmp_add").rearrange("p (a n) -> p a n", a=TT).unsqueeze(2), shape)
                    keep = bc(cst("cmp_keep").rearrange("p (a n) -> p a n", a=TT).unsqueeze(2), shape)
                    for e_ in range(2):
                        i = v.tensor_tensor(cmp_s[:, e_], M[:, e_, 0:P].rearrange("p (a h n) -> p a h n", a=TT, h=4), add, ALU.add)
                    link(i)
                    cs2 = cols(3072, 256).rearrange("p (i n) -> p i n", n=16)
                    link(v.tensor_reduce(st[:, 8:24], cs2, AX, ALU.max))
                    v.tensor_tensor(cs2, cs2, bc(st[:, 8:24].unsqueeze(2), [P, 16, 16]), ALU.subtract).then_inc(cs_sub, 1)
                    dve.wait_ge(cs_exp, 1)
                    for e_ in range(2):
                        i = v.tensor_tensor(cmp_s[:, e_], cmp_s[:, e_], keep, ALU.mult)
                    link(i)
                    link(v.tensor_reduce(st[:, 24:40], cs2, AX, ALU.add))
                    link(v.tensor_scalar(st[:, 24:40], st[:, 24:40], 1e-30, None, ALU.max))
                    link(v.reciprocal(st[:, 24:40], st[:, 24:40]))
                    coef = st[:, 24:40].rearrange("p (e a h) -> p e a h", e=2, a=TT)
                    gates0 = bgate[:, :, 0:8].rearrange("p a (h e) -> p e a h", e=2)
                    link(v.tensor_tensor(coef, coef, gates0, ALU.mult))
                    cp = cmp_p.rearrange("p (a h e n) -> p e a h n", a=TT, h=4, e=2)
                    for e_ in range(2):
                        i = v.tensor_tensor(cp[:, e_], cmp_s[:, e_], bc(coef[:, e_].unsqueeze(3), shape), ALU.mult)
                    i.then_inc(cp_ready, 1)

                    def attention_max(i):
                        dve.wait_ge(at_s, i + 1)
                        if i:
                            dve.wait_ge(at_pT, i)
                        causal = cst("causal")
                        v.tensor_tensor(prob[:, 0:1024].rearrange("p (b n) -> p b n", b=4),
                                        MF[:, 0:1024].rearrange("p (b n) -> p b n", b=4),
                                        bc(causal.unsqueeze(1), [P, 4, T]), ALU.add)
                        link(v.tensor_tensor(prob[:, 1024:1536].rearrange("p (b n) -> p b n", b=4),
                                             M[:, 2, :].rearrange("p (b n) -> p b n", b=4),
                                             bc(causal[:, P:T].unsqueeze(1), [P, 4, P]), ALU.add))
                        v.tensor_reduce(st[:, 40:44], prob[:, 0:1024].rearrange("p (b n) -> p b n", b=4), AX, ALU.max, negate=True)
                        v.tensor_reduce(st[:, 44:48], prob[:, 1024:1536].rearrange("p (b n) -> p b n", b=4), AX, ALU.max,
                                        negate=True).then_inc(at_max, 1)

                    def attention_out(i):
                        y, h = i // NKV, i % NKV
                        dve.wait_ge(at_exp, 8 * (i + 1))
                        link(v.reciprocal(st[:, 56:64], st[:, 48:56]))
                        cf = st[:, 64:72].rearrange("p (a g) -> p a g", a=TT)
                        link(v.tensor_tensor(cf, st[:, 56:64].rearrange("p (a g) -> p a g", a=TT),
                                             bgate[:, :, 8 * (y + 1) + 4 * h:8 * (y + 1) + 4 * h + 4], ALU.mult))
                        dve.wait_ge(at_o, i + 1)
                        src = M[:, 3, :].rearrange("p (a g d) -> p a g d", a=TT, g=4)
                        cfb = bc(cf.unsqueeze(3), [P, TT, 4, HD])
                        dst = no4[:, :, 4 * h:4 * h + 4, :]
                        if y == 0:
                            v.tensor_tensor(dst, src, cfb, ALU.mult).then_inc(at_no, 1)
                            dve.wait_ge(at_no, i + 1)
                        else:
                            tmp = att_t.rearrange("p (a g d) -> p a g d", a=TT, g=4)
                            link(v.tensor_tensor(tmp, src, cfb, ALU.mult))
                            v.tensor_tensor(dst, dst, tmp, ALU.add).then_inc(at_no, 1)

                    branch("lru", 0)
                    attention_max(0)
                    branch("lru", 1)
                    gate_times("ret")
                    dve.wait_ge(yr_ready, 1)
                    gated("ret", flat(qT[:, :, :]))
                    lo_of_gated("ret")
                    attention_out(0)
                    attention_max(1)
                    attention_out(1)
                    attention_max(2)
                    branch("ret", 0)
                    branch("ret", 1)
                    attention_out(2)
                    attention_max(3)
                    gate_times("nsa")
                    attention_out(3)
                    dve.wait_ge(co_done, 1)
                    dve.wait_ge(at_no, 4)
                    v.tensor_tensor(nq, nq, MF[:, 0:1024], ALU.add).then_inc(no_cmp, 1)
                    dve.wait_ge(yn_ready, 1)
                    gated("nsa", flat(nqT[:, :, :]))
                    lo_of_gated("nsa")
                    branch("nsa", 0)
                    branch("nsa", 1)
                    for b in range(4):
                        dve.wait_ge(mhi_done, b + 1)
                        v.tensor_tensor(flat(h_lo[:, 2 * b:2 * b + 2, :]), M[:, b, :],
                                        flat(h_hi[:, 2 * b:2 * b + 2, :]).bitcast(f32), ALU.subtract).then_inc(mlo_done, 1)
                    for half in range(2):
                        full = f"out_{half}"
                        dst = x[:, :, 512 * half:512 * half + 512]
                        dve.wait_ge(chunk_done, ch(full))
                        v.scalar_tensor_tensor(dst, pr(full)[:, :].rearrange("p (a n) -> p a n", a=TT), 0.25, dst,
                                               ALU.mult, ALU.add).then_inc(evac(full), 1)

                @block.tensor
                def _(pe):
                    mm = nc.tensor.matmul

                    def tr(dst, src, rows_=P):
                        return nc.tensor.transpose(dst, src, ident[0:rows_, 0:rows_])

                    def split_product(dst, left, right, start, stop):
                        for n, (i, j) in enumerate(((0, 0), (0, 1), (1, 0))):
                            last = mm(dst, left[i], right[j], start=start and n == 0, stop=stop and n == 2, skip_group_check=True)
                        return last

                    def chunk(name, part=2):
                        c = CHUNK[name]
                        _, kt, w = CHUNKS[c]
                        first = UNIT_END[c - 1] if c else 0
                        n_units = UNIT_END[c] - first
                        kind = name.split("_")[0]
                        todo = {0: range(n_units // 2), 1: range(n_units // 2, n_units), 2: range(n_units)}[part]
                        ps = pr(name)
                        if c >= 2 and part != 1:
                            pe.wait_ge(evacuated[c % 2], c // 2)
                        for n in todo:
                            u = first + n
                            _, k0, nk, _ = UNITS[u]
                            pe.wait_ge(lo_done, u + 1)
                            s = u % N_SPLIT
                            for kk in range(nk):
                                k = k0 + kk
                                st_, sp_ = k == 0, k == kt - 1
                                if name == "u_s5":
                                    pe.wait_ge(hlo_done, k + 1)

                                def wt(lo, hi):
                                    return tuple(t[:, s, kk * w + lo:kk * w + hi] for t in (w_hi, w_lo))

                                def ht(lo, hi, pair=(h_hi, h_lo)):
                                    return tuple(t[:, k, lo:hi] for t in pair)

                                if kind == "u" or kind == "gate":
                                    for m in range(4):
                                        last = split_product(ps[:, m * T:(m + 1) * T], wt(m * P, (m + 1) * P), ht(0, T), st_ and m % 2 == 0, sp_)
                                elif kind == "glu":
                                    for m in range(4):
                                        last = split_product(ps[:, m * T:(m + 1) * T], wt(m * P, (m + 1) * P), ht(0, T, (ys_hi, ys_lo)), st_ and m % 2 == 0, sp_)
                                elif kind == "cmp":
                                    for m in range(2):
                                        last = split_product(ps[:, m * T:(m + 1) * T], wt(m * P, (m + 1) * P), ht(0, T), st_ and m == 0, sp_)
                                    for t in range(TT):
                                        last = split_product(ps[:, 512 + 24 * t:536 + 24 * t], ht(t * P, (t + 1) * P), wt(256, CMP_W), st_ and t == 0, sp_)
                                elif kind in ("ck", "cv"):
                                    m = kind == "cv"
                                    blk = tuple(flat(t[:, :, :])[:, (16 * m + k) * 32:(16 * m + k + 1) * 32] for t in (ys_hi, ys_lo))
                                    for half in range(2):
                                        last = split_product(ps[:, 512 * half:512 * half + 32], wt(half * P, (half + 1) * P), blk, st_, sp_)
                                else:
                                    pair = (ys_hi, ys_lo) if kind == "branch" else (h_hi, h_lo)
                                    for t in range(TT):
                                        last = split_product(ps[:, 512 * t:512 * t + w], ht(t * P, (t + 1) * P, pair), wt(0, w), st_, sp_)
                            if n == n_units - 1:
                                last.then_inc(chunk_done, 1)
                            else:
                                last.then_inc(unit_used, 1)

                    pe.wait_ge(dt_rows, 1)
                    tr(proj[1][:, 0:V_ROWS], rows[0:V_ROWS, :], V_ROWS).then_inc(vecT_done, 1)
                    tr(proj[1][:, P:P + 32], rows2[:, :], 32).then_inc(vecT_done, 1)
                    pe.wait_ge(x_norm, TT)
                    for k in range(KD):
                        for t in range(TT):
                            last = tr(M[:, k // 2, (k % 2) * T + t * P:(k % 2) * T + (t + 1) * P], merged[:, t, k * P:(k + 1) * P])
                        if k % 2:
                            last.then_inc(xT_done, 1)
                    chunk("u_s5")
                    pe.wait_ge(hlo_done, KD)
                    pe.wait_ge(b_ready, 2)
                    for f in range(2):
                        for q in range(KB):
                            last = tr(M[:, 2 + f, q * P:(q + 1) * P],
                                      b_exp[:, f, 4 * q:4 * q + 4].rearrange("p s g c -> p (s g c)"))
                    last.then_inc(bT_done, 1)
                    pe.wait_ge(c_ready, 2)
                    for f in range(2):
                        for q in range(KB):
                            last = tr(M[:, f, q * P:(q + 1) * P], c_nat[:, f, q].rearrange("p g n -> p (g n)"))
                    last.then_inc(cT_done, 1)

                    def state_inputs(p):
                        if p == 0:
                            pe.wait_ge(bcT_ready, 2)
                            pe.wait_ge(evac("u_s5"), ev("u_s5"))
                        else:
                            pe.wait_ge(bu_used, p)
                        q = p // 2
                        for j in range(2):
                            r = slice(32 * (2 * (p % 2) + j), 32 * (2 * (p % 2) + j) + 32)
                            for f in range(2):
                                last = mm(M[:, j, f * T:(f + 1) * T], bT[r, f, q, :], u_s5[r, q, :], start=True, stop=True)
                        last.then_inc(bu_done, 1)

                    def state_outputs(p):
                        q = p // 2
                        pe.wait_ge(h_done, p + 1)
                        if q >= 2 and p % 2 == 0:
                            pe.wait_ge(y_used, q - 1)
                        for j in range(2):
                            r = slice(32 * (2 * (p % 2) + j), 32 * (2 * (p % 2) + j) + 32)
                            dst = M[r, 2 + q % 2, 0:T]
                            for f in range(2):
                                last = mm(dst, cT[:, f, q, r], s5_h[:, p % 2, f, j, :], start=f == 0, stop=f == 1)
                        last.then_inc(y_done, 1)

                    pe.wait_ge(vec_ready, 1)
                    chunk("u_lru")
                    state_inputs(0)
                    chunk("ret_v")
                    state_inputs(1)
                    state_outputs(0)
                    chunk("nsa_kv")
                    state_inputs(2)
                    state_outputs(1)
                    chunk("cmp")
                    state_inputs(3)
                    state_outputs(2)
                    pe.wait_ge(blk_lo, 1)
                    chunk("ck")
                    chunk("cv")
                    state_inputs(4)
                    state_outputs(3)
                    chunk("gate_s5")
                    state_inputs(5)
                    state_outputs(4)
                    chunk("gate_lru")
                    state_inputs(6)
                    state_outputs(5)
                    chunk("merge_s5_0")
                    state_inputs(7)
                    state_outputs(6)
                    chunk("merge_s5_1")
                    state_outputs(7)
                    chunk("ret_q")
                    pe.wait_ge(xc_ready, 1)
                    pe.wait_ge(wl_loaded, 64)
                    pe.wait_ge(y_used, KB)
                    for f, w in enumerate((wa, wx)):
                        for t in range(KB):
                            last = mm(MF[:, f * 1024 + t * T:f * 1024 + (t + 1) * T], w[:, t, :], xc[:, t, :], start=True, stop=True)
                    last.then_inc(lru_mm, 1)
                    chunk("ret_k")

                    def blocks_T(at, src):
                        for n in range(4):
                            for t in range(TT):
                                last = tr(MF[:, at + n * T + t * P:at + n * T + (t + 1) * P], src[:, (4 * t + n) * P:(4 * t + n + 1) * P])
                        return last

                    pe.wait_ge(rope_ready, 1)
                    pe.wait_ge(lru_act, 2 * KB)
                    blocks_T(0, ro).then_inc(qkT_done, 1)
                    chunk("nsa_q")
                    pe.wait_ge(rope_ready, 2)
                    blocks_T(1024, ro).then_inc(qkT_done, 1)
                    pe.wait_ge(z_lo, 1)
                    chunk("glu_a")
                    pe.wait_ge(nrope_ready, 1)
                    pe.wait_ge(qkT_ready, 1)
                    blocks_T(0, nq).then_inc(nT_done, 1)
                    chunk("glu_b")
                    pe.wait_ge(nrope_ready, 2)
                    pe.wait_ge(qkT_ready, 2)
                    blocks_T(1024, kd[:, :, :, :, :, :].rearrange("p a y h u d -> p (a y h u d)")).then_inc(nT_done, 1)
                    pe.wait_ge(nT_ready, 1)

                    def ret_scores(h):
                        if h >= 2:
                            pe.wait_ge(rs_ready, h - 1)
                        mm(M[:, h % 2, 0:T], kT[:, h, 0:P], qT[:, h, :], start=True, stop=True)
                        mm(M[:, h % 2, T:T + P], kT[:, h, P:T], qT[:, h, P:T], start=True, stop=True).then_inc(rs_done, 1)

                    def ret_out(h):
                        pe.wait_ge(rs_ready, h + 1)
                        e = slice(h * P, (h + 1) * P)
                        mm(M[:, 2, e], ret_s[:, h % 2, 0:P], ret_v[:, 0, e], start=True, stop=True)
                        mm(M[:, 3, e], ret_s[:, h % 2, P:T], ret_v[:, 0, e], start=True, stop=False)
                        mm(M[:, 3, e], ret_s[:, h % 2, T:T + P], ret_v[:, 1, e], start=False, stop=True).then_inc(ro_done, 1)

                    ret_scores(0)
                    ret_scores(1)
                    pe.wait_ge(yg_lo, 1)
                    chunk("branch_s5_0")
                    pe.wait_ge(nT_ready, 2)
                    ret_out(0)
                    ret_out(1)
                    ret_scores(2)
                    ret_scores(3)
                    chunk("branch_s5_1")
                    chunk("merge_lru_0", 0)
                    ret_out(2)
                    ret_out(3)
                    pe.wait_ge(cw_loaded, 32)
                    pe.wait_ge(hid_ready, 1)
                    for k in range(2):
                        mm(M[0:32, 0, 0:HD], hid[:, 0, k, :], cw2[:, 0, k, :], start=k == 0, stop=k == 1)
                    for k in range(2):
                        last = mm(M[:, 0, HD:2 * HD], hid8[:, k].rearrange("p h n -> p (h n)"), cw2[:, 1, k, :], start=k == 0, stop=k == 1)
                    last.then_inc(cw_done, 1)
                    chunk("merge_lru_0", 1)
                    pe.wait_ge(kc_ready, 1)
                    tr(M[:, 1, 0:32], kc[:, :, :].rearrange("p u d -> p (u d)"), 32).then_inc(kcT_done, 1)
                    chunk("merge_lru_1", 0)
                    pe.wait_ge(rn_ready, 1)
                    blocks_T(1024, ro).then_inc(rnT_done, 1)
                    pe.wait_ge(vbd_ready, 1)
                    pe.wait_ge(kcT_ready, 1)
                    for e in range(2):
                        r = slice(64 * e, 64 * e + 64)
                        for t in range(TT):
                            for h in range(4):
                                at = t * 64 + h * 16
                                last = mm(M[:, e, at:at + 16], nqT[r, h, t * P:(t + 1) * P], kcT[r, (h // 2) * 16:(h // 2) * 16 + 16],
                                          start=True, stop=True)
                    last.then_inc(cs_done, 1)
                    chunk("merge_lru_1", 1)
                    pe.wait_ge(cp_ready, 1)
                    pe.wait_ge(yr_ready, 1)
                    for t in range(TT):
                        last = tr(M[:, 3, t * P:(t + 1) * P], cmp_p[:, t * P:(t + 1) * P])
                    last.then_inc(cpT_done, 1)

                    def attention_scores(i):
                        h = i % NKV
                        if i:
                            pe.wait_ge(at_pT_ready, i)
                        for e in range(2):
                            r = slice(64 * e, 64 * e + 64)
                            def small_():
                                for n in range(2):
                                    at = (2 * e + n) * P
                                    last_ = mm(M[:, 2, at:at + P], nqT[r, 2 * h + n, 0:P], nkT[r, i, 0:P], start=True, stop=True)
                                return last_
                            if e == 0:
                                small_().then_inc(at_even, 1)
                            for n in range(2):
                                mm(M[:, e, n * T:(n + 1) * T], nqT[r, 2 * h + n, P:T], nkT[r, i, :], start=True, stop=True)
                            if e == 1:
                                pe.wait_ge(at_even, i + 1)
                                last = small_()
                        last.then_inc(at_s, 1)

                    def attention_T(i):
                        pe.wait_ge(at_exp, 8 * (i + 1))
                        for b in range(12):
                            last = tr(MF[:, b * P:(b + 1) * P], prob[:, b * P:(b + 1) * P])
                        last.then_inc(at_pT, 1)

                    def attention_product(i):
                        pe.wait_ge(at_pT_ready, i + 1)
                        if i:
                            pe.wait_ge(at_no, i)
                        for b, g in enumerate((0, 2, 1, 3)):
                            mm(M[:, 3, g * HD:(g + 1) * HD], probT[:, 8 + b, :], nv[:, 0, i, :], start=True, stop=True)
                            mm(M[:, 3, 256 + g * HD:256 + (g + 1) * HD], probT[:, 2 * b, :], nv[:, 0, i, :], start=True, stop=False)
                            last = mm(M[:, 3, 256 + g * HD:256 + (g + 1) * HD], probT[:, 2 * b + 1, :], nv[:, 1, i, :], start=False, stop=True)
                        last.then_inc(at_o, 1)

                    pe.wait_ge(yg_lo, 2)
                    chunk("branch_lru_0")
                    attention_scores(0)
                    chunk("branch_lru_1")
                    chunk("gate_ret", 0)
                    attention_T(0)
                    chunk("gate_ret", 1)
                    pe.wait_ge(cpT_ready, 1)
                    attention_product(0)
                    attention_scores(1)
                    chunk("merge_ret_0")
                    attention_T(1)
                    chunk("merge_ret_1", 0)
                    attention_product(1)
                    attention_scores(2)
                    chunk("merge_ret_1", 1)
                    pe.wait_ge(yg_lo, 3)
                    chunk("branch_ret_0")
                    attention_T(2)
                    chunk("branch_ret_1")
                    attention_product(2)
                    attention_scores(3)
                    chunk("gate_nsa")
                    attention_T(3)
                    chunk("merge_nsa_0", 0)
                    attention_product(3)
                    pe.wait_ge(at_pT_ready, 4)
                    for t in range(TT):
                        last = mm(M[:, t, :], cmp_pT[:, t * P:(t + 1) * P], vbd[:, :, :].rearrange("p h d -> p (h d)"), start=True, stop=True)
                    last.then_inc(co_done, 1)
                    chunk("merge_nsa_0", 1)
                    pe.wait_ge(no_cmp, 1)
                    blocks_T(1024, nq).then_inc(noT_done, 1)
                    chunk("merge_nsa_1")
                    pe.wait_ge(yg_lo, 4)
                    chunk("branch_nsa_0")
                    chunk("branch_nsa_1")
                    pe.wait_ge(mt_free, 6)
                    for k in range(KD):
                        for t in range(TT):
                            last = tr(M[:, k // 2, (k % 2) * T + t * P:(k % 2) * T + (t + 1) * P], merged[:, t, k * P:(k + 1) * P])
                        if k % 2:
                            last.then_inc(mT_done, 1)
                    pe.wait_ge(mlo_done, 4)
                    chunk("out_0")
                    chunk("out_1")

            with nc.Block() as block:
                @block.gpsimd
                def _(gp):
                    gp.sem_clear(range(sems[0].num, sems[-1].num + 1))

        with nc.Block() as block:
            norm_loaded, sq, var, rstd, scaled, normed = fin
            g_row = mt[:, 0].rearrange("p a n -> p (a n)")

            @block.sync
            def _(sp):
                sp.dma_start(g_row, a["final_norm_g"].unsqueeze(0).to_broadcast([P, D])).then_inc(norm_loaded, 16)
                for t in range(TT):
                    sp.wait_ge(normed, t + 1)
                    sp.dma_start(out[0, t * P:(t + 1) * P, :], merged[:, t, :]).then_inc(prologue, 16)
                sp.wait_ge(prologue, 16 * TT)

            @block.scalar
            def _(act):
                for t in range(TT):
                    nc.scalar.activation(merged[:, t, :], x[:, t, :], ACT.Square, accum_out=st[:, 4 + t:5 + t]).then_inc(sq, 1)

            @block.gpsimd
            def _(gp):
                gp.wait_ge(var, 1)
                nc.gpsimd.tensor_tensor(st[:, 2:4], st[:, 0:2], m_half[:, 0:2], ALU.pow).then_inc(rstd, 1)

            @block.vector
            def _(dve):
                dve.wait_ge(sq, TT)
                nc.vector.tensor_scalar(st[:, 0:2], st[:, 4:6], 1.0 / D, EPS, ALU.mult, ALU.add).then_inc(var, 1)
                dve.wait_ge(rstd, 1)
                dve.wait_ge(norm_loaded, 16)
                for t in range(TT):
                    nc.vector.scalar_tensor_tensor(merged[:, t, :], x[:, t, :], st[:, 2 + t:3 + t], g_row,
                                                   ALU.mult, ALU.mult).then_inc(normed, 1)


_INS = ["x", "norm_g", "w_in", "lru_conv_w", "lru_conv_b", "lru_wa", "lru_ba", "lru_wx", "lru_bx", "lru_lambda",
        "s5_lambda_re", "s5_lambda_im", "s5_b_re", "s5_b_im", "s5_c_re", "s5_c_im", "s5_log_dt", "s5_d",
        "s5_w_glu", "s5_b_glu", "nsa_pos_k", "nsa_pos_v", "nsa_ck_w1", "nsa_ck_w2", "nsa_cv_w1", "nsa_cv_w2",
        "w_branch", "w_out", "final_norm_g"]


def kernel(**inputs):
    import numpy as _np
    import concourse.bacc as _bacc
    from concourse import mybir as _mybir
    from concourse.bass_utils import run_bass_kernel_spmd as _run

    nc = _bacc.Bacc("TRN2", target_bir_lowering=False, num_devices=1)
    arrays = {name: _np.ascontiguousarray(inputs[name]) for name in _INS}
    arrays["constants"] = shape_constants()
    aps = {n: nc.dram_tensor(f"in_{n}", v.shape, _mybir.dt.from_np(v.dtype), kind="ExternalInput").ap()
           for n, v in arrays.items()}
    result = nc.dram_tensor("out", (1, T, D), _mybir.dt.float32, kind="ExternalOutput").ap()
    hybrid_trunk(nc, aps, result)
    r = _run(nc, [{f"in_{n}": v for n, v in arrays.items()}], core_ids=[0])
    return r.results[0]["out"]
```

```python
import math
from contextlib import ExitStack

import numpy as np
import concourse.bass as bass
from concourse import mybir

P = 128
D = 1024
T = 256
TT = T // P
DEPTH = 2
BW = 512
KD = D // P
KB = BW // P
NH_RET = 4
HD_RET = 128
NHQ = 8
NKV = 2
HD = 64
NCMP = (T - 32) // 16 + 1
NS5 = 32 * 64 // P
EPS = 1e-6
EPS_RET = 1e-5
CMP_W = 280

COL_LRU, COL_S5, COL_RET, COL_NQ, COL_CMP, COL_KV, COL_BG, COL_GATE, COL_MERGE = (
    0, 512, 1024, 2560, 3072, 3328, 3840, 3864, 5912)
GATE_OF = {"lru": 0, "s5": 1, "ret": 2, "nsa": 3}

CHUNKS = [("u_s5", 8, 512), ("cmp", 8, CMP_W), ("u_lru", 8, 512), ("ret_v", 8, 512), ("nsa_kv", 8, 512),
          ("ck", 16, 256), ("gate_s5", 8, 512), ("cv", 16, 256), ("gate_lru", 8, 512),
          ("merge_s5_0", 8, 512), ("merge_s5_1", 8, 512), ("ret_q", 8, 512), ("ret_k", 8, 512),
          ("nsa_q", 8, 512), ("glu_a", 4, 512), ("glu_b", 4, 512), ("gate_ret", 8, 512), ("branch_s5_0", 4, 512),
          ("branch_s5_1", 4, 512), ("merge_lru_0", 8, 512), ("merge_lru_1", 8, 512),
          ("branch_lru_0", 4, 512), ("branch_lru_1", 4, 512),
          ("merge_ret_0", 8, 512), ("merge_ret_1", 8, 512), ("branch_ret_0", 4, 512),
          ("branch_ret_1", 4, 512), ("gate_nsa", 8, 512), ("merge_nsa_0", 8, 512),
          ("merge_nsa_1", 8, 512), ("branch_nsa_0", 4, 512), ("branch_nsa_1", 4, 512),
          ("out_0a", 4, 512), ("out_1a", 4, 512), ("out_0b", 4, 512), ("out_1b", 4, 512)]
CHUNK = {name: c for c, (name, _, _) in enumerate(CHUNKS)}
BRANCHES = ["s5", "lru", "ret", "nsa"]

UNITS, UNIT_END, UNIT_USED = [], [], []
for _c, (_name, _kt, _w) in enumerate(CHUNKS):
    if _name not in ("ck", "cv"):
        _k0 = 4 if _name[-1] == "b" and _name[:3] == "out" else 0
        UNITS += [(_c, k, 2, _w) for k in range(_k0, _k0 + _kt, 2)]
    UNIT_END.append(len(UNITS))
NU = len(UNITS)
for _u in range(NU):
    UNIT_USED.append((UNIT_USED[-1] if _u else 0) + (_u + 1 != UNIT_END[UNITS[_u][0]]))
N_RAW = 4
N_SPLIT = 5

V_NORM, V_CONV, V_CONVB, V_BA, V_BX, V_LAM, V_D, V_BGLU, V_LR, V_LI, V_DT, V_ROWS = (
    0, 8, 24, 28, 32, 36, 40, 44, 52, 68, 96, 112)

TWO_PI = 2.0 * math.pi
PI2_A = 6.28125
PI2_B = 0.0019350051879882812
PI2_C = TWO_PI - PI2_A - PI2_B
TURN = 6.2831845
ROUND = 12582912.0
GELU_C = math.sqrt(2.0 / math.pi)

CONST = {}
_at = 0
for _n, _s in (("ident", P), ("ret_cos", TT * 64), ("ret_sin", TT * 64), ("nsa_cos", TT * 8), ("nsa_sin", TT * 8),
               ("cmp_cos", 8), ("cmp_sin", 8), ("decay", NH_RET * T), ("causal", 2 * P), ("cmp_add", TT * 16),
               ("cmp_keep", TT * 16), ("head", NHQ), ("group", 2), ("time", T)):
    CONST[_n] = (_at, _s)
    _at += _s
N_CONST = _at


def shape_constants():
    f32 = np.float32
    out = np.zeros((P, N_CONST), f32)

    def put(name, a):
        at, size = CONST[name]
        out[:a.shape[0], at:at + size] = a.reshape(a.shape[0], size)

    def rope(pos, base, rot):
        half = rot // 2
        inv = (f32(base) ** (-np.arange(half, dtype=f32) * f32(2.0) / f32(rot))).astype(f32)
        ang = (pos.astype(f32)[..., None] * inv).astype(f32).astype(np.float64)
        return np.cos(ang).astype(f32), np.sin(ang).astype(f32)

    p = np.arange(P)
    tok = p[:, None] + P * np.arange(TT)[None, :]
    put("ident", np.eye(P, dtype=f32))
    c, s = rope(tok, 10000.0, HD_RET)
    put("ret_cos", c), put("ret_sin", s)
    c, s = rope(tok, 500000.0, HD // 4)
    put("nsa_cos", c), put("nsa_sin", s)
    c, s = rope((np.arange(32) % 16) * 16 + 31, 500000.0, HD // 4)
    put("cmp_cos", c), put("cmp_sin", s)
    gamma = 1.0 - np.exp(np.linspace(math.log(1 / 32), math.log(1 / 512), NH_RET))
    diff = np.arange(T)[None, :] - p[:, None]
    put("decay", np.stack([np.where(diff >= 0, g ** np.maximum(diff, 0), 0) for g in gamma], 1) * HD_RET ** -0.5)
    m = np.zeros((P, 2, P), f32)
    m[:, 1] = np.where(p[None, :] <= p[:, None], 0, -1e30)
    put("causal", m)
    n = np.arange(16)
    keep = (n * 16 + 31 <= tok[:, :, None]) & (n < NCMP)
    put("cmp_add", np.where(keep, 0, -1e30)), put("cmp_keep", keep * 1.0)
    put("head", ((p[:, None] // 16 == np.arange(NHQ)[None, :]) & (p[:, None] % 16 < NCMP)) * 1.0)
    put("group", ((p[:, None] // 16) % 2 == np.arange(2)[None, :]) * 1.0)
    put("time", np.broadcast_to(np.arange(T), (P, T)))
    return out


def hybrid_trunk(nc, a, out):
    f32, f32r = mybir.dt.float32, mybir.dt.float32r
    ALU, ACT, AX = mybir.AluOpType, mybir.ActivationFunctionType, mybir.AxisListType.X
    ctx = ExitStack()
    with ctx:
        def sb(name, shape, dt=f32):
            return ctx.enter_context(nc.sbuf_tensor(name, shape, dt))

        sems = []

        def sem(name):
            sems.append(ctx.enter_context(nc.semaphore(name)))
            return sems[-1]

        const = sb("const", [P, N_CONST])
        x = sb("x", [P, TT, D])
        raw = sb("raw", [P, N_RAW, 1024])
        w_hi = sb("w_hi", [P, N_SPLIT, 1024], f32r)
        w_lo = sb("w_lo", [P, N_SPLIT, 1024], f32r)
        h_hi = sb("h_hi", [P, KD, T], f32r)
        h_lo = sb("h_lo", [P, KD, T], f32r)
        ys_hi = sb("ys_hi", [P, KB, T], f32r)
        ys_lo = sb("ys_lo", [P, KB, T], f32r)
        merged = sb("merged", [P, TT, D])
        mt = sb("mt", [P, 2, TT, 512])
        gate = sb("gate", [P, 2, KB, T])
        rows = sb("rows", [P, P])
        rows2 = sb("rows2", [32, P])
        dt_in = sb("dt_in", [P, 2])
        vec = sb("vec", [P, V_ROWS])
        pos = sb("pos", [P, 2, 16])
        small = sb("small", [P, 30, 16])
        wa = sb("wa", [P, KB, P])
        wx = sb("wx", [P, KB, P])
        cw2 = sb("cw2", [P, 2, 2, HD])
        bT = sb("bT", [P, 2, KB, P])
        cT = sb("cT", [P, 2, KB, P])
        u_s5 = sb("u_s5", [P, KB, T])
        u_lru = sb("u_lru", [P, KB, T + 3])
        ret_v = sb("ret_v", [P, TT, BW])
        kd = sb("kd", [P, TT, 2, NKV, 2, HD])
        nv = sb("nv", [P, TT, 4, HD])
        hid = sb("hid", [P, 2, 2, 32])
        hid8 = sb("hid8", [P, 2, NHQ, 16])
        vbd = sb("vbd", [P, NHQ, HD])
        kc = sb("kc", [32, 2, HD])
        kcT = sb("kcT", [P, 32])
        bgate = sb("bgate", [P, TT, 24])
        st = sb("st", [P, 96])
        qT = sb("qT", [P, NH_RET, T])
        kT = sb("kT", [P, NH_RET, T])
        nqT = sb("nqT", [P, 4, T])
        nkT = sb("nkT", [P, 4, T])
        sc = sb("sc", [P, 7936])
        zero = sb("zero", [P, 1])
        half_pi = sb("half_pi", [P, 1])
        m_half = sb("m_half", [P, 8])
        proj = [ctx.enter_context(nc.psum_tensor(f"proj{i}", [P, 1024], f32)) for i in range(2)]
        M = ctx.enter_context(nc.psum_tensor("M", [P, 4, 512], f32))

        def cst(name):
            at, size = CONST[name]
            return const[:, at:at + size]

        def S(i, n=1):
            return small[:, i, :] if n == 1 else small[:, i:i + n, :]

        def cols(at, n):
            return sc[:, at:at + n]

        ident = cst("ident")
        cos_sin = cols(0, 2048).rearrange("p (b f j t) -> p b f j t", b=2, f=2, j=2)
        ang_a = cols(2048, 512).rearrange("p (j t) -> p j t", j=2)
        ang_s = cols(2560, 512).rearrange("p (j t) -> p j t", j=2)
        s5_t = cols(3072, 2048).rearrange("p (f j t) -> p f j t", f=4, j=2)
        s5_h = cols(5120, 2048).rearrange("p (b f j t) -> p b f j t", b=2, f=2, j=2)
        b_exp = cols(3072, 1024).rearrange("p (f s g c) -> p f s g c", f=2, s=NS5, g=2)
        b_tmp = cols(4096, 512).rearrange("p (f s c) -> p f s c", f=2, s=NS5)
        b_nat = cols(6656, 512).rearrange("p (f s c) -> p f s c", f=2, s=NS5)
        c_nat = cols(5120, 1024).rearrange("p (f q g n) -> p f q g n", f=2, q=KB, g=2)
        gelu_t = cols(2048, 1024)
        y_s5 = qT
        x2 = kT[:, 0:2, :].rearrange("p m (h t) -> p m h t", h=NKV)
        blocks = nqT[:, :, :].rearrange("p a (b h n) -> p (a b) h n", b=8, h=2)
        cmp_tm = qT[:, 2:4, :]
        hid_y = kT[:, 2, 0:128]
        hid_q = kT[:, 3, 0:128]
        xc = cols(0, 1024).rearrange("p (t n) -> p t n", t=KB)
        l_r = cols(1024, 1024).rearrange("p (t n) -> p t n", t=KB)
        l_i = cols(2048, 1024).rearrange("p (t n) -> p t n", t=KB)
        l_a = cols(3072, 1024).rearrange("p (t n) -> p t n", t=KB)
        l_m = cols(4096, 1024).rearrange("p (t n) -> p t n", t=KB)
        l_h = cols(5120, 1024).rearrange("p (t n) -> p t n", t=KB)
        ret_s = cols(6144, 768).rearrange("p (b n) -> p b n", b=2)
        rope_t = cols(6912, 1024).rearrange("p (f a h c) -> p f a h c", f=2, a=TT, h=NH_RET)
        rope_n = cols(6912, 512).rearrange("p (f a h c) -> p f a h c", f=4, a=TT, h=NHQ)
        ro = u_lru[:, :, :].rearrange("p a b -> p (a b)")[:, 0:1024]
        nq = u_s5[:, :, :].rearrange("p a b -> p (a b)")
        nq4 = nq.rearrange("p (a h c) -> p a h c", a=TT, h=NHQ)
        no4 = nq4
        prob = cols(0, 1536)
        probT = cols(1536, 1536).rearrange("p (b n) -> p b n", b=12)
        cmp_s = cols(3072, 256).rearrange("p (e a h n) -> p e a h n", e=2, a=TT, h=4)
        cmp_pT = cols(3328, 256)
        cmp_p = cols(3584, 256)
        att_t = cols(4096, 512)
        glu_v = cols(6912, 1024)
        glu_t = cols(0, 1024)
        bn = cols(6912, 48).rearrange("p (i n) -> p i n", n=6)
        mv = cols(6960, 16).rearrange("p (i n) -> p i n", n=2)
        kc_t = cols(7040, 32)[0:32].rearrange("p (f n) -> p f n", f=4)
        MF = M[:, :, :].rearrange("p b n -> p (b n)")

        x_loaded, const_loaded = (ctx.enter_context(nc.semaphore(n)) for n in ("x_loaded", "const_loaded"))
        cw1_loaded = sem("cw1_loaded")
        raw_loaded = [sem(f"raw_loaded{i}") for i in range(N_RAW)]
        hi_done, lo_done, unit_used = sem("hi_done"), sem("lo_done"), sem("unit_used")
        chunk_done = sem("chunk_done")
        evacuated = [sem("evacuated0"), sem("evacuated1")]
        dve_order = sem("dve_order")
        x_norm, xT_done = sem("x_norm"), sem("xT_done")
        hhi_done, hlo_done = sem("hhi_done"), sem("hlo_done")
        lam_abs, lam_exp, dt_exp, mag_arg, mag_exp = (sem(n) for n in ("lam_abs", "lam_exp", "dt_exp", "mag_arg", "mag_exp"))
        th_ready, th_sin = sem("th_ready"), sem("th_sin")
        b_ready, c_ready, bT_done, cT_done, bcT_ready = (sem(n) for n in ("b_ready", "c_ready", "bT_done", "cT_done", "bcT_ready"))
        ang_ready, trig_done, bu_done, bu_used, h_done, y_done = (sem(n) for n in (
            "ang_ready", "trig_done", "bu_done", "bu_used", "h_done", "y_done"))
        y_used = sem("y_used")
        z_arg, z_tanh, z_ready, z_hi, z_lo = (sem(n) for n in ("z_arg", "z_tanh", "z_ready", "z_hi", "z_lo"))
        cmp_read, cmpT_done, blk_ready = (sem(n) for n in ("cmp_read", "cmpT_done", "blk_ready"))
        hid_arg, hid_tanh, hid_ready = (sem(n) for n in ("hid_arg", "hid_tanh", "hid_ready"))
        gate_tanh, mt_free = (sem(n) for n in ("gate_tanh", "mt_free"))
        yg_ready, yg_hi, yg_lo = (sem(n) for n in ("yg_ready", "yg_hi", "yg_lo"))
        xc_ready, lru_mm, lru_act, lru_m2, lru_sqrt = (sem(n) for n in ("xc_ready", "lru_mm", "lru_act", "lru_m2", "lru_sqrt"))
        rope_ready, qkT_done, qkT_ready = sem("rope_ready"), sem("qkT_done"), sem("qkT_ready")
        rs_done, rs_ready, ro_done, rvar, rrstd, rn_ready, rnT_done, yr_ready = (sem(n) for n in (
            "rs_done", "rs_ready", "ro_done", "rvar", "rrstd", "rn_ready", "rnT_done", "yr_ready"))
        nrope_ready, nT_done, nT_ready = (sem(n) for n in (
            "nrope_ready", "nT_done", "nT_ready"))
        cw_done, kc_ready, vbd_ready, kcT_done, kcT_ready = (sem(n) for n in (
            "cw_done", "kc_ready", "vbd_ready", "kcT_done", "kcT_ready"))
        cs_done, cs_sub, cs_exp, cp_ready, cpT_done, cpT_ready, co_done, no_cmp = (sem(n) for n in (
            "cs_done", "cs_sub", "cs_exp", "cp_ready", "cpT_done", "cpT_ready", "co_done", "no_cmp"))
        at_even, at_s, at_max, at_exp, at_pT, at_pT_ready, at_o, at_no = (sem(n) for n in (
            "at_even", "at_s", "at_max", "at_exp", "at_pT", "at_pT_ready", "at_o", "at_no"))
        noT_done, yn_ready = sem("noT_done"), sem("yn_ready")
        mT_done, mhi_done, mlo_done = (sem(n) for n in ("mT_done", "mhi_done", "mlo_done"))
        x_half = sem("x_half")
        STAGE = ("vectors_loaded", "matrices_loaded", "raw_first", "dt_rows", "vecT", "vec_ready", "sq", "msq", "var", "rstd")
        nxt = {n: sem("next_" + n) for n in STAGE}
        first = {n: ctx.enter_context(nc.semaphore("first_" + n)) for n in STAGE}
        norm_loaded, normed, stored = (ctx.enter_context(nc.semaphore(n)) for n in ("norm_loaded", "normed", "stored"))

        raw_target = []
        _count = [0] * N_RAW
        for u, (c, _, _, _) in enumerate(UNITS):
            if u >= N_RAW:
                _count[u % N_RAW] += 32 if c == CHUNK["cmp"] else 16
            raw_target.append(_count[u % N_RAW])

        def ch(name):
            return CHUNK[name] + 1

        def wait_unit_read(eng, u):
            c = UNITS[u][0]
            if u + 1 == UNIT_END[c]:
                eng.wait_ge(chunk_done, c + 1)
            else:
                eng.wait_ge(unit_used, UNIT_USED[u])

        def pr(name):
            return proj[CHUNK[name] % 2]

        def evac(name):
            return evacuated[CHUNK[name] % 2]

        def ev(name):
            return CHUNK[name] // 2 + 1

        def cw1(n):
            return merged[:, n, :] if n < 2 else mt[:, n - 2].rearrange("p a n -> p (a n)")

        def flat(t):
            return t.rearrange("p a b -> p (a b)")

        def bc(ap, shape):
            return ap.to_broadcast(shape)

        def load_unit(sp, u, l, signal):
            c, k, n, w = UNITS[u]
            name = CHUNKS[c][0]
            
            dst = raw[:, u % N_RAW, 0:n * w].rearrange("p (k n) -> p k n", k=n)

            def load(d, src):
                sp.dma_start(d, src.rearrange("(k p) n -> p k n", p=P)).then_inc(signal, 16)

            def w_in(col, width, d=None):
                load(dst if d is None else d, a["w_in"][l][k * P:(k + n) * P, col:col + width])

            kind = name.split("_")[0]
            half = 512 * int(name[4] if kind == "out" else name[-1]) if kind in ("merge", "branch", "out") else 0
            if kind == "u":
                w_in(COL_S5 if name == "u_s5" else COL_LRU, w)
            elif kind == "ret":
                w_in(COL_RET + BW * "qkv".index(name[-1]), w)
            elif name == "nsa_q":
                w_in(COL_NQ, w)
            elif name == "nsa_kv":
                w_in(COL_KV, w)
            elif name == "cmp":
                w_in(COL_CMP, 256, dst[:, :, 0:256])
                w_in(COL_BG, 24, dst[:, :, 256:CMP_W])
            elif kind == "gate":
                w_in(COL_GATE + BW * GATE_OF[name[5:]], w)
            elif kind == "merge":
                w_in(COL_MERGE + D * GATE_OF[name[6:-2]] + half, w)
            elif kind == "glu":
                at = 512 * "ab".index(name[-1])
                load(dst, a["s5_w_glu"][l][k * P:(k + n) * P, at:at + w])
            elif kind == "branch":
                load(dst, a["w_branch"][l][GATE_OF[name[7:-2]]][k * P:(k + n) * P, half:half + w])
            else:
                load(dst, a["w_out"][l][k * P:(k + n) * P, half:half + w])


        def load_vectors(sp, l, signal):
            def load(dst, src):
                sp.dma_start(dst, src).then_inc(signal, 16)

            for name, at, n in (("norm_g", V_NORM, 8), ("lru_conv_w", V_CONV, 16), ("lru_conv_b", V_CONVB, 4),
                                ("lru_ba", V_BA, 4), ("lru_bx", V_BX, 4), ("lru_lambda", V_LAM, 4), ("s5_d", V_D, 4),
                                ("s5_b_glu", V_BGLU, 8), ("s5_lambda_re", V_LR, 16), ("s5_lambda_im", V_LI, 16)):
                src = a[name][l]
                if name == "lru_conv_w":
                    src = src.rearrange("k (t p) -> (k t) p", p=P)
                elif len(src.shape) == 2:
                    src = src.rearrange("(s g) n -> s (g n)", g=2)
                else:
                    src = src.rearrange("(t p) -> t p", p=P)
                load(rows[at:at + n, :], src)
            load(dt_in[V_DT:V_ROWS, :], a["s5_log_dt"][l].rearrange("(s g) -> s g", g=2))
            for m, name in enumerate(("nsa_pos_k", "nsa_pos_v")):
                load(rows2[16 * m:16 * m + 16, :], a[name][l].rearrange("(r s) d -> r (s d)", s=2))

        def load_matrices(sp, l, signal):
            def load(dst, src):
                sp.dma_start(dst, src).then_inc(signal, 16)

            for f, name in enumerate(("s5_b_re", "s5_b_im")):
                load(b_nat[:, f], a[name][l].rearrange("(s g) n c -> (g n) s c", g=2))
            for f, name in enumerate(("s5_c_re", "s5_c_im")):
                for g in range(2):
                    load(c_nat[:, f, :, g], a[name][l].rearrange("(q r) c n -> (r c) q n", q=KB))
            for tile, name in ((wa, "lru_wa"), (wx, "lru_wx")):
                for g in range(2):
                    load(tile[64 * g:64 * g + 64, :, 64 * g:64 * g + 64],
                         a[name][l].rearrange("(t g) i j -> g i t j", g=2)[g])
            for m, name in enumerate(("nsa_ck_w2", "nsa_cv_w2")):
                load(cw2[:, m], a[name][l].rearrange("(k p) d -> p k d", p=P))

        VECTORS_ALL, MATRICES_ALL, RAW_ALL = 16 * 13, 16 * 12, 16 * N_RAW

        def expand_dt(stage):
            nc.vector.tensor_copy(rows[V_DT:V_ROWS, :].rearrange("p (g n) -> p g n", g=2),
                                  bc(dt_in[V_DT:V_ROWS, :].unsqueeze(2), [16, 2, 64])).then_inc(stage["dt_rows"], 1)

        def turn_vectors(stage):
            for dst, src, n in ((M[:, 0, 0:V_ROWS], rows[0:V_ROWS, :], V_ROWS), (M[:, 0, P:P + 32], rows2[:, :], 32)):
                nc.tensor.transpose(dst, src, ident[0:n, 0:n]).then_inc(stage["vecT"], 1)

        def keep_vectors(stage):
            nc.vector.tensor_copy(vec[:, :], M[:, 0, 0:V_ROWS])
            nc.vector.tensor_copy(flat(pos[:, :, :]), M[:, 0, P:P + 32]).then_inc(stage["vec_ready"], 1)

        def squares(stage, half):
            for t in range(TT):
                e = slice(512 * half, 512 * half + 512)
                nc.scalar.activation(merged[:, t, e], x[:, t, e], ACT.Square,
                                     accum_out=st[:, 4 + 2 * half + t:5 + 2 * half + t]).then_inc(stage["sq"], 1)

        def mean_square(dve, stage):
            dve.wait_ge(stage["sq"], 2 * TT)
            nc.vector.tensor_tensor(st[:, 0:2], st[:, 4:6], st[:, 6:8], ALU.add).then_inc(stage["msq"], 1)
            dve.wait_ge(stage["msq"], 1)
            nc.vector.tensor_scalar(st[:, 0:2], st[:, 0:2], 1.0 / D, EPS, ALU.mult, ALU.add).then_inc(stage["var"], 1)

        def inverse_root(gp, stage):
            gp.wait_ge(stage["var"], 1)
            nc.gpsimd.tensor_tensor(st[:, 2:4], st[:, 0:2], m_half[:, 0:2], ALU.pow).then_inc(stage["rstd"], 1)

        with nc.Block() as block:
            @block.sync
            def _(sp):
                sp.dma_start(x[:, :, :], a["x"][0].rearrange("(t p) d -> p t d", p=P)).then_inc(x_loaded, 16)
                sp.wait_ge(first["dt_rows"], 1)
                load_vectors(sp, 0, first["vectors_loaded"])
                sp.dma_start(const[:, :], a["constants"]).then_inc(const_loaded, 16)
                for u in range(N_RAW):
                    load_unit(sp, u, 0, first["raw_first"])
                load_matrices(sp, 0, first["matrices_loaded"])
                sp.wait_ge(first["raw_first"], RAW_ALL)
                sp.wait_ge(first["matrices_loaded"], MATRICES_ALL)

            @block.gpsimd
            def _(gp):
                gp.memset(zero[:, :], 0.0)
                gp.memset(half_pi[:, :], math.pi / 2)
                gp.memset(m_half[:, :], -0.5)
                gp.memset(wa[:], 0.0)
                gp.memset(wx[:], 0.0)
                gp.memset(rows[:], 0.0).then_inc(first["dt_rows"], 1)
                gp.wait_ge(first["dt_rows"], 1)
                inverse_root(gp, first)

            @block.scalar
            def _(act):
                act.wait_ge(x_loaded, 16)
                for half in range(2):
                    squares(first, half)

            @block.vector
            def _(dve):
                mean_square(dve, first)
                dve.wait_ge(first["vectors_loaded"], VECTORS_ALL)
                expand_dt(first)
                dve.wait_ge(first["vecT"], 2)
                keep_vectors(first)

            @block.tensor
            def _(pe):
                pe.wait_ge(const_loaded, 16)
                pe.wait_ge(first["dt_rows"], 2)
                turn_vectors(first)

        with nc.Fori(0, DEPTH) as l:
            with nc.Block() as block:
                @block.sync
                def _(sp):
                    def load_cw1(name):
                        for n in range(4):
                            sp.dma_start(cw1(n).rearrange("p (k n) -> p k n", k=4),
                                         a[f"nsa_{name}_w1"][l][512 * n:512 * n + 512, :].rearrange("(k p) n -> p k n", p=P)
                                         ).then_inc(cw1_loaded, 16)

                    cw1_at = {8: "ck", UNIT_END[CHUNK["gate_s5"]] + 2: "cv"}
                    for u in range(N_RAW, NU):
                        if u in cw1_at:
                            name = cw1_at[u]
                            if name == "ck":
                                sp.wait_ge(xT_done, 4)
                            else:
                                sp.wait_ge(chunk_done, ch("ck"))
                            load_cw1(name)
                        if u == UNIT_END[CHUNK["merge_nsa_0"]]:
                            sp.wait_ge(at_max, 4)
                            load_vectors(sp, (l + 1) % DEPTH, nxt["vectors_loaded"])
                            load_matrices(sp, (l + 1) % DEPTH, nxt["matrices_loaded"])
                        sp.wait_ge(lo_done, u - N_RAW + 1)
                        load_unit(sp, u, l, raw_loaded[u % N_RAW])
                    for u in range(N_RAW):
                        sp.wait_ge(lo_done, max(w for w in range(NU) if w % N_RAW == u) + 1)
                        load_unit(sp, u, (l + 1) % DEPTH, nxt["raw_first"])
                    sp.wait_ge(nxt["raw_first"], RAW_ALL)
                    sp.wait_ge(nxt["matrices_loaded"], MATRICES_ALL)

                @block.gpsimd
                def _(gp):
                    done = [0]

                    def split_lo(upto):
                        for u in range(done[0], upto):
                            c, _, n, w = UNITS[u]
                            gp.wait_ge(hi_done, u + 1)
                            if u >= N_SPLIT:
                                wait_unit_read(gp, u - N_SPLIT)
                            nc.gpsimd.tensor_tensor(w_lo[:, u % N_SPLIT, 0:n * w], raw[:, u % N_RAW, 0:n * w],
                                                    w_hi[:, u % N_SPLIT, 0:n * w].bitcast(f32), ALU.subtract).then_inc(lo_done, 1)
                        done[0] = max(done[0], upto)

                    split_lo(UNIT_END[CHUNK["merge_lru_0"]] + 1)
                    gp.wait_ge(rvar, 1)
                    nc.gpsimd.tensor_tensor(st[:, 88:96], st[:, 80:88], m_half[:, :], ALU.pow).then_inc(rrstd, 1)
                    split_lo(NU)
                    inverse_root(gp, nxt)

                @block.scalar
                def _(act):
                    done = [0]

                    def run(out_, in_, func, signal=None, **kw):
                        i = nc.scalar.activation(out_, in_, func, **kw)
                        if signal is not None:
                            i.then_inc(signal, 1)

                    def cast_units(upto):
                        for u in range(done[0], upto):
                            c, _, n, w = UNITS[u]
                            if u >= N_RAW:
                                act.wait_ge(raw_loaded[u % N_RAW], raw_target[u])
                            if u >= N_SPLIT:
                                wait_unit_read(act, u - N_SPLIT)
                            run(w_hi[:, u % N_SPLIT, 0:n * w], raw[:, u % N_RAW, 0:n * w], ACT.Copy, hi_done)
                        done[0] = max(done[0], upto)

                    def next_cast(name):
                        cast_units(min(NU, UNIT_END[CHUNK[name]] + N_SPLIT - 1))
                        act.wait_ge(chunk_done, ch(name))

                    cast_units(2)
                    act.wait_ge(lam_abs, 1)
                    run(S(1)[:, 0:4], S(0)[:, 0:4], ACT.Exp, lam_exp, scale=-1.0)
                    run(S(8), vec[:, V_DT:V_ROWS], ACT.Exp, dt_exp)
                    for k in range(KD):
                        if k % 2 == 0:
                            act.wait_ge(xT_done, k // 2 + 1)
                        run(h_hi[:, k, :], M[:, k // 2, (k % 2) * T:(k % 2 + 1) * T], ACT.Copy, hhi_done,
                            scale=vec[:, V_NORM + k:V_NORM + k + 1])
                    cast_units(N_SPLIT)
                    act.wait_ge(mag_arg, 1)
                    run(S(10), S(9), ACT.Exp, mag_exp)
                    nc.scalar.preload_act_table_set("silu_and_others")
                    act.wait_ge(th_ready, 1)
                    run(S(13), S(12), ACT.Abs, th_sin)
                    act.wait_ge(th_sin, 1)
                    run(S(14), S(13), ACT.Sin, th_sin, bias=half_pi[:, 0:1], scale=-1.0)
                    run(S(15), S(12), ACT.Sin, th_sin)

                    def trig(p):
                        act.wait_ge(ang_ready, p + 1)
                        run(ang_s, ang_a, ACT.Abs, trig_done)
                        run(cos_sin[:, p % 2, 1], ang_a, ACT.Sin, trig_done, scale=TURN)
                        act.wait_ge(trig_done, 3 * p + 1)
                        run(cos_sin[:, p % 2, 0], ang_s, ACT.Sin, trig_done, scale=-TURN, bias=half_pi[:, 0:1])

                    next_cast("u_s5")
                    run(flat(u_s5[:, :, :]), pr("u_s5")[:, :], ACT.Copy, evac("u_s5"))
                    act.wait_ge(bT_done, 1)
                    run(bT[:, :, :, :].rearrange("p f q n -> p (f q n)"), MF[:, 1024:2048], ACT.Copy, bcT_ready)
                    act.wait_ge(cT_done, 1)
                    run(cT[:, :, :, :].rearrange("p f q n -> p (f q n)"), MF[:, 0:1024], ACT.Copy, bcT_ready)
                    trig(0)
                    next_cast("cmp")
                    cm = pr("cmp")[:, :].rearrange("p (a n) -> p a n", a=TT)
                    run(cmp_tm, cm[:, :, 0:256], ACT.Copy, cmp_read)
                    run(bgate[:, :, :], cm[:, :, 256:CMP_W], ACT.Tanh, cmp_read, scale=0.5)
                    trig(1)
                    next_cast("u_lru")
                    run(u_lru[:, :, 3:T + 3], pr("u_lru")[:, :].rearrange("p (t n) -> p t n", t=KB), ACT.Copy, evac("u_lru"))
                    act.wait_ge(cmpT_done, 1)
                    for h in range(NKV):
                        for s in range(2):
                            run(x2[64 * s:64 * s + 64, :, h, :],
                                pr("cmp")[64 * h:64 * h + 64, 0:512].rearrange("p (m t s) -> p m t s", m=2, s=2)[:, :, :, s],
                                ACT.Copy, evac("cmp") if h and s else None)
                    trig(2)
                    next_cast("ret_v")
                    run(flat(ret_v[:, :, :]), pr("ret_v")[:, :], ACT.Copy, evac("ret_v"))
                    next_cast("nsa_kv")
                    kv = pr("nsa_kv")[:, :].rearrange("p (a y o h d) -> p a y o h d", a=TT, y=2, o=2, h=NKV)
                    for t in range(TT):
                        for dup in range(2):
                            run(kd[:, t, :, :, dup, :], kv[:, t, :, 0], ACT.Copy)
                        run(nv[:, t].rearrange("p (y h) d -> p y h d", y=2), kv[:, t, :, 1], ACT.Copy,
                            evac("nsa_kv") if t else None)
                    trig(3)

                    def hidden(m, name):
                        next_cast(name)
                        run(hid_y[:, 64 * m:64 * m + 64].rearrange("p (k n) -> p k n", k=2),
                            pr(name)[:, :].rearrange("p (k n) -> p k n", k=2)[:, :, 0:32], ACT.Copy, evac(name))

                    hidden(0, "ck")

                    def gate_chunk(name):
                        i = BRANCHES.index(name)
                        next_cast("gate_" + name)
                        if i >= 2:
                            act.wait_ge(yg_lo, i - 1)
                        run(flat(gate[:, i % 2]), pr("gate_" + name)[:, :], ACT.Tanh, gate_tanh, scale=0.5)

                    def merge_chunk(name, half):
                        i = BRANCHES.index(name)
                        full = f"merge_{name}_{half}"
                        next_cast(full)
                        if i == 1:
                            act.wait_ge(evac(f"branch_s5_{half}"), ev(f"branch_s5_{half}"))
                        if i > 1:
                            act.wait_ge(mt_free, 2 * (i - 2) + half + 1)
                        run(flat(mt[:, half]), pr(full)[:, :], ACT.Tanh, evac(full), scale=0.5)

                    def hi_of_gated(name):
                        i = BRANCHES.index(name)
                        act.wait_ge(yg_ready, i + 1)
                        act.wait_ge(chunk_done, ch("glu_b" if i == 0 else f"branch_{BRANCHES[i - 1]}_1"))
                        run(flat(ys_hi[:, :, :]), flat(gate[:, i % 2]), ACT.Copy, yg_hi)

                    def attention_exp(i):
                        act.wait_ge(at_max, i + 1)
                        for b, g in enumerate((0, 2, 1, 3)):
                            run(prob[:, b * T:(b + 1) * T], prob[:, b * T:(b + 1) * T], ACT.Exp, at_exp,
                                bias=st[:, 40 + b:41 + b], accum_out=st[:, 52 + g:53 + g])
                            at = 1024 + b * P
                            run(prob[:, at:at + P], prob[:, at:at + P], ACT.Exp, at_exp,
                                bias=st[:, 44 + b:45 + b], accum_out=st[:, 48 + g:49 + g])

                    def attention_evac(i):
                        act.wait_ge(at_pT, i + 1)
                        if i:
                            act.wait_ge(at_o, i)
                        run(flat(probT), MF[:, 0:1536], ACT.Copy, at_pT_ready)

                    gate_chunk("s5")
                    trig(4)
                    hidden(1, "cv")
                    act.wait_ge(hid_arg, 1)
                    run(hid_q, hid_q, ACT.Tanh, hid_tanh, scale=GELU_C)
                    gate_chunk("lru")
                    trig(5)
                    merge_chunk("s5", 0)
                    trig(6)
                    merge_chunk("s5", 1)
                    trig(7)
                    cast_units(UNIT_END[CHUNK["ret_q"]] + N_SPLIT)
                    act.wait_ge(z_arg, 1)
                    run(gelu_t, gelu_t, ACT.Tanh, z_tanh, scale=GELU_C)
                    cast_units(UNIT_END[CHUNK["ret_k"]] + N_SPLIT - 2)
                    act.wait_ge(z_ready, 1)
                    run(flat(ys_hi[:, :, :]), flat(y_s5[:, :, :]), ACT.Copy, z_hi)
                    act.wait_ge(qkT_done, 1)
                    act.wait_ge(z_lo, 1)
                    run(flat(qT[:, :, :]), MF[:, 0:1024], ACT.Copy, qkT_ready)
                    next_cast("nsa_q")
                    run(nq, pr("nsa_q")[:, :], ACT.Copy, evac("nsa_q"), scale=HD ** -0.5)
                    cast_units(UNIT_END[CHUNK["nsa_q"]] + N_SPLIT)
                    act.wait_ge(lru_mm, 1)
                    for t in range(KB):
                        run(l_r[:, t, :], MF[:, t * T:(t + 1) * T], ACT.Tanh, lru_act, scale=0.5, bias=S(3)[:, t:t + 1])
                    for t in range(KB):
                        run(l_i[:, t, :], MF[:, 1024 + t * T:1024 + (t + 1) * T], ACT.Tanh, lru_act, scale=0.5,
                            bias=S(3)[:, 4 + t:5 + t])
                    nc.scalar.preload_act_table_set("exp_and_others")
                    act.wait_ge(lru_act, KB)
                    for t in range(KB):
                        run(l_a[:, t, :], l_r[:, t, :], ACT.Exp, lru_act, scale=S(4)[:, t:t + 1], bias=S(4)[:, t:t + 1])
                        run(l_m[:, t, :], l_r[:, t, :], ACT.Tanh, lru_act, scale=S(4)[:, 4 + t:5 + t], bias=S(4)[:, 4 + t:5 + t])
                    next_cast("glu_a")
                    act.wait_ge(qkT_done, 2)
                    run(flat(kT[:, :, :]), MF[:, 1024:2048], ACT.Copy, qkT_ready)
                    next_cast("glu_b")
                    act.wait_ge(lru_m2, 1)
                    for t in range(KB):
                        run(glu_t[:, t * T:(t + 1) * T], pr("glu_b")[:, t * T:(t + 1) * T], ACT.Tanh,
                            evac("glu_b") if t == KB - 1 else None, scale=0.5, bias=S(5)[:, t:t + 1])
                    act.wait_ge(nT_done, 1)
                    run(flat(nkT[:, :, :]), MF[:, 0:1024], ACT.Copy, nT_ready)
                    hi_of_gated("s5")
                    gate_chunk("ret")
                    act.wait_ge(nT_done, 2)
                    run(flat(nqT[:, :, :]), MF[:, 1024:2048], ACT.Copy, nT_ready)
                    run(flat(l_m), flat(l_m), ACT.Sqrt, lru_sqrt, scale=0.25)
                    nc.scalar.preload_act_table_set("exp_and_others")
                    cast_units(UNIT_END[CHUNK["merge_lru_0"]])
                    hi_of_gated("lru")
                    merge_chunk("lru", 0)
                    act.wait_ge(kcT_done, 1)
                    run(kcT[:, :], M[:, 1, 0:32], ACT.Copy, kcT_ready)
                    cast_units(UNIT_END[CHUNK["merge_lru_1"]])
                    act.wait_ge(rnT_done, 1)
                    run(flat(qT[:, :, :]), MF[:, 1024:2048], ACT.Copy, yr_ready)
                    act.wait_ge(cs_sub, 1)
                    run(cols(3072, 256), cols(3072, 256), ACT.Exp, cs_exp)
                    merge_chunk("lru", 1)
                    act.wait_ge(cpT_done, 1)
                    run(cmp_pT, M[:, 3, 0:256], ACT.Copy, cpT_ready)
                    cast_units(UNIT_END[CHUNK["merge_lru_1"]] + N_SPLIT)
                    attention_exp(0)
                    cast_units(UNIT_END[CHUNK["branch_lru_1"]] + N_SPLIT - 1)
                    attention_evac(0)
                    hi_of_gated("ret")
                    cast_units(UNIT_END[CHUNK["branch_lru_1"]] + N_SPLIT)
                    attention_exp(1)
                    merge_chunk("ret", 0)
                    attention_evac(1)
                    cast_units(UNIT_END[CHUNK["merge_ret_1"]] - 2 + N_SPLIT)
                    attention_exp(2)
                    merge_chunk("ret", 1)
                    next_cast("branch_ret_0")
                    attention_evac(2)
                    next_cast("branch_ret_1")
                    attention_exp(3)
                    gate_chunk("nsa")
                    attention_evac(3)
                    merge_chunk("nsa", 0)
                    act.wait_ge(noT_done, 1)
                    run(flat(nqT[:, :, :]), MF[:, 1024:2048], ACT.Copy, yn_ready)
                    hi_of_gated("nsa")
                    merge_chunk("nsa", 1)
                    cast_units(UNIT_END[CHUNK["branch_nsa_0"]] + N_SPLIT)
                    for b in range(4):
                        act.wait_ge(mT_done, b + 1)
                        if b == 2:
                            cast_units(UNIT_END[CHUNK["branch_nsa_1"]] + N_SPLIT)
                        run(flat(h_hi[:, 2 * b:2 * b + 2, :]), M[:, b, :], ACT.Copy, mhi_done)
                    cast_units(NU)
                    for half in range(2):
                        act.wait_ge(x_half, half + 1)
                        squares(nxt, half)

                @block.vector
                def _(dve):
                    v = nc.vector
                    links = [0]

                    def link(i):
                        links[0] += 1
                        i.then_inc(dve_order, 1)
                        dve.wait_ge(dve_order, links[0])

                    v.memset(u_lru[:, :, 0:3], 0.0)
                    for half in range(2):
                        for t in range(TT):
                            e = slice(512 * half, 512 * half + 512)
                            v.tensor_scalar(merged[:, t, e], x[:, t, e], st[:, 2 + t:3 + t], None, ALU.mult).then_inc(x_norm, 1)
                    lam, lam_i, lam_r = vec[:, V_LAM:V_LAM + 4], vec[:, V_LI:V_LI + 16], vec[:, V_LR:V_LR + 16]
                    v.scalar_tensor_tensor(S(0)[:, 0:4], lam, -1.0, lam, ALU.mult, ALU.max).then_inc(lam_abs, 1)
                    v.tensor_scalar(S(3)[:, 0:8], vec[:, V_BA:V_BA + 8], 0.5, None, ALU.mult)
                    v.tensor_scalar(S(5)[:, 0:4], vec[:, V_BGLU + 4:V_BGLU + 8], 0.5, None, ALU.mult)
                    v.tensor_scalar(S(11), lam_r, -1e-4, None, ALU.min)
                    dve.wait_ge(dt_exp, 1)
                    link(v.tensor_tensor(S(19), lam_i, S(8), ALU.mult))
                    v.tensor_tensor(S(9), S(11), S(8), ALU.mult).then_inc(mag_arg, 1)
                    link(v.tensor_scalar(S(18), S(19), 1.0 / TWO_PI, None, ALU.mult))
                    link(v.tensor_scalar(S(18), S(18), ROUND, ROUND, ALU.add, ALU.subtract))
                    for part in (PI2_A, PI2_B, PI2_C):
                        link(v.scalar_tensor_tensor(S(19), S(18), -part, S(19), ALU.mult, ALU.add))
                    v.tensor_scalar(S(12), S(19), 3.1415925, -3.1415925, ALU.min, ALU.max).then_inc(th_ready, 1)
                    for k in range(KD):
                        dve.wait_ge(hhi_done, k // 2 * 2 + 2)
                        v.scalar_tensor_tensor(h_lo[:, k, :], M[:, k // 2, (k % 2) * T:(k % 2 + 1) * T],
                                               vec[:, V_NORM + k:V_NORM + k + 1], h_hi[:, k, :].bitcast(f32),
                                               ALU.mult, ALU.subtract).then_inc(hlo_done, 1)
                    dve.wait_ge(th_ready, 1)
                    link(v.tensor_scalar(S(19), S(12), 1.0 / TWO_PI, None, ALU.mult))
                    link(v.tensor_scalar(S(16), S(19), 4096.0, ROUND, ALU.mult, ALU.add))
                    link(v.tensor_scalar(S(16), S(16), ROUND, 1.0 / 4096.0, ALU.subtract, ALU.mult))
                    link(v.tensor_tensor(S(17), S(19), S(16), ALU.subtract))

                    def angles(p):
                        if p:
                            dve.wait_ge(trig_done, 3 * p)
                        for j in range(2):
                            i = v.tensor_scalar(ang_a[:, j, :], cst("time"), S(16)[:, 2 * p + j:2 * p + j + 1], None, ALU.mult)
                        link(i)
                        for j in range(2):
                            i = v.scalar_tensor_tensor(ang_s[:, j, :], cst("time"), S(17)[:, 2 * p + j:2 * p + j + 1],
                                                       ang_a[:, j, :], ALU.mult, ALU.add)
                        link(i)
                        link(v.tensor_scalar(ang_s, ang_s, ROUND, ROUND, ALU.add, ALU.subtract))
                        link(v.tensor_tensor(ang_a, ang_a, ang_s, ALU.subtract))
                        for j in range(2):
                            i = v.scalar_tensor_tensor(ang_a[:, j, :], cst("time"), S(17)[:, 2 * p + j:2 * p + j + 1],
                                                       ang_a[:, j, :], ALU.mult, ALU.add)
                        link(i)
                        v.tensor_scalar(ang_a, ang_a, 0.5, -0.5, ALU.min, ALU.max).then_inc(ang_ready, 1)

                    dve.wait_ge(th_sin, 3)
                    dve.wait_ge(mag_exp, 1)
                    v.memset(cols(3072, 1024), 0.0)
                    link(v.tensor_tensor(S(21), S(15), S(10), ALU.mult))
                    link(v.tensor_tensor(S(20), S(14), S(10), ALU.mult))
                    link(v.tensor_scalar(S(20), S(20), 1.0, None, ALU.subtract))
                    v.tensor_tensor(S(22), S(11), S(11), ALU.mult)
                    link(v.tensor_tensor(S(26), lam_i, lam_i, ALU.mult))
                    link(v.tensor_tensor(S(22), S(22), S(26), ALU.add))
                    link(v.reciprocal(S(23), S(22)))
                    v.tensor_tensor(S(24), S(20), S(11), ALU.mult)
                    v.tensor_tensor(S(25), S(21), S(11), ALU.mult)
                    v.tensor_tensor(S(26), S(21), lam_i, ALU.mult)
                    link(v.tensor_tensor(S(27), S(20), lam_i, ALU.mult))
                    v.tensor_tensor(S(24), S(24), S(26), ALU.add)
                    link(v.tensor_tensor(S(25), S(25), S(27), ALU.subtract))
                    v.tensor_tensor(S(24), S(24), S(23), ALU.mult)
                    link(v.tensor_tensor(S(25), S(25), S(23), ALU.mult))
                    f_re = bc(S(24).unsqueeze(2), [P, NS5, 16])
                    f_im = bc(S(25).unsqueeze(2), [P, NS5, 16])
                    for f, (b0, b1, op) in enumerate(((0, 1, ALU.subtract), (1, 0, ALU.add))):
                        v.tensor_tensor(b_tmp[:, 0], b_nat[:, b0], f_re, ALU.mult)
                        link(v.tensor_tensor(b_tmp[:, 1], b_nat[:, b1], f_im, ALU.mult))
                        for g in range(2):
                            h = slice(64 * g, 64 * g + 64)
                            i = v.tensor_tensor(b_exp[h, f, :, g, :], b_tmp[h, 0], b_tmp[h, 1], op)
                        i.then_inc(b_ready, 1)
                        dve.wait_ge(b_ready, f + 1)
                    for f in range(2):
                        v.tensor_tensor(c_nat[:, f], c_nat[:, f], bc(cst("group").unsqueeze(1).unsqueeze(3), [P, KB, 2, 64]),
                                        ALU.mult).then_inc(c_ready, 1)
                    angles(0)
                    e, s_, s2, q_, m_ = S(1)[:, 0:4], S(6)[:, 0:4], S(6)[:, 4:8], S(7)[:, 0:4], S(7)[:, 4:8]
                    dve.wait_ge(lam_exp, 1)
                    v.tensor_scalar(m_, lam, -1.0, 0.0, ALU.mult, ALU.max)
                    link(v.tensor_scalar(s_, e, 2.0, None, ALU.add))
                    link(v.reciprocal(s_, s_))
                    link(v.tensor_tensor(s_, s_, e, ALU.mult))
                    link(v.tensor_tensor(s2, s_, s_, ALU.mult))
                    link(v.tensor_scalar(q_, s2, 1.0 / 15.0, None, ALU.mult))
                    for n in (13, 11, 9, 7, 5, 3):
                        link(v.scalar_tensor_tensor(q_, q_, 1.0 / n, s2, ALU.add, ALU.mult))
                    link(v.scalar_tensor_tensor(q_, q_, 1.0, s_, ALU.add, ALU.mult))
                    link(v.scalar_tensor_tensor(q_, q_, 2.0, m_, ALU.mult, ALU.add))
                    v.tensor_scalar(S(4)[:, 0:4], q_, -0.5 * 8.0, None, ALU.mult)
                    link(v.tensor_scalar(S(4)[:, 4:8], q_, 0.5 * 8.0, None, ALU.mult))

                    def scan_pair(p):
                        b = p % 2
                        cos, sin = cos_sin[:, b, 0], cos_sin[:, b, 1]
                        t0, t1, t2, t3 = (s5_t[:, f] for f in range(4))
                        re, im = M[:, 0:2, 0:T], M[:, 0:2, T:2 * T]
                        if p:
                            dve.wait_ge(h_done, p)
                        dve.wait_ge(trig_done, 3 * p + 3)
                        dve.wait_ge(bu_done, p + 1)
                        v.tensor_tensor(t0, re, cos, ALU.mult)
                        v.tensor_tensor(t1, im, sin, ALU.mult)
                        v.tensor_tensor(t2, im, cos, ALU.mult)
                        v.tensor_tensor(t3, re, sin, ALU.mult).then_inc(bu_used, 1)
                        dve.wait_ge(bu_used, p + 1)
                        v.tensor_tensor(t0, t0, t1, ALU.add)
                        link(v.tensor_tensor(t2, t2, t3, ALU.subtract))
                        for j in range(2):
                            mag = bc(S(10)[:, 2 * p + j:2 * p + j + 1], [P, T])
                            v.tensor_tensor_scan(t1[:, j, :], mag, t0[:, j, :], 0.0, ALU.mult, ALU.add)
                            i = v.tensor_tensor_scan(t3[:, j, :], mag, t2[:, j, :], 0.0, ALU.mult, ALU.add)
                        link(i)
                        if p >= 2:
                            dve.wait_ge(y_done, p - 1)
                        h_re, h_im = s5_h[:, b, 0], s5_h[:, b, 1]
                        v.tensor_tensor(h_re, t1, cos, ALU.mult)
                        v.tensor_tensor(t0, t3, sin, ALU.mult)
                        v.tensor_tensor(h_im, t3, cos, ALU.mult)
                        link(v.tensor_tensor(t2, t1, sin, ALU.mult))
                        v.tensor_tensor(h_re, h_re, t0, ALU.subtract)
                        v.scalar_tensor_tensor(h_im, h_im, -1.0, t2, ALU.mult, ALU.subtract).then_inc(h_done, 1)

                    def s5_out(q):
                        dve.wait_ge(y_done, 2 * q + 2)
                        v.scalar_tensor_tensor(y_s5[:, q, :], u_s5[:, q, :], vec[:, V_D + q:V_D + q + 1],
                                               M[:, 2 + q % 2, 0:T], ALU.mult, ALU.add).then_inc(y_used, 1)

                    def gate_times(name):
                        i = BRANCHES.index(name)
                        g = flat(gate[:, i % 2])
                        dve.wait_ge(gate_tanh, i + 1)
                        v.scalar_tensor_tensor(g, g, 1.0, pr("gate_" + name)[:, :], ALU.add, ALU.mult).then_inc(evac("gate_" + name), 1)

                    def gated(name, y):
                        i = BRANCHES.index(name)
                        g = flat(gate[:, i % 2])
                        dve.wait_ge(evac("gate_" + name), ev("gate_" + name))
                        v.tensor_tensor(g, g, y, ALU.mult).then_inc(yg_ready, 1)

                    def lo_of_gated(name):
                        i = BRANCHES.index(name)
                        dve.wait_ge(yg_hi, i + 1)
                        v.tensor_tensor(flat(ys_lo[:, :, :]), flat(gate[:, i % 2]), flat(ys_hi[:, :, :]).bitcast(f32),
                                        ALU.subtract).then_inc(yg_lo, 1)

                    def branch(name, half):
                        i = BRANCHES.index(name)
                        full = f"branch_{name}_{half}"
                        dst = merged[:, :, 512 * half:512 * half + 512]
                        dve.wait_ge(chunk_done, ch(full))
                        src = pr(full)[:, :].rearrange("p (a n) -> p a n", a=TT)
                        if i == 0:
                            v.scalar_tensor_tensor(dst, mt[:, half], 1.0, src, ALU.add, ALU.mult).then_inc(evac(full), 1)
                        else:
                            v.scalar_tensor_tensor(mt[:, half], mt[:, half], 1.0, src, ALU.add, ALU.mult).then_inc(evac(full), 1)
                            dve.wait_ge(evac(full), ev(full))
                            v.tensor_tensor(dst, dst, mt[:, half], ALU.add).then_inc(mt_free, 1)

                    angles(1)
                    scan_pair(0)
                    dve.wait_ge(evac("cmp"), ev("cmp"))
                    v.memset(blocks[:, :, :, NCMP:16], 0.0)
                    for m in range(2):
                        for r8 in range(2):
                            src = x2[:, m].rearrange("p h (n r) -> p r h n", r=8)[:, :, :, r8:r8 + NCMP]
                            at = 16 * m + 8 * r8
                            i = v.tensor_tensor(blocks[:, at:at + 8, :, 0:NCMP], src,
                                                bc(pos[:, m, 8 * r8:8 * r8 + 8].unsqueeze(2).unsqueeze(3), [P, 8, 2, NCMP]), ALU.add)
                    i.then_inc(blk_ready, 1)
                    v.tensor_scalar(bgate[:, :, :], bgate[:, :, :], 1.0, 0.5, ALU.add, ALU.mult)
                    angles(2)
                    scan_pair(1)
                    angles(3)
                    scan_pair(2)
                    s5_out(0)
                    angles(4)
                    scan_pair(3)
                    gate_times("s5")
                    angles(5)
                    scan_pair(4)
                    s5_out(1)
                    dve.wait_ge(evac("ck"), ev("ck"))
                    dve.wait_ge(evac("cv"), ev("cv"))
                    link(v.tensor_tensor(hid_q, hid_y, hid_y, ALU.mult))
                    link(v.tensor_scalar(hid_q, hid_q, 0.044715, 1.0, ALU.mult, ALU.add))
                    v.tensor_tensor(hid_q, hid_q, hid_y, ALU.mult).then_inc(hid_arg, 1)
                    gate_times("lru")
                    angles(6)
                    scan_pair(5)
                    dve.wait_ge(hid_tanh, 1)
                    link(v.tensor_scalar(hid_q, hid_q, 0.5, 0.5, ALU.mult, ALU.add))
                    link(v.tensor_tensor(hid[:, :, :, :].rearrange("p m k n -> p (m k n)"), hid_q, hid_y, ALU.mult))
                    for k in range(2):
                        i = v.tensor_copy(hid8[:, k].rearrange("p (h g) n -> p h g n", h=NKV),
                                          bc(hid[:, 1, k].rearrange("p (h n) -> p h n", h=NKV).unsqueeze(2), [P, NKV, 4, 16]))
                    i.then_inc(hid_ready, 1)
                    angles(7)
                    scan_pair(6)
                    s5_out(2)
                    scan_pair(7)
                    s5_out(3)
                    def rope_ret(n, name):
                        ro4 = merged[:, n].rearrange("p (a h c) -> p a h c", a=TT, h=NH_RET)
                        src = pr(name)[:, :].rearrange("p (a h c) -> p a h c", a=TT, h=NH_RET)
                        shape = [P, TT, NH_RET, 64]
                        cos = bc(cst("ret_cos").rearrange("p (a c) -> p a c", a=TT).unsqueeze(2), shape)
                        sin = bc(cst("ret_sin").rearrange("p (a c) -> p a c", a=TT).unsqueeze(2), shape)
                        lo, hi = slice(0, 64), slice(64, 128)
                        dve.wait_ge(chunk_done, ch(name))
                        if n:
                            dve.wait_ge(rope_ready, n)
                        v.tensor_tensor(ro4[:, :, :, lo], src[:, :, :, lo], cos, ALU.mult)
                        v.tensor_tensor(rope_t[:, 0], src[:, :, :, hi], sin, ALU.mult)
                        v.tensor_tensor(ro4[:, :, :, hi], src[:, :, :, hi], cos, ALU.mult)
                        v.tensor_tensor(rope_t[:, 1], src[:, :, :, lo], sin, ALU.mult).then_inc(evac(name), 1)
                        dve.wait_ge(evac(name), ev(name))
                        v.tensor_tensor(ro4[:, :, :, lo], ro4[:, :, :, lo], rope_t[:, 0], ALU.subtract)
                        v.tensor_tensor(ro4[:, :, :, hi], ro4[:, :, :, hi], rope_t[:, 1], ALU.add).then_inc(rope_ready, 1)

                    dve.wait_ge(y_used, KB)
                    yf = flat(y_s5[:, :, :])
                    link(v.tensor_tensor(gelu_t, yf, yf, ALU.mult))
                    link(v.tensor_scalar(gelu_t, gelu_t, 0.044715, 1.0, ALU.mult, ALU.add))
                    v.tensor_tensor(gelu_t, gelu_t, yf, ALU.mult).then_inc(z_arg, 1)
                    rope_ret(0, "ret_q")
                    dve.wait_ge(z_tanh, 1)
                    link(v.tensor_scalar(gelu_t, gelu_t, 0.5, 0.5, ALU.mult, ALU.add))
                    v.tensor_tensor(yf, yf, gelu_t, ALU.mult).then_inc(z_ready, 1)
                    dve.wait_ge(z_hi, 1)
                    v.tensor_tensor(flat(ys_lo[:, :, :]), yf, flat(ys_hi[:, :, :]).bitcast(f32), ALU.subtract).then_inc(z_lo, 1)

                    dve.wait_ge(evac("u_lru"), ev("u_lru"))

                    def tap(k, t):
                        return vec[:, V_CONV + KB * k + t:V_CONV + KB * k + t + 1]

                    for t in range(KB):
                        i = v.tensor_scalar(xc[:, t, :], u_lru[:, t, 0:T], tap(0, t), vec[:, V_CONVB + t:V_CONVB + t + 1],
                                            ALU.mult, ALU.add)
                    link(i)
                    for k in range(1, 4):
                        for t in range(KB):
                            i = v.scalar_tensor_tensor(xc[:, t, :], u_lru[:, t, k:k + T], tap(k, t), xc[:, t, :], ALU.mult, ALU.add)
                        if k < 3:
                            link(i)
                    i.then_inc(xc_ready, 1)
                    rope_ret(1, "ret_k")

                    def rope_nsa(x4):
                        shape = [P, TT, NHQ, 8]
                        cos = bc(cst("nsa_cos").rearrange("p (a c) -> p a c", a=TT).unsqueeze(2), shape)
                        sin = bc(cst("nsa_sin").rearrange("p (a c) -> p a c", a=TT).unsqueeze(2), shape)
                        x1, x2_ = x4[:, :, :, 0:8], x4[:, :, :, 8:16]
                        v.tensor_tensor(rope_n[:, 0], x1, cos, ALU.mult)
                        v.tensor_tensor(rope_n[:, 1], x2_, sin, ALU.mult)
                        v.tensor_tensor(rope_n[:, 2], x2_, cos, ALU.mult)
                        link(v.tensor_tensor(rope_n[:, 3], x1, sin, ALU.mult))
                        v.tensor_tensor(x1, rope_n[:, 0], rope_n[:, 1], ALU.subtract)
                        v.tensor_tensor(x2_, rope_n[:, 2], rope_n[:, 3], ALU.add).then_inc(nrope_ready, 1)

                    rope_nsa_kd = kd[:, :, :, :, :, :].rearrange("p a y h u d -> p a (y h u) d")
                    dve.wait_ge(evac("nsa_kv"), ev("nsa_kv"))
                    dve.wait_ge(rope_ready, 2)
                    rope_nsa(rope_nsa_kd)
                    dve.wait_ge(nrope_ready, 1)
                    dve.wait_ge(chunk_done, ch("glu_a"))
                    for t in range(KB):
                        i = v.tensor_scalar(glu_v[:, t * T:(t + 1) * T], pr("glu_a")[:, t * T:(t + 1) * T],
                                            vec[:, V_BGLU + t:V_BGLU + t + 1], 0.5, ALU.add, ALU.mult)
                    i.then_inc(evac("glu_a"), 1)
                    dve.wait_ge(lru_act, 4 * KB)
                    link(v.tensor_tensor(l_r, l_a, l_a, ALU.mult))
                    v.scalar_tensor_tensor(flat(l_i), flat(l_i), 1.0, flat(xc), ALU.add, ALU.mult)
                    v.scalar_tensor_tensor(flat(l_m), flat(l_r), 1.0, flat(l_m), ALU.add, ALU.mult).then_inc(lru_m2, 1)

                    dve.wait_ge(evac("glu_a"), ev("glu_a"))
                    dve.wait_ge(evac("glu_b"), ev("glu_b"))
                    link(v.scalar_tensor_tensor(glu_v, glu_t, 1.0, glu_v, ALU.add, ALU.mult))
                    gated("s5", glu_v)
                    lo_of_gated("s5")

                    def decay_scores(h):
                        dve.wait_ge(rs_done, h + 1)
                        if h >= 2:
                            dve.wait_ge(ro_done, h - 1)
                        dec = cst("decay").rearrange("p (h t) -> p h t", h=NH_RET)[:, h, :]
                        v.tensor_tensor(ret_s[:, h % 2, 0:T], M[:, h % 2, 0:T], dec, ALU.mult)
                        v.tensor_tensor(ret_s[:, h % 2, T:T + P], M[:, h % 2, T:T + P], dec[:, 0:P], ALU.mult).then_inc(rs_ready, 1)

                    dve.wait_ge(evac("nsa_q"), ev("nsa_q"))
                    dve.wait_ge(yg_ready, 1)
                    rope_nsa(nq4)
                    gate_times("ret")
                    decay_scores(0)
                    decay_scores(1)
                    branch("s5", 0)
                    dve.wait_ge(lru_sqrt, 1)
                    link(v.tensor_tensor(l_i, l_i, l_m, ALU.mult))
                    for t in range(KB):
                        i = v.tensor_tensor_scan(l_h[:, t, :], l_a[:, t, :], l_i[:, t, :], 0.0, ALU.mult, ALU.add)
                    link(i)
                    gated("lru", flat(l_h))
                    branch("s5", 1)
                    decay_scores(2)
                    decay_scores(3)
                    lo_of_gated("lru")
                    dve.wait_ge(ro_done, NH_RET)
                    o_ret = MF[:, 1024:2048].rearrange("p (i c) -> p i c", c=P)
                    for n in range(TT * NH_RET):
                        i = v.bn_stats(bn[:, n, :], o_ret[:, n, :])
                    link(i)
                    for n in range(TT * NH_RET):
                        i = v.bn_aggr(mv[:, n, :], bn[:, n, :])
                    link(i)
                    v.tensor_scalar(st[:, 80:88], mv[:, :, 1], EPS_RET, None, ALU.add).then_inc(rvar, 1)
                    dve.wait_ge(cw_done, 1)
                    kps = M[0:32, 0, 0:HD]
                    cc, ss = cst("cmp_cos")[0:32], cst("cmp_sin")[0:32]
                    v.tensor_copy(kc[:, :, :], bc(kps.unsqueeze(1), [32, 2, HD]))
                    v.tensor_tensor(kc_t[:, 0], kps[:, 0:8], cc, ALU.mult)
                    v.tensor_tensor(kc_t[:, 1], kps[:, 8:16], ss, ALU.mult)
                    v.tensor_tensor(kc_t[:, 2], kps[:, 8:16], cc, ALU.mult)
                    link(v.tensor_tensor(kc_t[:, 3], kps[:, 0:8], ss, ALU.mult))
                    v.tensor_tensor(kc[:, :, 0:8], bc(kc_t[:, 0].unsqueeze(1), [32, 2, 8]), bc(kc_t[:, 1].unsqueeze(1), [32, 2, 8]), ALU.subtract)
                    v.tensor_tensor(kc[:, :, 8:16], bc(kc_t[:, 2].unsqueeze(1), [32, 2, 8]), bc(kc_t[:, 3].unsqueeze(1), [32, 2, 8]), ALU.add).then_inc(kc_ready, 1)
                    v.tensor_tensor(vbd[:, :, :], bc(M[:, 0, HD:2 * HD].unsqueeze(1), [P, NHQ, HD]),
                                    bc(cst("head").unsqueeze(2), [P, NHQ, HD]), ALU.mult).then_inc(vbd_ready, 1)
                    dve.wait_ge(rrstd, 1)
                    for n in range(TT * NH_RET):
                        i = v.tensor_scalar(ro[:, n * P:(n + 1) * P], o_ret[:, n, :], mv[:, n, 0:1], st[:, 88 + n:89 + n],
                                            ALU.subtract, ALU.mult)
                    i.then_inc(rn_ready, 1)
                    dve.wait_ge(cs_done, 1)
                    shape = [P, TT, 4, 16]
                    add = bc(cst("cmp_add").rearrange("p (a n) -> p a n", a=TT).unsqueeze(2), shape)
                    keep = bc(cst("cmp_keep").rearrange("p (a n) -> p a n", a=TT).unsqueeze(2), shape)
                    for e_ in range(2):
                        i = v.tensor_tensor(cmp_s[:, e_], M[:, e_, 0:P].rearrange("p (a h n) -> p a h n", a=TT, h=4), add, ALU.add)
                    link(i)
                    cs2 = cols(3072, 256).rearrange("p (i n) -> p i n", n=16)
                    link(v.tensor_reduce(st[:, 8:24], cs2, AX, ALU.max))
                    v.tensor_tensor(cs2, cs2, bc(st[:, 8:24].unsqueeze(2), [P, 16, 16]), ALU.subtract).then_inc(cs_sub, 1)
                    dve.wait_ge(cs_exp, 1)
                    for e_ in range(2):
                        i = v.tensor_tensor(cmp_s[:, e_], cmp_s[:, e_], keep, ALU.mult)
                    link(i)
                    link(v.tensor_reduce(st[:, 24:40], cs2, AX, ALU.add))
                    link(v.tensor_scalar(st[:, 24:40], st[:, 24:40], 1e-30, None, ALU.max))
                    link(v.reciprocal(st[:, 24:40], st[:, 24:40]))
                    coef = st[:, 24:40].rearrange("p (e a h) -> p e a h", e=2, a=TT)
                    gates0 = bgate[:, :, 0:8].rearrange("p a (h e) -> p e a h", e=2)
                    link(v.tensor_tensor(coef, coef, gates0, ALU.mult))
                    cp = cmp_p.rearrange("p (a h e n) -> p e a h n", a=TT, h=4, e=2)
                    for e_ in range(2):
                        i = v.tensor_tensor(cp[:, e_], cmp_s[:, e_], bc(coef[:, e_].unsqueeze(3), shape), ALU.mult)
                    i.then_inc(cp_ready, 1)

                    def attention_max(i):
                        dve.wait_ge(at_s, i + 1)
                        if i:
                            dve.wait_ge(at_pT, i)
                        causal = cst("causal")
                        v.tensor_tensor(prob[:, 0:1024].rearrange("p (b n) -> p b n", b=4),
                                        MF[:, 0:1024].rearrange("p (b n) -> p b n", b=4),
                                        bc(causal.unsqueeze(1), [P, 4, T]), ALU.add)
                        link(v.tensor_tensor(prob[:, 1024:1536].rearrange("p (b n) -> p b n", b=4),
                                             M[:, 2, :].rearrange("p (b n) -> p b n", b=4),
                                             bc(causal[:, P:T].unsqueeze(1), [P, 4, P]), ALU.add))
                        v.tensor_reduce(st[:, 40:44], prob[:, 0:1024].rearrange("p (b n) -> p b n", b=4), AX, ALU.max, negate=True)
                        v.tensor_reduce(st[:, 44:48], prob[:, 1024:1536].rearrange("p (b n) -> p b n", b=4), AX, ALU.max,
                                        negate=True).then_inc(at_max, 1)

                    def attention_out(i):
                        y, h = i // NKV, i % NKV
                        dve.wait_ge(at_exp, 8 * (i + 1))
                        link(v.reciprocal(st[:, 56:64], st[:, 48:56]))
                        cf = st[:, 64:72].rearrange("p (a g) -> p a g", a=TT)
                        link(v.tensor_tensor(cf, st[:, 56:64].rearrange("p (a g) -> p a g", a=TT),
                                             bgate[:, :, 8 * (y + 1) + 4 * h:8 * (y + 1) + 4 * h + 4], ALU.mult))
                        dve.wait_ge(at_o, i + 1)
                        src = M[:, 3, :].rearrange("p (a g d) -> p a g d", a=TT, g=4)
                        cfb = bc(cf.unsqueeze(3), [P, TT, 4, HD])
                        dst = no4[:, :, 4 * h:4 * h + 4, :]
                        if y == 0:
                            v.tensor_tensor(dst, src, cfb, ALU.mult).then_inc(at_no, 1)
                            dve.wait_ge(at_no, i + 1)
                        else:
                            tmp = att_t.rearrange("p (a g d) -> p a g d", a=TT, g=4)
                            link(v.tensor_tensor(tmp, src, cfb, ALU.mult))
                            v.tensor_tensor(dst, dst, tmp, ALU.add).then_inc(at_no, 1)

                    attention_max(0)
                    branch("lru", 0)
                    branch("lru", 1)
                    dve.wait_ge(yr_ready, 1)
                    gated("ret", flat(qT[:, :, :]))
                    lo_of_gated("ret")
                    attention_out(0)
                    attention_max(1)
                    attention_out(1)
                    attention_max(2)
                    branch("ret", 0)
                    branch("ret", 1)
                    attention_out(2)
                    attention_max(3)
                    gate_times("nsa")
                    attention_out(3)
                    dve.wait_ge(co_done, 1)
                    dve.wait_ge(at_no, 4)
                    v.tensor_tensor(nq, nq, MF[:, 0:1024], ALU.add).then_inc(no_cmp, 1)
                    dve.wait_ge(yn_ready, 1)
                    gated("nsa", flat(nqT[:, :, :]))
                    lo_of_gated("nsa")
                    branch("nsa", 0)
                    dve.wait_ge(nxt["vectors_loaded"], VECTORS_ALL)
                    expand_dt(nxt)
                    for b in range(4):
                        dve.wait_ge(mhi_done, b + 1)
                        v.tensor_tensor(flat(h_lo[:, 2 * b:2 * b + 2, :]), M[:, b, :],
                                        flat(h_hi[:, 2 * b:2 * b + 2, :]).bitcast(f32), ALU.subtract).then_inc(mlo_done, 1)
                        if b == 1:
                            branch("nsa", 1)
                    dve.wait_ge(nxt["vecT"], 2)
                    keep_vectors(nxt)
                    for half in range(2):
                        full = f"out_{half}b"
                        dst = x[:, :, 512 * half:512 * half + 512]
                        dve.wait_ge(chunk_done, ch(full))
                        v.scalar_tensor_tensor(dst, pr(full)[:, :].rearrange("p (a n) -> p a n", a=TT), 0.25, dst,
                                               ALU.mult, ALU.add).then_inc(x_half, 1)
                    mean_square(dve, nxt)

                @block.tensor
                def _(pe):
                    mm = nc.tensor.matmul

                    def tr(dst, src, rows_=P):
                        return nc.tensor.transpose(dst, src, ident[0:rows_, 0:rows_])

                    def split_product(dst, left, right, start, stop):
                        for n, (i, j) in enumerate(((0, 0), (0, 1), (1, 0))):
                            last = mm(dst, left[i], right[j], start=start and n == 0, stop=stop and n == 2, skip_group_check=True)
                        return last

                    def chunk(name, part=2):
                        c = CHUNK[name]
                        _, kt, w = CHUNKS[c]
                        u0 = UNIT_END[c - 1] if c else 0
                        n_units = UNIT_END[c] - u0
                        kind = name.split("_")[0]
                        todo = {0: range(n_units // 2), 1: range(n_units // 2, n_units), 2: range(n_units)}[part]
                        ps = pr(name)
                        if c >= 2 and part != 1 and name not in ("out_0b", "out_1b"):
                            pe.wait_ge(evacuated[c % 2], c // 2)
                        for n in todo:
                            u = u0 + n
                            _, k0, nk, _ = UNITS[u]
                            pe.wait_ge(lo_done, u + 1)
                            s = u % N_SPLIT
                            for kk in range(nk):
                                k = k0 + kk
                                st_, sp_ = k == 0, k == (KD if kind == "out" else kt) - 1
                                if name == "u_s5":
                                    pe.wait_ge(hlo_done, k + 1)

                                def wt(lo, hi):
                                    return tuple(t[:, s, kk * w + lo:kk * w + hi] for t in (w_hi, w_lo))

                                def ht(lo, hi, pair=(h_hi, h_lo)):
                                    return tuple(t[:, k, lo:hi] for t in pair)

                                if kind == "u" or kind == "gate":
                                    for m in range(4):
                                        last = split_product(ps[:, m * T:(m + 1) * T], wt(m * P, (m + 1) * P), ht(0, T), st_ and m % 2 == 0, sp_)
                                elif kind == "glu":
                                    for m in range(4):
                                        last = split_product(ps[:, m * T:(m + 1) * T], wt(m * P, (m + 1) * P), ht(0, T, (ys_hi, ys_lo)), st_ and m % 2 == 0, sp_)
                                else:
                                    pair = (ys_hi, ys_lo) if kind == "branch" else (h_hi, h_lo)
                                    for t in range(TT):
                                        last = split_product(ps[:, 512 * t:512 * t + w], ht(t * P, (t + 1) * P, pair), wt(0, w), st_, sp_)
                            if n == n_units - 1:
                                last.then_inc(chunk_done, 1)
                            else:
                                last.then_inc(unit_used, 1)

                    def compress(m, name):
                        c = CHUNK[name]
                        pe.wait_ge(evacuated[c % 2], c // 2)
                        if m == 0:
                            pe.wait_ge(blk_ready, 1)
                        pe.wait_ge(cw1_loaded, 64 * (m + 1))
                        for k in range(16):
                            for half in range(2):
                                at = (k % 4) * 256 + half * P
                                last = mm(pr(name)[:, 512 * half:512 * half + 32], cw1(k // 4)[:, at:at + P],
                                          flat(nqT[:, :, :])[:, (16 * m + k) * 32:(16 * m + k + 1) * 32],
                                          start=k == 0, stop=k == 15, skip_group_check=True)
                        last.then_inc(chunk_done, 1)

                    def features_T(halves, src, signal):
                        for k in halves:
                            for t in range(TT):
                                last = tr(M[:, k // 2, (k % 2) * T + t * P:(k % 2) * T + (t + 1) * P], src[:, t, k * P:(k + 1) * P])
                            if k % 2:
                                last.then_inc(signal, 1)

                    for half in range(2):
                        pe.wait_ge(x_norm, TT * (half + 1))
                        features_T(range(4 * half, 4 * half + 4), merged, xT_done)
                    chunk("u_s5")
                    pe.wait_ge(hlo_done, KD)
                    pe.wait_ge(b_ready, 2)
                    for f in range(2):
                        for q in range(KB):
                            last = tr(M[:, 2 + f, q * P:(q + 1) * P],
                                      b_exp[:, f, 4 * q:4 * q + 4].rearrange("p s g c -> p (s g c)"))
                    last.then_inc(bT_done, 1)
                    pe.wait_ge(c_ready, 2)
                    for f in range(2):
                        for q in range(KB):
                            last = tr(M[:, f, q * P:(q + 1) * P], c_nat[:, f, q].rearrange("p g n -> p (g n)"))
                    last.then_inc(cT_done, 1)

                    def state_inputs(p):
                        if p == 0:
                            pe.wait_ge(bcT_ready, 2)
                            pe.wait_ge(evac("u_s5"), ev("u_s5"))
                        else:
                            pe.wait_ge(bu_used, p)
                        q = p // 2
                        for j in range(2):
                            r = slice(32 * (2 * (p % 2) + j), 32 * (2 * (p % 2) + j) + 32)
                            for f in range(2):
                                last = mm(M[:, j, f * T:(f + 1) * T], bT[r, f, q, :], u_s5[r, q, :], start=True, stop=True)
                        last.then_inc(bu_done, 1)

                    def state_outputs(p):
                        q = p // 2
                        pe.wait_ge(h_done, p + 1)
                        if q >= 2 and p % 2 == 0:
                            pe.wait_ge(y_used, q - 1)
                        for j in range(2):
                            r = slice(32 * (2 * (p % 2) + j), 32 * (2 * (p % 2) + j) + 32)
                            dst = M[r, 2 + q % 2, 0:T]
                            for f in range(2):
                                last = mm(dst, cT[:, f, q, r], s5_h[:, p % 2, f, j, :], start=f == 0, stop=f == 1)
                        last.then_inc(y_done, 1)

                    chunk("cmp")
                    state_inputs(0)
                    chunk("u_lru")
                    pe.wait_ge(cmp_read, 2)
                    for m in range(2):
                        for t in range(TT):
                            at = (2 * m + t) * P
                            last = tr(pr("cmp")[:, at:at + P], cmp_tm[:, t, m * P:(m + 1) * P])
                    last.then_inc(cmpT_done, 1)
                    state_inputs(1)
                    state_outputs(0)
                    chunk("ret_v")
                    state_inputs(2)
                    state_outputs(1)
                    chunk("nsa_kv")
                    state_inputs(3)
                    state_outputs(2)
                    compress(0, "ck")
                    chunk("gate_s5")
                    state_inputs(4)
                    state_outputs(3)
                    compress(1, "cv")
                    chunk("gate_lru")
                    state_inputs(5)
                    state_outputs(4)
                    chunk("merge_s5_0")
                    state_inputs(6)
                    state_outputs(5)
                    chunk("merge_s5_1")
                    state_inputs(7)
                    state_outputs(6)
                    chunk("ret_q")
                    state_outputs(7)
                    def blocks_T(at, src):
                        for n in range(4):
                            for t in range(TT):
                                last = tr(MF[:, at + n * T + t * P:at + n * T + (t + 1) * P], src[:, (4 * t + n) * P:(4 * t + n + 1) * P])
                        return last

                    chunk("ret_k")
                    pe.wait_ge(y_used, KB)
                    pe.wait_ge(rope_ready, 1)
                    blocks_T(0, merged[:, 0]).then_inc(qkT_done, 1)
                    chunk("nsa_q")
                    pe.wait_ge(xc_ready, 1)
                    pe.wait_ge(qkT_ready, 1)
                    for f, w in enumerate((wa, wx)):
                        for t in range(KB):
                            last = mm(MF[:, f * 1024 + t * T:f * 1024 + (t + 1) * T], w[:, t, :], xc[:, t, :], start=True, stop=True)
                    last.then_inc(lru_mm, 1)
                    pe.wait_ge(z_lo, 1)
                    chunk("glu_a")
                    pe.wait_ge(rope_ready, 2)
                    pe.wait_ge(lru_act, 2 * KB)
                    blocks_T(1024, merged[:, 1]).then_inc(qkT_done, 1)
                    chunk("glu_b")
                    pe.wait_ge(nrope_ready, 1)
                    pe.wait_ge(qkT_ready, 1)
                    blocks_T(0, kd[:, :, :, :, :, :].rearrange("p a y h u d -> p (a y h u d)")).then_inc(nT_done, 1)
                    chunk("gate_ret")
                    pe.wait_ge(qkT_ready, 2)
                    pe.wait_ge(nT_ready, 1)

                    def ret_scores(h):
                        if h >= 2:
                            pe.wait_ge(rs_ready, h - 1)
                        mm(M[:, h % 2, 0:T], kT[:, h, 0:P], qT[:, h, :], start=True, stop=True)
                        mm(M[:, h % 2, T:T + P], kT[:, h, P:T], qT[:, h, P:T], start=True, stop=True).then_inc(rs_done, 1)

                    def ret_out(h):
                        pe.wait_ge(rs_ready, h + 1)
                        e = slice(h * P, (h + 1) * P)
                        mm(M[:, 2, e], ret_s[:, h % 2, 0:P], ret_v[:, 0, e], start=True, stop=True)
                        mm(M[:, 3, e], ret_s[:, h % 2, P:T], ret_v[:, 0, e], start=True, stop=False)
                        mm(M[:, 3, e], ret_s[:, h % 2, T:T + P], ret_v[:, 1, e], start=False, stop=True).then_inc(ro_done, 1)

                    ret_scores(0)
                    ret_scores(1)
                    pe.wait_ge(yg_lo, 1)
                    chunk("branch_s5_0")
                    pe.wait_ge(nrope_ready, 2)
                    blocks_T(1024, nq).then_inc(nT_done, 1)
                    chunk("branch_s5_1")
                    pe.wait_ge(nT_ready, 2)
                    ret_out(0)
                    ret_out(1)
                    ret_scores(2)
                    ret_scores(3)
                    chunk("merge_lru_0", 0)
                    ret_out(2)
                    ret_out(3)
                    pe.wait_ge(hid_ready, 1)
                    for k in range(2):
                        mm(M[0:32, 0, 0:HD], hid[:, 0, k, :], cw2[:, 0, k, :], start=k == 0, stop=k == 1)
                    for k in range(2):
                        last = mm(M[:, 0, HD:2 * HD], hid8[:, k].rearrange("p h n -> p (h n)"), cw2[:, 1, k, :], start=k == 0, stop=k == 1)
                    last.then_inc(cw_done, 1)
                    chunk("merge_lru_0", 1)
                    pe.wait_ge(kc_ready, 1)
                    tr(M[:, 1, 0:32], kc[:, :, :].rearrange("p u d -> p (u d)"), 32).then_inc(kcT_done, 1)
                    chunk("merge_lru_1", 0)
                    pe.wait_ge(rn_ready, 1)
                    blocks_T(1024, ro).then_inc(rnT_done, 1)
                    pe.wait_ge(vbd_ready, 1)
                    pe.wait_ge(kcT_ready, 1)
                    for e in range(2):
                        r = slice(64 * e, 64 * e + 64)
                        for t in range(TT):
                            for h in range(4):
                                at = t * 64 + h * 16
                                last = mm(M[:, e, at:at + 16], nqT[r, h, t * P:(t + 1) * P], kcT[r, (h // 2) * 16:(h // 2) * 16 + 16],
                                          start=True, stop=True)
                    last.then_inc(cs_done, 1)
                    chunk("merge_lru_1", 1)
                    pe.wait_ge(cp_ready, 1)
                    pe.wait_ge(yr_ready, 1)
                    for t in range(TT):
                        last = tr(M[:, 3, t * P:(t + 1) * P], cmp_p[:, t * P:(t + 1) * P])
                    last.then_inc(cpT_done, 1)

                    def attention_scores(i):
                        h = i % NKV
                        if i:
                            pe.wait_ge(at_pT_ready, i)
                        for e in range(2):
                            r = slice(64 * e, 64 * e + 64)
                            def small_():
                                for n in range(2):
                                    at = (2 * e + n) * P
                                    last_ = mm(M[:, 2, at:at + P], nqT[r, 2 * h + n, 0:P], nkT[r, i, 0:P], start=True, stop=True)
                                return last_
                            if e == 0:
                                small_().then_inc(at_even, 1)
                            for n in range(2):
                                mm(M[:, e, n * T:(n + 1) * T], nqT[r, 2 * h + n, P:T], nkT[r, i, :], start=True, stop=True)
                            if e == 1:
                                pe.wait_ge(at_even, i + 1)
                                last = small_()
                        last.then_inc(at_s, 1)

                    def attention_T(i):
                        pe.wait_ge(at_exp, 8 * (i + 1))
                        for b in range(12):
                            last = tr(MF[:, b * P:(b + 1) * P], prob[:, b * P:(b + 1) * P])
                        last.then_inc(at_pT, 1)

                    def attention_product(i):
                        pe.wait_ge(at_pT_ready, i + 1)
                        if i:
                            pe.wait_ge(at_no, i)
                        for b, g in enumerate((0, 2, 1, 3)):
                            mm(M[:, 3, g * HD:(g + 1) * HD], probT[:, 8 + b, :], nv[:, 0, i, :], start=True, stop=True)
                            mm(M[:, 3, 256 + g * HD:256 + (g + 1) * HD], probT[:, 2 * b, :], nv[:, 0, i, :], start=True, stop=False)
                            last = mm(M[:, 3, 256 + g * HD:256 + (g + 1) * HD], probT[:, 2 * b + 1, :], nv[:, 1, i, :], start=False, stop=True)
                        last.then_inc(at_o, 1)

                    attention_scores(0)
                    pe.wait_ge(yg_lo, 2)
                    chunk("branch_lru_0")
                    chunk("branch_lru_1")
                    attention_T(0)
                    pe.wait_ge(cpT_ready, 1)
                    attention_product(0)
                    attention_scores(1)
                    chunk("merge_ret_0")
                    attention_T(1)
                    chunk("merge_ret_1", 0)
                    attention_product(1)
                    attention_scores(2)
                    chunk("merge_ret_1", 1)
                    pe.wait_ge(yg_lo, 3)
                    chunk("branch_ret_0")
                    attention_T(2)
                    chunk("branch_ret_1")
                    attention_product(2)
                    attention_scores(3)
                    chunk("gate_nsa")
                    attention_T(3)
                    chunk("merge_nsa_0", 0)
                    attention_product(3)
                    pe.wait_ge(at_pT_ready, 4)
                    for t in range(TT):
                        last = mm(M[:, t, :], cmp_pT[:, t * P:(t + 1) * P], vbd[:, :, :].rearrange("p h d -> p (h d)"), start=True, stop=True)
                    last.then_inc(co_done, 1)
                    chunk("merge_nsa_0", 1)
                    pe.wait_ge(no_cmp, 1)
                    blocks_T(1024, nq).then_inc(noT_done, 1)
                    chunk("merge_nsa_1")
                    pe.wait_ge(yg_lo, 4)
                    chunk("branch_nsa_0")
                    chunk("branch_nsa_1", 0)
                    pe.wait_ge(mt_free, 5)
                    features_T(range(0, 4), merged, mT_done)
                    chunk("branch_nsa_1", 1)
                    pe.wait_ge(mlo_done, 2)
                    chunk("out_0a")
                    pe.wait_ge(mt_free, 6)
                    features_T(range(4, 8), merged, mT_done)
                    chunk("out_1a")
                    pe.wait_ge(nxt["dt_rows"], 1)
                    turn_vectors(nxt)
                    pe.wait_ge(mlo_done, 4)
                    chunk("out_0b")
                    chunk("out_1b")

            with nc.Block() as block:
                @block.gpsimd
                def _(gp):
                    gp.sem_clear(range(sems[0].num, sems[-1].num + 1))

        with nc.Block() as block:
            g_row = mt[:, 0].rearrange("p a n -> p (a n)")

            @block.sync
            def _(sp):
                sp.dma_start(g_row, a["final_norm_g"].unsqueeze(0).to_broadcast([P, D])).then_inc(norm_loaded, 16)
                for t in range(TT):
                    sp.wait_ge(normed, t + 1)
                    sp.dma_start(out[0, t * P:(t + 1) * P, :], merged[:, t, :]).then_inc(stored, 16)
                sp.wait_ge(stored, 16 * TT)

            @block.vector
            def _(dve):
                dve.wait_ge(norm_loaded, 16)
                for t in range(TT):
                    nc.vector.scalar_tensor_tensor(merged[:, t, :], x[:, t, :], st[:, 2 + t:3 + t], g_row,
                                                   ALU.mult, ALU.mult).then_inc(normed, 1)


_INS = ["x", "norm_g", "w_in", "lru_conv_w", "lru_conv_b", "lru_wa", "lru_ba", "lru_wx", "lru_bx", "lru_lambda",
        "s5_lambda_re", "s5_lambda_im", "s5_b_re", "s5_b_im", "s5_c_re", "s5_c_im", "s5_log_dt", "s5_d",
        "s5_w_glu", "s5_b_glu", "nsa_pos_k", "nsa_pos_v", "nsa_ck_w1", "nsa_ck_w2", "nsa_cv_w1", "nsa_cv_w2",
        "w_branch", "w_out", "final_norm_g"]


def kernel(**inputs):
    import numpy as _np
    import concourse.bacc as _bacc
    from concourse import mybir as _mybir
    from concourse.bass_utils import run_bass_kernel_spmd as _run

    nc = _bacc.Bacc("TRN2", target_bir_lowering=False, num_devices=1)
    arrays = {name: _np.ascontiguousarray(inputs[name]) for name in _INS}
    arrays["constants"] = shape_constants()
    aps = {n: nc.dram_tensor(f"in_{n}", v.shape, _mybir.dt.from_np(v.dtype), kind="ExternalInput").ap()
           for n, v in arrays.items()}
    result = nc.dram_tensor("out", (1, T, D), _mybir.dt.float32, kind="ExternalOutput").ap()
    hybrid_trunk(nc, aps, result)
    r = _run(nc, [{f"in_{n}": v for n, v in arrays.items()}], core_ids=[0])
    return r.results[0]["out"]
```

```python
import math
from contextlib import ExitStack

import numpy as np
import concourse.bass as bass
from concourse import mybir

P = 128
D = 1024
T = 256
TT = T // P
DEPTH = 2
BW = 512
KD = D // P
KB = BW // P
NH_RET = 4
HD_RET = 128
NHQ = 8
NKV = 2
HD = 64
NCMP = (T - 32) // 16 + 1
NS5 = 32 * 64 // P
EPS = 1e-6
EPS_RET = 1e-5
CMP_W = 280

COL_LRU, COL_S5, COL_RET, COL_NQ, COL_CMP, COL_KV, COL_BG, COL_GATE, COL_MERGE = (
    0, 512, 1024, 2560, 3072, 3328, 3840, 3864, 5912)
GATE_OF = {"lru": 0, "s5": 1, "ret": 2, "nsa": 3}

CHUNKS = [("u_s5", 8, 512), ("cmp", 8, CMP_W), ("u_lru", 8, 512), ("ret_v", 8, 512), ("nsa_kv", 8, 512),
          ("ck", 16, 256), ("gate_s5", 8, 512), ("cv", 16, 256), ("gate_lru", 8, 512),
          ("merge_s5_0", 8, 512), ("merge_s5_1", 8, 512), ("ret_q", 8, 512), ("ret_k", 8, 512),
          ("nsa_q", 8, 512), ("glu_a", 4, 512), ("glu_b", 4, 512), ("gate_ret", 8, 512), ("branch_s5_0", 4, 512),
          ("branch_s5_1", 4, 512), ("merge_lru_0", 8, 512), ("merge_lru_1", 8, 512),
          ("branch_lru_0", 4, 512), ("branch_lru_1", 4, 512),
          ("merge_ret_0", 8, 512), ("merge_ret_1", 8, 512), ("branch_ret_0", 4, 512),
          ("branch_ret_1", 4, 512), ("gate_nsa", 8, 512), ("merge_nsa_0", 8, 512),
          ("merge_nsa_1", 8, 512), ("branch_nsa_0", 4, 512), ("branch_nsa_1", 4, 512),
          ("out_0a", 4, 512), ("out_1a", 4, 512), ("out_0b", 4, 512), ("out_1b", 4, 512)]
CHUNK = {name: c for c, (name, _, _) in enumerate(CHUNKS)}
BRANCHES = ["s5", "lru", "ret", "nsa"]

UNITS, UNIT_END, UNIT_USED = [], [], []
for _c, (_name, _kt, _w) in enumerate(CHUNKS):
    if _name not in ("ck", "cv"):
        _k0 = 4 if _name[-1] == "b" and _name[:3] == "out" else 0
        UNITS += [(_c, k, 2, _w) for k in range(_k0, _k0 + _kt, 2)]
    UNIT_END.append(len(UNITS))
NU = len(UNITS)
for _u in range(NU):
    UNIT_USED.append((UNIT_USED[-1] if _u else 0) + (_u + 1 != UNIT_END[UNITS[_u][0]]))
N_RAW = 4
N_FIRST = 2
N_SPLIT = 5

V_NORM, V_CONV, V_CONVB, V_BA, V_BX, V_LAM, V_D, V_BGLU, V_LR, V_LI, V_DT, V_ROWS = (
    0, 8, 24, 28, 32, 36, 40, 44, 52, 68, 96, 112)

TWO_PI = 2.0 * math.pi
PI2_A = 6.28125
PI2_B = 0.0019350051879882812
PI2_C = TWO_PI - PI2_A - PI2_B
TURN = 6.2831845
ROUND = 12582912.0
GELU_C = math.sqrt(2.0 / math.pi)

CONST = {}
_at = 0
for _n, _s in (("ident", P), ("ret_cos", TT * 64), ("ret_sin", TT * 64), ("nsa_cos", TT * 8), ("nsa_sin", TT * 8),
               ("cmp_cos", 8), ("cmp_sin", 8), ("decay", NH_RET * T), ("causal", 2 * P), ("cmp_add", TT * 16),
               ("cmp_keep", TT * 16), ("head", NHQ), ("group", 2), ("time", T)):
    CONST[_n] = (_at, _s)
    _at += _s
N_CONST = _at


def shape_constants():
    f32 = np.float32
    out = np.zeros((P, N_CONST), f32)

    def put(name, a):
        at, size = CONST[name]
        out[:a.shape[0], at:at + size] = a.reshape(a.shape[0], size)

    def rope(pos, base, rot):
        half = rot // 2
        inv = (f32(base) ** (-np.arange(half, dtype=f32) * f32(2.0) / f32(rot))).astype(f32)
        ang = (pos.astype(f32)[..., None] * inv).astype(f32).astype(np.float64)
        return np.cos(ang).astype(f32), np.sin(ang).astype(f32)

    p = np.arange(P)
    tok = p[:, None] + P * np.arange(TT)[None, :]
    put("ident", np.eye(P, dtype=f32))
    c, s = rope(tok, 10000.0, HD_RET)
    put("ret_cos", c), put("ret_sin", s)
    c, s = rope(tok, 500000.0, HD // 4)
    put("nsa_cos", c), put("nsa_sin", s)
    c, s = rope((np.arange(32) % 16) * 16 + 31, 500000.0, HD // 4)
    put("cmp_cos", c), put("cmp_sin", s)
    gamma = 1.0 - np.exp(np.linspace(math.log(1 / 32), math.log(1 / 512), NH_RET))
    diff = np.arange(T)[None, :] - p[:, None]
    put("decay", np.stack([np.where(diff >= 0, g ** np.maximum(diff, 0), 0) for g in gamma], 1) * HD_RET ** -0.5)
    m = np.zeros((P, 2, P), f32)
    m[:, 1] = np.where(p[None, :] <= p[:, None], 0, -1e30)
    put("causal", m)
    n = np.arange(16)
    keep = (n * 16 + 31 <= tok[:, :, None]) & (n < NCMP)
    put("cmp_add", np.where(keep, 0, -1e30)), put("cmp_keep", keep * 1.0)
    put("head", ((p[:, None] // 16 == np.arange(NHQ)[None, :]) & (p[:, None] % 16 < NCMP)) * 1.0)
    put("group", ((p[:, None] // 16) % 2 == np.arange(2)[None, :]) * 1.0)
    put("time", np.broadcast_to(np.arange(T), (P, T)))
    return out


def hybrid_trunk(nc, a, out):
    f32, f32r = mybir.dt.float32, mybir.dt.float32r
    ALU, ACT, AX = mybir.AluOpType, mybir.ActivationFunctionType, mybir.AxisListType.X
    ctx = ExitStack()
    with ctx:
        def sb(name, shape, dt=f32):
            return ctx.enter_context(nc.sbuf_tensor(name, shape, dt))

        sems = []

        def sem(name):
            sems.append(ctx.enter_context(nc.semaphore(name)))
            return sems[-1]

        const = sb("const", [P, N_CONST])
        x = sb("x", [P, TT, D])
        raw = sb("raw", [P, N_RAW, 1024])
        w_hi = sb("w_hi", [P, N_SPLIT, 1024], f32r)
        w_lo = sb("w_lo", [P, N_SPLIT, 1024], f32r)
        h_hi = sb("h_hi", [P, KD, T], f32r)
        h_lo = sb("h_lo", [P, KD, T], f32r)
        ys_hi = sb("ys_hi", [P, KB, T], f32r)
        ys_lo = sb("ys_lo", [P, KB, T], f32r)
        merged = sb("merged", [P, TT, D])
        mt = sb("mt", [P, 2, TT, 512])
        gate = sb("gate", [P, 2, KB, T])
        rows = sb("rows", [P, P])
        rows2 = sb("rows2", [32, P])
        dt_in = sb("dt_in", [P, 2])
        vec = sb("vec", [P, V_ROWS])
        pos = sb("pos", [P, 2, 16])
        small = sb("small", [P, 30, 16])
        wa = sb("wa", [P, KB, P])
        wx = sb("wx", [P, KB, P])
        cw2 = sb("cw2", [P, 2, 2, HD])
        bT_hi = sb("bT_hi", [P, 2, KB, P], f32r)
        bT_lo = sb("bT_lo", [P, 2, KB, P], f32r)
        cT = sb("cT", [P, 2, KB, P])
        u_s5 = sb("u_s5", [P, KB, T])
        u_lru = sb("u_lru", [P, KB, T + 3])
        ret_v = sb("ret_v", [P, TT, BW])
        kd = sb("kd", [P, TT, 2, NKV, 2, HD])
        nv = sb("nv", [P, TT, 4, HD])
        hid = sb("hid", [P, 2, 2, 32])
        hid8 = sb("hid8", [P, 2, NHQ, 16])
        vbd = sb("vbd", [P, NHQ, HD])
        kc = sb("kc", [32, 2, HD])
        kcT = sb("kcT", [P, 32])
        bgate = sb("bgate", [P, TT, 24])
        st = sb("st", [P, 96])
        qT = sb("qT", [P, NH_RET, T])
        kT = sb("kT", [P, NH_RET, T])
        nqT = sb("nqT", [P, 4, T])
        nkT = sb("nkT", [P, 4, T])
        sc = sb("sc", [P, 7168])
        half_pi = sb("half_pi", [P, 1])
        m_half = sb("m_half", [P, 8])
        proj = [ctx.enter_context(nc.psum_tensor(f"proj{i}", [P, 1024], f32)) for i in range(2)]
        M = ctx.enter_context(nc.psum_tensor("M", [P, 4, 512], f32))

        def cst(name):
            at, size = CONST[name]
            return const[:, at:at + size]

        def S(i, n=1):
            return small[:, i, :] if n == 1 else small[:, i:i + n, :]

        def cols(at, n):
            return sc[:, at:at + n]

        ident = cst("ident")
        cos_sin = cols(0, 2048).rearrange("p (b f j t) -> p b f j t", b=2, f=2, j=2)
        ang_a = cols(2048, 512).rearrange("p (j t) -> p j t", j=2)
        ang_s = cols(2560, 512).rearrange("p (j t) -> p j t", j=2)
        s5_t = cols(3072, 2048).rearrange("p (f j t) -> p f j t", f=4, j=2)
        s5_h = cols(5120, 2048).rearrange("p (b f j t) -> p b f j t", b=2, f=2, j=2)
        b_exp = cols(3072, 1024).rearrange("p (f s g c) -> p f s g c", f=2, s=NS5, g=2)
        b_tmp = cols(4096, 512).rearrange("p (f s c) -> p f s c", f=2, s=NS5)
        b_nat = cols(6144, 512).rearrange("p (f s c) -> p f s c", f=2, s=NS5)
        c_nat = cols(5120, 1024).rearrange("p (f q g n) -> p f q g n", f=2, q=KB, g=2)
        gelu_t = cols(2048, 1024)
        y_s5 = qT
        x2 = kT[:, 0:2, :].rearrange("p m (h t) -> p m h t", h=NKV)
        blocks = nqT[:, :, :].rearrange("p a (b h n) -> p (a b) h n", b=8, h=2)
        cmp_tm = qT[:, 2:4, :]
        hid_tm = kT[0:32, 0:2, :]
        u_hi, u_lo = ys_hi, ys_lo
        hid_y = kT[:, 2, 0:128]
        hid_q = kT[:, 3, 0:128]
        xc = cols(0, 1024).rearrange("p (t n) -> p t n", t=KB)
        l_r = cols(1024, 1024).rearrange("p (t n) -> p t n", t=KB)
        l_i = cols(2048, 1024).rearrange("p (t n) -> p t n", t=KB)
        l_a = cols(3072, 1024).rearrange("p (t n) -> p t n", t=KB)
        l_m = cols(4096, 1024).rearrange("p (t n) -> p t n", t=KB)
        l_h = cols(5120, 1024).rearrange("p (t n) -> p t n", t=KB)
        ret_s = cols(6144, 768).rearrange("p (b n) -> p b n", b=2)
        rope_t = kT[:, :, :].rearrange("p a b -> p (a b)").rearrange("p (f a h c) -> p f a h c", f=2, a=TT, h=NH_RET)
        rope_n = cols(5120, 512).rearrange("p (f a h c) -> p f a h c", f=4, a=TT, h=NHQ)
        ro = u_lru[:, :, :].rearrange("p a b -> p (a b)")[:, 0:1024]
        nq = u_s5[:, :, :].rearrange("p a b -> p (a b)")
        nq4 = nq.rearrange("p (a h c) -> p a h c", a=TT, h=NHQ)
        no4 = nq4
        prob = cols(0, 1536)
        probT = cols(1536, 1536).rearrange("p (b n) -> p b n", b=12)
        cmp_s = cols(3072, 256).rearrange("p (e a h n) -> p e a h n", e=2, a=TT, h=4)
        cmp_pT = cols(3328, 256)
        cmp_p = cols(3584, 256)
        att_t = cols(4096, 512)
        glu_v = cols(5120, 1024)
        glu_t = cols(0, 1024)
        bn = cols(6912, 48).rearrange("p (i n) -> p i n", n=6)
        mv = cols(6960, 16).rearrange("p (i n) -> p i n", n=2)
        kc_t = cols(7040, 32)[0:32].rearrange("p (f n) -> p f n", f=4)
        MF = M[:, :, :].rearrange("p b n -> p (b n)")
        g_row = kd[:, :, :, :, :, :].rearrange("p a y h u d -> p (a y h u d)")

        x_loaded, const_loaded = (ctx.enter_context(nc.semaphore(n)) for n in ("x_loaded", "const_loaded"))
        b_loaded, c_loaded, wl_loaded, cw1_loaded, cw_loaded = (sem(n) for n in (
            "b_loaded", "c_loaded", "wl_loaded", "cw1_loaded", "cw_loaded"))
        raw_loaded = [sem(f"raw_loaded{i}") for i in range(N_RAW)]
        hi_done, lo_done, unit_used = sem("hi_done"), sem("lo_done"), sem("unit_used")
        chunk_done = sem("chunk_done")
        evacuated = [sem("evacuated0"), sem("evacuated1")]
        dve_order = sem("dve_order")
        x_norm, xT_done = sem("x_norm"), sem("xT_done")
        hhi_done, hlo_done = sem("hhi_done"), sem("hlo_done")
        lam_abs, lam_exp, dt_exp, mag_arg, mag_exp = (sem(n) for n in ("lam_abs", "lam_exp", "dt_exp", "mag_arg", "mag_exp"))
        th_ready, th_sin = sem("th_ready"), sem("th_sin")
        b_ready, c_ready, bT_done, cT_done, bcT_ready = (sem(n) for n in ("b_ready", "c_ready", "bT_done", "cT_done", "bcT_ready"))
        ang_ready, trig_done, bu_done, bu_used, h_done, y_done = (sem(n) for n in (
            "ang_ready", "trig_done", "bu_done", "bu_used", "h_done", "y_done"))
        y_used, s5_split = sem("y_used"), sem("s5_split")
        z_arg, z_tanh, z_ready, z_hi, z_lo = (sem(n) for n in ("z_arg", "z_tanh", "z_ready", "z_hi", "z_lo"))
        cmp_read, cmpT_done, blk_ready = (sem(n) for n in ("cmp_read", "cmpT_done", "blk_ready"))
        hid_tm_ready, hidT_done, hid_arg, hid_tanh, hid_ready = (sem(n) for n in (
            "hid_tm_ready", "hidT_done", "hid_arg", "hid_tanh", "hid_ready"))
        gate_tanh, mt_free = (sem(n) for n in ("gate_tanh", "mt_free"))
        yg_ready, yg_hi, yg_lo = (sem(n) for n in ("yg_ready", "yg_hi", "yg_lo"))
        xc_ready, lru_mm, lru_act, lru_m2, lru_sqrt = (sem(n) for n in ("xc_ready", "lru_mm", "lru_act", "lru_m2", "lru_sqrt"))
        rope_ready, qkT_done, qkT_ready = sem("rope_ready"), sem("qkT_done"), sem("qkT_ready")
        rs_done, rs_ready, ro_done, rvar, rrstd, rn_ready, rnT_done, yr_ready = (sem(n) for n in (
            "rs_done", "rs_ready", "ro_done", "rvar", "rrstd", "rn_ready", "rnT_done", "yr_ready"))
        nrope_ready, nT_done, nT_ready = (sem(n) for n in (
            "nrope_ready", "nT_done", "nT_ready"))
        cw_done, kc_ready, vbd_ready, kcT_done, kcT_ready = (sem(n) for n in (
            "cw_done", "kc_ready", "vbd_ready", "kcT_done", "kcT_ready"))
        cs_done, cs_sub, cs_exp, cp_ready, cpT_done, cpT_ready, co_done, no_cmp = (sem(n) for n in (
            "cs_done", "cs_sub", "cs_exp", "cp_ready", "cpT_done", "cpT_ready", "co_done", "no_cmp"))
        at_even, at_s, at_max, at_exp, at_pT, at_pT_ready, at_o, at_no = (sem(n) for n in (
            "at_even", "at_s", "at_max", "at_exp", "at_pT", "at_pT_ready", "at_o", "at_no"))
        noT_done = sem("noT_done")
        mT_done, mhi_done, mlo_done = sem("mT_done"), sem("mhi_done"), sem("mlo_done")
        out_token, x_half = sem("out_token"), sem("x_half")
        STAGE = ("vectors_loaded", "raw_first", "dt_rows", "vecT", "vec_ready", "sq", "msq", "var", "rstd", "g_loaded")
        nxt = {n: sem("next_" + n) for n in STAGE}
        first = {n: ctx.enter_context(nc.semaphore("first_" + n)) for n in STAGE}
        normed, stored = (ctx.enter_context(nc.semaphore(n)) for n in ("normed", "stored"))

        raw_target = []
        _count = [0] * N_RAW
        for u, (c, _, _, _) in enumerate(UNITS):
            if u >= N_FIRST:
                _count[u % N_RAW] += 32 if c == CHUNK["cmp"] else 16
            raw_target.append(_count[u % N_RAW])

        def ch(name):
            return CHUNK[name] + 1

        def wait_unit_read(eng, u):
            c = UNITS[u][0]
            if u + 1 == UNIT_END[c]:
                eng.wait_ge(chunk_done, c + 1)
            else:
                eng.wait_ge(unit_used, UNIT_USED[u])

        def pr(name):
            return proj[CHUNK[name] % 2]

        def evac(name):
            return evacuated[CHUNK[name] % 2]

        def ev(name):
            return CHUNK[name] // 2 + 1

        def cw1(n):
            return merged[:, n, :] if n < 2 else mt[:, n - 2].rearrange("p a n -> p (a n)")

        def flat(t):
            return t.rearrange("p a b -> p (a b)")

        def gated_features(name):
            return {"s5": flat(gate[:, 0]), "lru": flat(gate[:, 1]), "ret": flat(qT[:, :, :]), "nsa": MF[:, 1024:2048]}[name]

        def bc(ap, shape):
            return ap.to_broadcast(shape)

        def load_unit(sp, u, l, signal):
            c, k, n, w = UNITS[u]
            name = CHUNKS[c][0]
            dst = raw[:, u % N_RAW, 0:n * w].rearrange("p (k n) -> p k n", k=n)

            def load(d, src):
                sp.dma_start(d, src.rearrange("(k p) n -> p k n", p=P)).then_inc(signal, 16)

            def w_in(col, width, d=None):
                load(dst if d is None else d, a["w_in"][l][k * P:(k + n) * P, col:col + width])

            kind = name.split("_")[0]
            half = 512 * int(name[4] if kind == "out" else name[-1]) if kind in ("merge", "branch", "out") else 0
            if kind == "u":
                w_in(COL_S5 if name == "u_s5" else COL_LRU, w)
            elif kind == "ret":
                w_in(COL_RET + BW * "qkv".index(name[-1]), w)
            elif name == "nsa_q":
                w_in(COL_NQ, w)
            elif name == "nsa_kv":
                w_in(COL_KV, w)
            elif name == "cmp":
                w_in(COL_CMP, 256, dst[:, :, 0:256])
                w_in(COL_BG, 24, dst[:, :, 256:CMP_W])
            elif kind == "gate":
                w_in(COL_GATE + BW * GATE_OF[name[5:]], w)
            elif kind == "merge":
                w_in(COL_MERGE + D * GATE_OF[name[6:-2]] + half, w)
            elif kind == "glu":
                at = 512 * "ab".index(name[-1])
                load(dst, a["s5_w_glu"][l][k * P:(k + n) * P, at:at + w])
            elif kind == "branch":
                load(dst, a["w_branch"][l][GATE_OF[name[7:-2]]][k * P:(k + n) * P, half:half + w])
            else:
                load(dst, a["w_out"][l][k * P:(k + n) * P, half:half + w])


        def load_vectors(sp, l, signal):
            def load(dst, src):
                sp.dma_start(dst, src).then_inc(signal, 16)

            for name, at, n in (("norm_g", V_NORM, 8), ("lru_conv_w", V_CONV, 16), ("lru_conv_b", V_CONVB, 4),
                                ("lru_ba", V_BA, 4), ("lru_bx", V_BX, 4), ("lru_lambda", V_LAM, 4), ("s5_d", V_D, 4),
                                ("s5_b_glu", V_BGLU, 8), ("s5_lambda_re", V_LR, 16), ("s5_lambda_im", V_LI, 16)):
                src = a[name][l]
                if name == "lru_conv_w":
                    src = src.rearrange("k (t p) -> (k t) p", p=P)
                elif len(src.shape) == 2:
                    src = src.rearrange("(s g) n -> s (g n)", g=2)
                else:
                    src = src.rearrange("(t p) -> t p", p=P)
                load(rows[at:at + n, :], src)
            load(dt_in[V_DT:V_ROWS, :], a["s5_log_dt"][l].rearrange("(s g) -> s g", g=2))
            for m, name in enumerate(("nsa_pos_k", "nsa_pos_v")):
                load(rows2[16 * m:16 * m + 16, :], a[name][l].rearrange("(r s) d -> r (s d)", s=2))

        VECTORS_ALL, RAW_ALL = 16 * 13, 16 * N_FIRST

        def expand_dt(stage):
            nc.vector.tensor_copy(rows[V_DT:V_ROWS, :].rearrange("p (g n) -> p g n", g=2),
                                  bc(dt_in[V_DT:V_ROWS, :].unsqueeze(2), [16, 2, 64])).then_inc(stage["dt_rows"], 1)

        def turn_vectors(stage):
            for dst, src, n in ((M[:, 0, 0:V_ROWS], rows[0:V_ROWS, :], V_ROWS), (M[:, 0, P:P + 32], rows2[:, :], 32)):
                nc.tensor.transpose(dst, src, ident[0:n, 0:n]).then_inc(stage["vecT"], 1)

        def keep_vectors(stage):
            nc.vector.tensor_copy(vec[:, :], M[:, 0, 0:V_ROWS])
            nc.vector.tensor_copy(flat(pos[:, :, :]), M[:, 0, P:P + 32]).then_inc(stage["vec_ready"], 1)

        def squares(stage, half, t):
            e = slice(512 * half, 512 * half + 512)
            nc.scalar.activation(merged[:, t, e], x[:, t, e], ACT.Square,
                                 accum_out=st[:, 4 + 2 * half + t:5 + 2 * half + t]).then_inc(stage["sq"], 1)

        def mean_square(dve, stage):
            dve.wait_ge(stage["sq"], 2 * TT)
            nc.vector.tensor_tensor(st[:, 0:2], st[:, 4:6], st[:, 6:8], ALU.add).then_inc(stage["msq"], 1)
            dve.wait_ge(stage["msq"], 1)
            nc.vector.tensor_scalar(st[:, 0:2], st[:, 0:2], 1.0 / D, EPS, ALU.mult, ALU.add).then_inc(stage["var"], 1)

        def inverse_root(gp, stage):
            gp.wait_ge(stage["var"], 1)
            nc.gpsimd.tensor_tensor(st[:, 2:4], st[:, 0:2], m_half[:, 0:2], ALU.pow).then_inc(stage["rstd"], 1)

        with nc.Block() as block:
            @block.sync
            def _(sp):
                sp.dma_start(x[:, :, :], a["x"][0].rearrange("(t p) d -> p t d", p=P)).then_inc(x_loaded, 16)
                sp.wait_ge(first["dt_rows"], 1)
                sp.dma_start(const[:, :], a["constants"]).then_inc(const_loaded, 16)
                load_vectors(sp, 0, first["vectors_loaded"])
                for u in range(N_FIRST):
                    load_unit(sp, u, 0, first["raw_first"])
                sp.wait_ge(first["raw_first"], RAW_ALL)

            @block.gpsimd
            def _(gp):
                gp.memset(half_pi[:, :], math.pi / 2)
                gp.memset(m_half[:, :], -0.5)
                gp.memset(wa[:], 0.0)
                gp.memset(wx[:], 0.0)
                gp.memset(rows[:], 0.0).then_inc(first["dt_rows"], 1)
                gp.wait_ge(first["dt_rows"], 1)
                inverse_root(gp, first)

            @block.scalar
            def _(act):
                act.wait_ge(x_loaded, 16)
                for half in range(2):
                    for t in range(TT):
                        squares(first, half, t)

            @block.vector
            def _(dve):
                mean_square(dve, first)
                dve.wait_ge(first["vectors_loaded"], VECTORS_ALL)
                expand_dt(first)
                dve.wait_ge(first["vecT"], 2)
                keep_vectors(first)

            @block.tensor
            def _(pe):
                pe.wait_ge(const_loaded, 16)
                pe.wait_ge(first["dt_rows"], 2)
                turn_vectors(first)

        with nc.Fori(0, DEPTH) as l:
            with nc.Block() as block:
                @block.sync
                def _(sp):
                    def load_cw1(name):
                        for n in range(4):
                            sp.dma_start(cw1(n).rearrange("p (k n) -> p k n", k=4),
                                         a[f"nsa_{name}_w1"][l][512 * n:512 * n + 512, :].rearrange("(k p) n -> p k n", p=P)
                                         ).then_inc(cw1_loaded, 16)

                    for u in range(N_FIRST, N_RAW):
                        load_unit(sp, u, l, raw_loaded[u])
                    for f, name in enumerate(("s5_b_re", "s5_b_im")):
                        sp.dma_start(b_nat[:, f], a[name][l].rearrange("(s g) n c -> (g n) s c", g=2)).then_inc(b_loaded, 16)
                    for f, name in enumerate(("s5_c_re", "s5_c_im")):
                        for g in range(2):
                            sp.dma_start(c_nat[:, f, :, g], a[name][l].rearrange("(q r) c n -> (r c) q n", q=KB)).then_inc(c_loaded, 16)
                    cw1_at = {UNIT_END[CHUNK["u_lru"]] + 3: "ck", UNIT_END[CHUNK["gate_s5"]] + 2: "cv"}
                    for u in range(N_RAW, NU):
                        if u in cw1_at:
                            name = cw1_at[u]
                            if name == "ck":
                                sp.wait_ge(xT_done, 4)
                            else:
                                sp.wait_ge(chunk_done, ch("ck"))
                            load_cw1(name)
                        if u == UNIT_END[CHUNK["nsa_kv"]]:
                            for tile, name in ((wa, "lru_wa"), (wx, "lru_wx")):
                                for g in range(2):
                                    sp.dma_start(tile[64 * g:64 * g + 64, :, 64 * g:64 * g + 64],
                                                 a[name][l].rearrange("(t g) i j -> g i t j", g=2)[g]).then_inc(wl_loaded, 16)
                            for m, name in enumerate(("nsa_ck_w2", "nsa_cv_w2")):
                                sp.dma_start(cw2[:, m], a[name][l].rearrange("(k p) d -> p k d", p=P)).then_inc(cw_loaded, 16)
                        if u == UNIT_END[CHUNK["merge_nsa_0"]]:
                            sp.wait_ge(nT_done, 2)
                            sp.dma_start(g_row, a["final_norm_g"].unsqueeze(0).to_broadcast([P, D])).then_inc(nxt["g_loaded"], 16)
                            load_vectors(sp, (l + 1) % DEPTH, nxt["vectors_loaded"])
                        sp.wait_ge(lo_done, u - N_RAW + 1)
                        load_unit(sp, u, l, raw_loaded[u % N_RAW])
                    for u in range(N_FIRST):
                        sp.wait_ge(lo_done, max(w for w in range(NU) if w % N_RAW == u) + 1)
                        load_unit(sp, u, (l + 1) % DEPTH, nxt["raw_first"])
                    sp.wait_ge(nxt["g_loaded"], 16)
                    sp.wait_ge(nxt["raw_first"], RAW_ALL)

                @block.gpsimd
                def _(gp):
                    done = [0]

                    def split_lo(upto):
                        for u in range(done[0], upto):
                            c, _, n, w = UNITS[u]
                            gp.wait_ge(hi_done, u + 1)
                            if u >= N_SPLIT:
                                wait_unit_read(gp, u - N_SPLIT)
                            nc.gpsimd.tensor_tensor(w_lo[:, u % N_SPLIT, 0:n * w], raw[:, u % N_RAW, 0:n * w],
                                                    w_hi[:, u % N_SPLIT, 0:n * w].bitcast(f32), ALU.subtract).then_inc(lo_done, 1)
                        done[0] = max(done[0], upto)

                    split_lo(UNIT_END[CHUNK["merge_lru_0"]] + 1)
                    gp.wait_ge(rvar, 1)
                    nc.gpsimd.tensor_tensor(st[:, 88:96], st[:, 80:88], m_half[:, :], ALU.pow).then_inc(rrstd, 1)
                    split_lo(NU)
                    inverse_root(gp, nxt)

                @block.scalar
                def _(act):
                    done = [0]

                    def run(out_, in_, func, signal=None, **kw):
                        i = nc.scalar.activation(out_, in_, func, **kw)
                        if signal is not None:
                            i.then_inc(signal, 1)

                    def cast_units(upto):
                        for u in range(done[0], upto):
                            c, _, n, w = UNITS[u]
                            if u >= N_FIRST:
                                act.wait_ge(raw_loaded[u % N_RAW], raw_target[u])
                            if u >= N_SPLIT:
                                wait_unit_read(act, u - N_SPLIT)
                            run(w_hi[:, u % N_SPLIT, 0:n * w], raw[:, u % N_RAW, 0:n * w], ACT.Copy, hi_done)
                        done[0] = max(done[0], upto)

                    def next_cast(name):
                        cast_units(min(NU, UNIT_END[CHUNK[name]] + N_SPLIT - 1))
                        act.wait_ge(chunk_done, ch(name))

                    cast_units(2)
                    act.wait_ge(lam_abs, 1)
                    run(S(1)[:, 0:4], S(0)[:, 0:4], ACT.Exp, lam_exp, scale=-1.0)
                    run(S(8), vec[:, V_DT:V_ROWS], ACT.Exp, dt_exp)
                    for k in range(KD):
                        if k % 2 == 0:
                            act.wait_ge(xT_done, k // 2 + 1)
                        run(h_hi[:, k, :], M[:, k // 2, (k % 2) * T:(k % 2 + 1) * T], ACT.Copy, hhi_done,
                            scale=vec[:, V_NORM + k:V_NORM + k + 1])
                    cast_units(3)
                    act.wait_ge(mag_arg, 1)
                    run(S(10), S(9), ACT.Exp, mag_exp)
                    nc.scalar.preload_act_table_set("silu_and_others")
                    act.wait_ge(th_ready, 1)
                    run(S(13), S(12), ACT.Abs, th_sin)
                    act.wait_ge(th_sin, 1)
                    run(S(14), S(13), ACT.Sin, th_sin, bias=half_pi[:, 0:1], scale=-1.0)
                    run(S(15), S(12), ACT.Sin, th_sin)
                    cast_units(N_SPLIT)

                    def trig(p):
                        act.wait_ge(ang_ready, p + 1)
                        run(ang_s, ang_a, ACT.Abs, trig_done)
                        run(cos_sin[:, p % 2, 1], ang_a, ACT.Sin, trig_done, scale=TURN)
                        act.wait_ge(trig_done, 3 * p + 1)
                        run(cos_sin[:, p % 2, 0], ang_s, ACT.Sin, trig_done, scale=-TURN, bias=half_pi[:, 0:1])

                    next_cast("u_s5")
                    run(flat(u_s5[:, :, :]), pr("u_s5")[:, :], ACT.Copy)
                    run(flat(u_hi[:, :, :]), pr("u_s5")[:, :], ACT.Copy, evac("u_s5"))
                    act.wait_ge(bT_done, 1)
                    run(bT_hi[:, :, :, :].rearrange("p f q n -> p (f q n)"), MF[:, 1024:2048], ACT.Copy, bcT_ready)
                    act.wait_ge(cT_done, 1)
                    run(cT[:, :, :, :].rearrange("p f q n -> p (f q n)"), MF[:, 0:1024], ACT.Copy, bcT_ready)
                    cast_units(UNIT_END[CHUNK["u_s5"]] + N_SPLIT)
                    trig(0)
                    next_cast("cmp")
                    cm = pr("cmp")[:, :].rearrange("p (a n) -> p a n", a=TT)
                    run(cmp_tm, cm[:, :, 0:256], ACT.Copy, cmp_read)
                    run(bgate[:, :, :], cm[:, :, 256:CMP_W], ACT.Tanh, cmp_read, scale=0.5)
                    trig(1)
                    act.wait_ge(cmpT_done, 1)
                    for h in range(NKV):
                        for s in range(2):
                            run(x2[64 * s:64 * s + 64, :, h, :],
                                pr("cmp")[64 * h:64 * h + 64, 0:512].rearrange("p (m t s) -> p m t s", m=2, s=2)[:, :, :, s],
                                ACT.Copy, evac("cmp") if h and s else None)
                    next_cast("u_lru")
                    run(u_lru[:, :, 3:T + 3], pr("u_lru")[:, :].rearrange("p (t n) -> p t n", t=KB), ACT.Copy, evac("u_lru"))
                    trig(2)
                    next_cast("ret_v")
                    run(flat(ret_v[:, :, :]), pr("ret_v")[:, :], ACT.Copy, evac("ret_v"))
                    next_cast("nsa_kv")
                    kv = pr("nsa_kv")[:, :].rearrange("p (a y o h d) -> p a y o h d", a=TT, y=2, o=2, h=NKV)
                    for t in range(TT):
                        for dup in range(2):
                            run(kd[:, t, :, :, dup, :], kv[:, t, :, 0], ACT.Copy)
                        run(nv[:, t].rearrange("p (y h) d -> p y h d", y=2), kv[:, t, :, 1], ACT.Copy,
                            evac("nsa_kv") if t else None)
                    trig(3)

                    def hidden(m, name):
                        next_cast(name)
                        run(hid_tm[:, m, :], pr(name)[0:32, 0:256], ACT.Copy, hid_tm_ready)
                        act.wait_ge(hidT_done, m + 1)
                        run(hid_y[:, 64 * m:64 * m + 64], pr(name)[:, 512:576], ACT.Copy, evac(name))

                    hidden(0, "ck")

                    def gate_chunk(name):
                        i = BRANCHES.index(name)
                        next_cast("gate_" + name)
                        if i >= 2:
                            act.wait_ge(yg_lo, i - 1)
                        run(flat(gate[:, i % 2]), pr("gate_" + name)[:, :], ACT.Tanh, gate_tanh, scale=0.5)

                    def merge_chunk(name, half):
                        i = BRANCHES.index(name)
                        full = f"merge_{name}_{half}"
                        next_cast(full)
                        if i == 1:
                            act.wait_ge(evac(f"branch_s5_{half}"), ev(f"branch_s5_{half}"))
                        if i > 1:
                            act.wait_ge(mt_free, 2 * (i - 2) + half + 1)
                        run(flat(mt[:, half]), pr(full)[:, :], ACT.Tanh, evac(full), scale=0.5)

                    def hi_of_gated(name):
                        i = BRANCHES.index(name)
                        act.wait_ge(yg_ready, i + 1)
                        act.wait_ge(chunk_done, ch("glu_b" if i == 0 else f"branch_{BRANCHES[i - 1]}_1"))
                        if name == "ret":
                            act.wait_ge(yr_ready, 1)
                        if name == "nsa":
                            act.wait_ge(noT_done, 1)
                        run(flat(ys_hi[:, :, :]), gated_features(name), ACT.Copy, yg_hi)

                    def attention_exp(i):
                        act.wait_ge(at_max, i + 1)
                        for b, g in enumerate((0, 2, 1, 3)):
                            run(prob[:, b * T:(b + 1) * T], prob[:, b * T:(b + 1) * T], ACT.Exp, at_exp,
                                bias=st[:, 40 + b:41 + b], accum_out=st[:, 52 + g:53 + g])
                            at = 1024 + b * P
                            run(prob[:, at:at + P], prob[:, at:at + P], ACT.Exp, at_exp,
                                bias=st[:, 44 + b:45 + b], accum_out=st[:, 48 + g:49 + g])

                    def attention_evac(i):
                        act.wait_ge(at_pT, i + 1)
                        if i:
                            act.wait_ge(at_o, i)
                        run(flat(probT), MF[:, 0:1536], ACT.Copy, at_pT_ready)

                    trig(4)
                    gate_chunk("s5")
                    trig(5)
                    hidden(1, "cv")
                    gate_chunk("lru")
                    trig(6)
                    merge_chunk("s5", 0)
                    act.wait_ge(hid_arg, 1)
                    run(hid_q, hid_q, ACT.Tanh, hid_tanh, scale=GELU_C)
                    trig(7)
                    merge_chunk("s5", 1)
                    cast_units(UNIT_END[CHUNK["ret_q"]] + N_SPLIT)
                    act.wait_ge(z_arg, 1)
                    run(gelu_t, gelu_t, ACT.Tanh, z_tanh, scale=GELU_C)
                    cast_units(UNIT_END[CHUNK["ret_k"]] + N_SPLIT - 2)
                    act.wait_ge(z_ready, 1)
                    run(flat(ys_hi[:, :, :]), flat(y_s5[:, :, :]), ACT.Copy, z_hi)
                    act.wait_ge(qkT_done, 1)
                    act.wait_ge(z_lo, 1)
                    run(flat(qT[:, :, :]), MF[:, 0:1024], ACT.Copy, qkT_ready)
                    next_cast("nsa_q")
                    run(nq, pr("nsa_q")[:, :], ACT.Copy, evac("nsa_q"), scale=HD ** -0.5)
                    cast_units(UNIT_END[CHUNK["nsa_q"]] + N_SPLIT)
                    act.wait_ge(lru_mm, 1)
                    for t in range(KB):
                        run(l_r[:, t, :], MF[:, t * T:(t + 1) * T], ACT.Tanh, lru_act, scale=0.5, bias=S(3)[:, t:t + 1])
                    for t in range(KB):
                        run(l_i[:, t, :], MF[:, 1024 + t * T:1024 + (t + 1) * T], ACT.Tanh, lru_act, scale=0.5,
                            bias=S(3)[:, 4 + t:5 + t])
                    nc.scalar.preload_act_table_set("exp_and_others")
                    act.wait_ge(lru_act, KB)
                    for t in range(KB):
                        run(l_a[:, t, :], l_r[:, t, :], ACT.Exp, lru_act, scale=S(4)[:, t:t + 1], bias=S(4)[:, t:t + 1])
                        run(l_m[:, t, :], l_r[:, t, :], ACT.Tanh, lru_act, scale=S(4)[:, 4 + t:5 + t], bias=S(4)[:, 4 + t:5 + t])
                    next_cast("glu_a")
                    act.wait_ge(qkT_done, 2)
                    run(flat(kT[:, :, :]), MF[:, 1024:2048], ACT.Copy, qkT_ready)
                    next_cast("glu_b")
                    act.wait_ge(lru_m2, 1)
                    for t in range(KB):
                        run(glu_t[:, t * T:(t + 1) * T], pr("glu_b")[:, t * T:(t + 1) * T], ACT.Tanh,
                            evac("glu_b") if t == KB - 1 else None, scale=0.5, bias=S(5)[:, t:t + 1])
                    act.wait_ge(nT_done, 1)
                    run(flat(nkT[:, :, :]), MF[:, 0:1024], ACT.Copy, nT_ready)
                    hi_of_gated("s5")
                    gate_chunk("ret")
                    act.wait_ge(nT_done, 2)
                    run(flat(nqT[:, :, :]), MF[:, 1024:2048], ACT.Copy, nT_ready)
                    run(flat(l_m), flat(l_m), ACT.Sqrt, lru_sqrt, scale=0.25)
                    nc.scalar.preload_act_table_set("exp_and_others")
                    cast_units(UNIT_END[CHUNK["merge_lru_0"]])
                    hi_of_gated("lru")
                    merge_chunk("lru", 0)
                    act.wait_ge(kcT_done, 1)
                    run(kcT[:, :], M[:, 1, 0:32], ACT.Copy, kcT_ready)
                    cast_units(UNIT_END[CHUNK["merge_lru_1"]])
                    act.wait_ge(rnT_done, 1)
                    run(flat(qT[:, :, :]), MF[:, 1024:2048], ACT.Copy, yr_ready)
                    act.wait_ge(cs_sub, 1)
                    run(cols(3072, 256), cols(3072, 256), ACT.Exp, cs_exp)
                    merge_chunk("lru", 1)
                    act.wait_ge(cpT_done, 1)
                    run(cmp_pT, M[:, 3, 0:256], ACT.Copy, cpT_ready)
                    def cast_room(name, read=0):
                        cast_units(min(NU, UNIT_END[CHUNK[name]] + read + N_SPLIT))

                    cast_room("merge_lru_1")
                    attention_exp(0)
                    cast_room("branch_lru_1", -1)
                    attention_evac(0)
                    hi_of_gated("ret")
                    cast_room("branch_lru_1", 2)
                    attention_exp(1)
                    merge_chunk("ret", 0)
                    cast_room("merge_ret_0", 1)
                    attention_evac(1)
                    merge_chunk("ret", 1)
                    cast_room("merge_ret_1")
                    attention_exp(2)
                    cast_room("branch_ret_1", -1)
                    attention_evac(2)
                    cast_room("branch_ret_1", 2)
                    attention_exp(3)
                    gate_chunk("nsa")
                    cast_room("gate_nsa", 1)
                    attention_evac(3)
                    merge_chunk("nsa", 0)
                    cast_room("merge_nsa_0", 1)
                    hi_of_gated("nsa")
                    merge_chunk("nsa", 1)
                    cast_room("branch_nsa_0")
                    for half in range(2):
                        act.wait_ge(mT_done, half + 1)
                        run(flat(h_hi[:, 4 * half:4 * half + 4, :]), MF[:, 1024 * half:1024 * half + 1024], ACT.Copy, mhi_done)
                        if not half:
                            cast_units(UNIT_END[CHUNK["branch_nsa_1"]] + N_SPLIT)
                    cast_units(NU)
                    for half in range(2):
                        for t in range(TT):
                            act.wait_ge(x_half, 1 + half * (t + 1))
                            squares(nxt, half, t)

                @block.vector
                def _(dve):
                    v = nc.vector
                    links = [0]

                    def link(i):
                        links[0] += 1
                        i.then_inc(dve_order, 1)
                        dve.wait_ge(dve_order, links[0])

                    v.memset(u_lru[:, :, 0:3], 0.0)
                    for half in range(2):
                        for t in range(TT):
                            e = slice(512 * half, 512 * half + 512)
                            v.tensor_scalar(merged[:, t, e], x[:, t, e], st[:, 2 + t:3 + t], None, ALU.mult).then_inc(x_norm, 1)
                    lam, lam_i, lam_r = vec[:, V_LAM:V_LAM + 4], vec[:, V_LI:V_LI + 16], vec[:, V_LR:V_LR + 16]
                    v.scalar_tensor_tensor(S(0)[:, 0:4], lam, -1.0, lam, ALU.mult, ALU.max).then_inc(lam_abs, 1)
                    v.tensor_scalar(S(3)[:, 0:8], vec[:, V_BA:V_BA + 8], 0.5, None, ALU.mult)
                    v.tensor_scalar(S(5)[:, 0:4], vec[:, V_BGLU + 4:V_BGLU + 8], 0.5, None, ALU.mult)
                    v.tensor_scalar(S(11), lam_r, -1e-4, None, ALU.min)
                    dve.wait_ge(dt_exp, 1)
                    link(v.tensor_tensor(S(19), lam_i, S(8), ALU.mult))
                    v.tensor_tensor(S(9), S(11), S(8), ALU.mult).then_inc(mag_arg, 1)
                    link(v.tensor_scalar(S(18), S(19), 1.0 / TWO_PI, None, ALU.mult))
                    link(v.tensor_scalar(S(18), S(18), ROUND, ROUND, ALU.add, ALU.subtract))
                    for part in (PI2_A, PI2_B, PI2_C):
                        link(v.scalar_tensor_tensor(S(19), S(18), -part, S(19), ALU.mult, ALU.add))
                    v.tensor_scalar(S(12), S(19), 3.1415925, -3.1415925, ALU.min, ALU.max).then_inc(th_ready, 1)
                    for k in range(KD):
                        dve.wait_ge(hhi_done, k // 2 * 2 + 2)
                        v.scalar_tensor_tensor(h_lo[:, k, :], M[:, k // 2, (k % 2) * T:(k % 2 + 1) * T],
                                               vec[:, V_NORM + k:V_NORM + k + 1], h_hi[:, k, :].bitcast(f32),
                                               ALU.mult, ALU.subtract).then_inc(hlo_done, 1)
                    dve.wait_ge(th_ready, 1)
                    link(v.tensor_scalar(S(19), S(12), 1.0 / TWO_PI, None, ALU.mult))
                    link(v.tensor_scalar(S(16), S(19), 4096.0, ROUND, ALU.mult, ALU.add))
                    link(v.tensor_scalar(S(16), S(16), ROUND, 1.0 / 4096.0, ALU.subtract, ALU.mult))
                    link(v.tensor_tensor(S(17), S(19), S(16), ALU.subtract))

                    def angles(p):
                        if p:
                            dve.wait_ge(trig_done, 3 * p)
                        for j in range(2):
                            i = v.tensor_scalar(ang_a[:, j, :], cst("time"), S(16)[:, 2 * p + j:2 * p + j + 1], None, ALU.mult)
                        link(i)
                        for j in range(2):
                            i = v.scalar_tensor_tensor(ang_s[:, j, :], cst("time"), S(17)[:, 2 * p + j:2 * p + j + 1],
                                                       ang_a[:, j, :], ALU.mult, ALU.add)
                        link(i)
                        link(v.tensor_scalar(ang_s, ang_s, ROUND, ROUND, ALU.add, ALU.subtract))
                        link(v.tensor_tensor(ang_a, ang_a, ang_s, ALU.subtract))
                        for j in range(2):
                            i = v.scalar_tensor_tensor(ang_a[:, j, :], cst("time"), S(17)[:, 2 * p + j:2 * p + j + 1],
                                                       ang_a[:, j, :], ALU.mult, ALU.add)
                        link(i)
                        v.tensor_scalar(ang_a, ang_a, 0.5, -0.5, ALU.min, ALU.max).then_inc(ang_ready, 1)

                    v.memset(cols(3072, 1024), 0.0)
                    dve.wait_ge(th_sin, 3)
                    dve.wait_ge(mag_exp, 1)
                    link(v.tensor_tensor(S(21), S(15), S(10), ALU.mult))
                    link(v.tensor_tensor(S(20), S(14), S(10), ALU.mult))
                    link(v.tensor_scalar(S(20), S(20), 1.0, None, ALU.subtract))
                    v.tensor_tensor(S(22), S(11), S(11), ALU.mult)
                    link(v.tensor_tensor(S(26), lam_i, lam_i, ALU.mult))
                    link(v.tensor_tensor(S(22), S(22), S(26), ALU.add))
                    link(v.reciprocal(S(23), S(22)))
                    v.tensor_tensor(S(24), S(20), S(11), ALU.mult)
                    v.tensor_tensor(S(25), S(21), S(11), ALU.mult)
                    v.tensor_tensor(S(26), S(21), lam_i, ALU.mult)
                    link(v.tensor_tensor(S(27), S(20), lam_i, ALU.mult))
                    v.tensor_tensor(S(24), S(24), S(26), ALU.add)
                    link(v.tensor_tensor(S(25), S(25), S(27), ALU.subtract))
                    v.tensor_tensor(S(24), S(24), S(23), ALU.mult)
                    link(v.tensor_tensor(S(25), S(25), S(23), ALU.mult))
                    dve.wait_ge(b_loaded, 32)
                    f_re = bc(S(24).unsqueeze(2), [P, NS5, 16])
                    f_im = bc(S(25).unsqueeze(2), [P, NS5, 16])
                    for f, (b0, b1, op) in enumerate(((0, 1, ALU.subtract), (1, 0, ALU.add))):
                        v.tensor_tensor(b_tmp[:, 0], b_nat[:, b0], f_re, ALU.mult)
                        link(v.tensor_tensor(b_tmp[:, 1], b_nat[:, b1], f_im, ALU.mult))
                        for g in range(2):
                            h = slice(64 * g, 64 * g + 64)
                            i = v.tensor_tensor(b_exp[h, f, :, g, :], b_tmp[h, 0], b_tmp[h, 1], op)
                        i.then_inc(b_ready, 1)
                        dve.wait_ge(b_ready, f + 1)
                    dve.wait_ge(c_loaded, 64)
                    for f in range(2):
                        v.tensor_tensor(c_nat[:, f], c_nat[:, f], bc(cst("group").unsqueeze(1).unsqueeze(3), [P, KB, 2, 64]),
                                        ALU.mult).then_inc(c_ready, 1)
                    angles(0)
                    dve.wait_ge(evac("u_s5"), ev("u_s5"))
                    v.tensor_tensor(flat(u_lo[:, :, :]), flat(u_s5[:, :, :]), flat(u_hi[:, :, :]).bitcast(f32), ALU.subtract).then_inc(s5_split, 1)
                    dve.wait_ge(bcT_ready, 1)
                    v.tensor_tensor(bT_lo[:, :, :, :].rearrange("p f q n -> p (f q n)"), MF[:, 1024:2048],
                                    bT_hi[:, :, :, :].rearrange("p f q n -> p (f q n)").bitcast(f32), ALU.subtract).then_inc(s5_split, 1)
                    def scan_pair(p, between=()):
                        b = p % 2
                        cos, sin = cos_sin[:, b, 0], cos_sin[:, b, 1]
                        t0, t1, t2, t3 = (s5_t[:, f] for f in range(4))
                        re, im = M[:, 0:2, 0:T], M[:, 0:2, T:2 * T]
                        if p:
                            dve.wait_ge(h_done, p)
                        dve.wait_ge(trig_done, 3 * p + 3)
                        dve.wait_ge(bu_done, p + 1)
                        v.tensor_tensor(t0, re, cos, ALU.mult)
                        v.tensor_tensor(t1, im, sin, ALU.mult)
                        v.tensor_tensor(t2, im, cos, ALU.mult)
                        v.tensor_tensor(t3, re, sin, ALU.mult).then_inc(bu_used, 1)
                        dve.wait_ge(bu_used, p + 1)
                        v.tensor_tensor(t0, t0, t1, ALU.add)
                        link(v.tensor_tensor(t2, t2, t3, ALU.subtract))
                        for j in range(2):
                            mag = bc(S(10)[:, 2 * p + j:2 * p + j + 1], [P, T])
                            v.tensor_tensor_scan(t1[:, j, :], mag, t0[:, j, :], 0.0, ALU.mult, ALU.add)
                            i = v.tensor_tensor_scan(t3[:, j, :], mag, t2[:, j, :], 0.0, ALU.mult, ALU.add)
                        link(i)
                        for name in between:
                            gate_times(name)
                        if p >= 2:
                            dve.wait_ge(y_done, p - 1)
                        h_re, h_im = s5_h[:, b, 0], s5_h[:, b, 1]
                        v.tensor_tensor(h_re, t1, cos, ALU.mult)
                        v.tensor_tensor(t0, t3, sin, ALU.mult)
                        v.tensor_tensor(h_im, t3, cos, ALU.mult)
                        link(v.tensor_tensor(t2, t1, sin, ALU.mult))
                        v.tensor_tensor(h_re, h_re, t0, ALU.subtract)
                        v.scalar_tensor_tensor(h_im, h_im, -1.0, t2, ALU.mult, ALU.subtract).then_inc(h_done, 1)

                    def s5_out(q):
                        dve.wait_ge(y_done, 2 * q + 2)
                        v.scalar_tensor_tensor(y_s5[:, q, :], u_s5[:, q, :], vec[:, V_D + q:V_D + q + 1],
                                               M[:, 2 + q % 2, 0:T], ALU.mult, ALU.add).then_inc(y_used, 1)

                    def gate_times(name):
                        i = BRANCHES.index(name)
                        g = flat(gate[:, i % 2])
                        dve.wait_ge(gate_tanh, i + 1)
                        v.scalar_tensor_tensor(g, g, 1.0, pr("gate_" + name)[:, :], ALU.add, ALU.mult).then_inc(evac("gate_" + name), 1)

                    def gated(name, y):
                        i = BRANCHES.index(name)
                        g = flat(gate[:, i % 2])
                        dve.wait_ge(evac("gate_" + name), ev("gate_" + name))
                        v.tensor_tensor(g, g, y, ALU.mult).then_inc(yg_ready, 1)

                    def lo_of_gated(name):
                        i = BRANCHES.index(name)
                        dve.wait_ge(yg_hi, i + 1)
                        v.tensor_tensor(flat(ys_lo[:, :, :]), gated_features(name), flat(ys_hi[:, :, :]).bitcast(f32),
                                        ALU.subtract).then_inc(yg_lo, 1)

                    def branch(name, half):
                        i = BRANCHES.index(name)
                        full = f"branch_{name}_{half}"
                        dst, m = merged[:, half, :], flat(mt[:, half])
                        dve.wait_ge(chunk_done, ch(full))
                        src = pr(full)[:, :]
                        if i == 0:
                            v.scalar_tensor_tensor(dst, m, 1.0, src, ALU.add, ALU.mult).then_inc(evac(full), 1)
                        else:
                            v.scalar_tensor_tensor(m, m, 1.0, src, ALU.add, ALU.mult).then_inc(evac(full), 1)
                            dve.wait_ge(evac(full), ev(full))
                            v.tensor_tensor(dst, dst, m, ALU.add).then_inc(mt_free, 1)

                    angles(1)
                    scan_pair(0)
                    angles(2)
                    e, s_, s2, q_, m_ = S(1)[:, 0:4], S(6)[:, 0:4], S(6)[:, 4:8], S(7)[:, 0:4], S(7)[:, 4:8]
                    dve.wait_ge(lam_exp, 1)
                    v.tensor_scalar(m_, lam, -1.0, 0.0, ALU.mult, ALU.max)
                    link(v.tensor_scalar(s_, e, 2.0, None, ALU.add))
                    link(v.reciprocal(s_, s_))
                    link(v.tensor_tensor(s_, s_, e, ALU.mult))
                    link(v.tensor_tensor(s2, s_, s_, ALU.mult))
                    link(v.tensor_scalar(q_, s2, 1.0 / 15.0, None, ALU.mult))
                    for n in (13, 11, 9, 7, 5, 3):
                        link(v.scalar_tensor_tensor(q_, q_, 1.0 / n, s2, ALU.add, ALU.mult))
                    link(v.scalar_tensor_tensor(q_, q_, 1.0, s_, ALU.add, ALU.mult))
                    link(v.scalar_tensor_tensor(q_, q_, 2.0, m_, ALU.mult, ALU.add))
                    v.tensor_scalar(S(4)[:, 0:4], q_, -0.5 * 8.0, None, ALU.mult)
                    link(v.tensor_scalar(S(4)[:, 4:8], q_, 0.5 * 8.0, None, ALU.mult))
                    dve.wait_ge(evac("cmp"), ev("cmp"))
                    v.memset(blocks[:, :, :, NCMP:16], 0.0)
                    for m in range(2):
                        for r8 in range(2):
                            src = x2[:, m].rearrange("p h (n r) -> p r h n", r=8)[:, :, :, r8:r8 + NCMP]
                            at = 16 * m + 8 * r8
                            i = v.tensor_tensor(blocks[:, at:at + 8, :, 0:NCMP], src,
                                                bc(pos[:, m, 8 * r8:8 * r8 + 8].unsqueeze(2).unsqueeze(3), [P, 8, 2, NCMP]), ALU.add)
                    i.then_inc(blk_ready, 1)
                    v.tensor_scalar(bgate[:, :, :], bgate[:, :, :], 1.0, 0.5, ALU.add, ALU.mult)
                    scan_pair(1)
                    angles(3)
                    scan_pair(2)
                    s5_out(0)
                    angles(4)
                    scan_pair(3)
                    angles(5)
                    scan_pair(4, ("s5",))
                    s5_out(1)
                    angles(6)
                    scan_pair(5)
                    gate_times("lru")
                    dve.wait_ge(evac("ck"), ev("ck"))
                    dve.wait_ge(evac("cv"), ev("cv"))
                    link(v.tensor_tensor(hid_q, hid_y, hid_y, ALU.mult))
                    link(v.tensor_scalar(hid_q, hid_q, 0.044715, 1.0, ALU.mult, ALU.add))
                    v.tensor_tensor(hid_q, hid_q, hid_y, ALU.mult).then_inc(hid_arg, 1)
                    angles(7)
                    scan_pair(6)
                    s5_out(2)
                    dve.wait_ge(hid_tanh, 1)
                    link(v.tensor_scalar(hid_q, hid_q, 0.5, 0.5, ALU.mult, ALU.add))
                    link(v.tensor_tensor(hid[:, :, :, :].rearrange("p m k n -> p (m k n)"), hid_q, hid_y, ALU.mult))
                    for k in range(2):
                        i = v.tensor_copy(hid8[:, k].rearrange("p (h g) n -> p h g n", h=NKV),
                                          bc(hid[:, 1, k].rearrange("p (h n) -> p h n", h=NKV).unsqueeze(2), [P, NKV, 4, 16]))
                    i.then_inc(hid_ready, 1)
                    scan_pair(7)
                    s5_out(3)

                    def rope_ret(n, name):
                        ro4 = merged[:, n].rearrange("p (a h c) -> p a h c", a=TT, h=NH_RET)
                        src = pr(name)[:, :].rearrange("p (a h c) -> p a h c", a=TT, h=NH_RET)
                        shape = [P, TT, NH_RET, 64]
                        cos = bc(cst("ret_cos").rearrange("p (a c) -> p a c", a=TT).unsqueeze(2), shape)
                        sin = bc(cst("ret_sin").rearrange("p (a c) -> p a c", a=TT).unsqueeze(2), shape)
                        lo, hi = slice(0, 64), slice(64, 128)
                        dve.wait_ge(chunk_done, ch(name))
                        if n:
                            dve.wait_ge(rope_ready, n)
                        v.tensor_tensor(ro4[:, :, :, lo], src[:, :, :, lo], cos, ALU.mult)
                        v.tensor_tensor(rope_t[:, 0], src[:, :, :, hi], sin, ALU.mult)
                        v.tensor_tensor(ro4[:, :, :, hi], src[:, :, :, hi], cos, ALU.mult)
                        v.tensor_tensor(rope_t[:, 1], src[:, :, :, lo], sin, ALU.mult).then_inc(evac(name), 1)
                        dve.wait_ge(evac(name), ev(name))
                        v.tensor_tensor(ro4[:, :, :, lo], ro4[:, :, :, lo], rope_t[:, 0], ALU.subtract)
                        v.tensor_tensor(ro4[:, :, :, hi], ro4[:, :, :, hi], rope_t[:, 1], ALU.add).then_inc(rope_ready, 1)

                    dve.wait_ge(y_used, KB)
                    yf = flat(y_s5[:, :, :])
                    link(v.tensor_tensor(gelu_t, yf, yf, ALU.mult))
                    link(v.tensor_scalar(gelu_t, gelu_t, 0.044715, 1.0, ALU.mult, ALU.add))
                    v.tensor_tensor(gelu_t, gelu_t, yf, ALU.mult).then_inc(z_arg, 1)
                    rope_ret(0, "ret_q")
                    dve.wait_ge(z_tanh, 1)
                    link(v.tensor_scalar(gelu_t, gelu_t, 0.5, 0.5, ALU.mult, ALU.add))
                    v.tensor_tensor(yf, yf, gelu_t, ALU.mult).then_inc(z_ready, 1)
                    dve.wait_ge(z_hi, 1)
                    v.tensor_tensor(flat(ys_lo[:, :, :]), yf, flat(ys_hi[:, :, :]).bitcast(f32), ALU.subtract).then_inc(z_lo, 1)

                    dve.wait_ge(evac("u_lru"), ev("u_lru"))

                    def tap(k, t):
                        return vec[:, V_CONV + KB * k + t:V_CONV + KB * k + t + 1]

                    for t in range(KB):
                        i = v.tensor_scalar(xc[:, t, :], u_lru[:, t, 0:T], tap(0, t), vec[:, V_CONVB + t:V_CONVB + t + 1],
                                            ALU.mult, ALU.add)
                    link(i)
                    for k in range(1, 4):
                        for t in range(KB):
                            i = v.scalar_tensor_tensor(xc[:, t, :], u_lru[:, t, k:k + T], tap(k, t), xc[:, t, :], ALU.mult, ALU.add)
                        if k < 3:
                            link(i)
                    i.then_inc(xc_ready, 1)
                    rope_ret(1, "ret_k")

                    def rope_nsa(x4):
                        shape = [P, TT, NHQ, 8]
                        cos = bc(cst("nsa_cos").rearrange("p (a c) -> p a c", a=TT).unsqueeze(2), shape)
                        sin = bc(cst("nsa_sin").rearrange("p (a c) -> p a c", a=TT).unsqueeze(2), shape)
                        x1, x2_ = x4[:, :, :, 0:8], x4[:, :, :, 8:16]
                        v.tensor_tensor(rope_n[:, 0], x1, cos, ALU.mult)
                        v.tensor_tensor(rope_n[:, 1], x2_, sin, ALU.mult)
                        v.tensor_tensor(rope_n[:, 2], x2_, cos, ALU.mult)
                        link(v.tensor_tensor(rope_n[:, 3], x1, sin, ALU.mult))
                        v.tensor_tensor(x1, rope_n[:, 0], rope_n[:, 1], ALU.subtract)
                        v.tensor_tensor(x2_, rope_n[:, 2], rope_n[:, 3], ALU.add).then_inc(nrope_ready, 1)

                    rope_nsa_kd = kd[:, :, :, :, :, :].rearrange("p a y h u d -> p a (y h u) d")
                    dve.wait_ge(evac("nsa_kv"), ev("nsa_kv"))
                    dve.wait_ge(rope_ready, 2)
                    rope_nsa(rope_nsa_kd)
                    dve.wait_ge(nrope_ready, 1)
                    dve.wait_ge(chunk_done, ch("glu_a"))
                    for t in range(KB):
                        i = v.tensor_scalar(glu_v[:, t * T:(t + 1) * T], pr("glu_a")[:, t * T:(t + 1) * T],
                                            vec[:, V_BGLU + t:V_BGLU + t + 1], 0.5, ALU.add, ALU.mult)
                    i.then_inc(evac("glu_a"), 1)
                    dve.wait_ge(lru_act, 4 * KB)
                    link(v.tensor_tensor(l_r, l_a, l_a, ALU.mult))
                    v.scalar_tensor_tensor(flat(l_i), flat(l_i), 1.0, flat(xc), ALU.add, ALU.mult)
                    v.scalar_tensor_tensor(flat(l_m), flat(l_r), 1.0, flat(l_m), ALU.add, ALU.mult).then_inc(lru_m2, 1)

                    dve.wait_ge(evac("glu_a"), ev("glu_a"))
                    dve.wait_ge(evac("glu_b"), ev("glu_b"))
                    link(v.scalar_tensor_tensor(glu_v, glu_t, 1.0, glu_v, ALU.add, ALU.mult))
                    gated("s5", glu_v)
                    lo_of_gated("s5")

                    def decay_scores(h):
                        dve.wait_ge(rs_done, h + 1)
                        if h >= 2:
                            dve.wait_ge(ro_done, h - 1)
                        dec = cst("decay").rearrange("p (h t) -> p h t", h=NH_RET)[:, h, :]
                        v.tensor_tensor(ret_s[:, h % 2, 0:T], M[:, h % 2, 0:T], dec, ALU.mult)
                        v.tensor_tensor(ret_s[:, h % 2, T:T + P], M[:, h % 2, T:T + P], dec[:, 0:P], ALU.mult).then_inc(rs_ready, 1)

                    dve.wait_ge(evac("nsa_q"), ev("nsa_q"))
                    dve.wait_ge(yg_ready, 1)
                    rope_nsa(nq4)
                    gate_times("ret")
                    decay_scores(0)
                    decay_scores(1)
                    branch("s5", 0)
                    dve.wait_ge(lru_sqrt, 1)
                    dve.wait_ge(nrope_ready, 2)
                    link(v.tensor_tensor(l_i, l_i, l_m, ALU.mult))
                    for t in range(KB):
                        i = v.tensor_tensor_scan(l_h[:, t, :], l_a[:, t, :], l_i[:, t, :], 0.0, ALU.mult, ALU.add)
                    link(i)
                    gated("lru", flat(l_h))
                    branch("s5", 1)
                    decay_scores(2)
                    decay_scores(3)
                    lo_of_gated("lru")
                    dve.wait_ge(ro_done, NH_RET)
                    o_ret = MF[:, 1024:2048].rearrange("p (i c) -> p i c", c=P)
                    for n in range(TT * NH_RET):
                        i = v.bn_stats(bn[:, n, :], o_ret[:, n, :])
                    link(i)
                    for n in range(TT * NH_RET):
                        i = v.bn_aggr(mv[:, n, :], bn[:, n, :])
                    link(i)
                    v.tensor_scalar(st[:, 80:88], mv[:, :, 1], EPS_RET, None, ALU.add).then_inc(rvar, 1)
                    dve.wait_ge(cw_done, 1)
                    kps = M[0:32, 0, 0:HD]
                    cc, ss = cst("cmp_cos")[0:32], cst("cmp_sin")[0:32]
                    v.tensor_copy(kc[:, :, :], bc(kps.unsqueeze(1), [32, 2, HD]))
                    v.tensor_tensor(kc_t[:, 0], kps[:, 0:8], cc, ALU.mult)
                    v.tensor_tensor(kc_t[:, 1], kps[:, 8:16], ss, ALU.mult)
                    v.tensor_tensor(kc_t[:, 2], kps[:, 8:16], cc, ALU.mult)
                    link(v.tensor_tensor(kc_t[:, 3], kps[:, 0:8], ss, ALU.mult))
                    v.tensor_tensor(kc[:, :, 0:8], bc(kc_t[:, 0].unsqueeze(1), [32, 2, 8]), bc(kc_t[:, 1].unsqueeze(1), [32, 2, 8]), ALU.subtract)
                    v.tensor_tensor(kc[:, :, 8:16], bc(kc_t[:, 2].unsqueeze(1), [32, 2, 8]), bc(kc_t[:, 3].unsqueeze(1), [32, 2, 8]), ALU.add).then_inc(kc_ready, 1)
                    v.tensor_tensor(vbd[:, :, :], bc(M[:, 0, HD:2 * HD].unsqueeze(1), [P, NHQ, HD]),
                                    bc(cst("head").unsqueeze(2), [P, NHQ, HD]), ALU.mult).then_inc(vbd_ready, 1)
                    dve.wait_ge(rrstd, 1)
                    for n in range(TT * NH_RET):
                        i = v.tensor_scalar(ro[:, n * P:(n + 1) * P], o_ret[:, n, :], mv[:, n, 0:1], st[:, 88 + n:89 + n],
                                            ALU.subtract, ALU.mult)
                    i.then_inc(rn_ready, 1)
                    dve.wait_ge(rn_ready, 1)
                    gated("ret", ro)
                    dve.wait_ge(cs_done, 2)
                    shape = [P, TT, 4, 16]
                    add = bc(cst("cmp_add").rearrange("p (a n) -> p a n", a=TT).unsqueeze(2), shape)
                    keep = bc(cst("cmp_keep").rearrange("p (a n) -> p a n", a=TT).unsqueeze(2), shape)
                    for e_ in range(2):
                        i = v.tensor_tensor(cmp_s[:, e_], M[:, e_, 0:P].rearrange("p (a h n) -> p a h n", a=TT, h=4), add, ALU.add)
                    link(i)
                    cs2 = cols(3072, 256).rearrange("p (i n) -> p i n", n=16)
                    link(v.tensor_reduce(st[:, 8:24], cs2, AX, ALU.max))
                    v.tensor_tensor(cs2, cs2, bc(st[:, 8:24].unsqueeze(2), [P, 16, 16]), ALU.subtract).then_inc(cs_sub, 1)
                    dve.wait_ge(cs_exp, 1)
                    for e_ in range(2):
                        i = v.tensor_tensor(cmp_s[:, e_], cmp_s[:, e_], keep, ALU.mult)
                    link(i)
                    link(v.tensor_reduce(st[:, 24:40], cs2, AX, ALU.add))
                    link(v.tensor_scalar(st[:, 24:40], st[:, 24:40], 1e-30, None, ALU.max))
                    link(v.reciprocal(st[:, 24:40], st[:, 24:40]))
                    coef = st[:, 24:40].rearrange("p (e a h) -> p e a h", e=2, a=TT)
                    gates0 = bgate[:, :, 0:8].rearrange("p a (h e) -> p e a h", e=2)
                    link(v.tensor_tensor(coef, coef, gates0, ALU.mult))
                    cp = cmp_p.rearrange("p (a h e n) -> p e a h n", a=TT, h=4, e=2)
                    for e_ in range(2):
                        i = v.tensor_tensor(cp[:, e_], cmp_s[:, e_], bc(coef[:, e_].unsqueeze(3), shape), ALU.mult)
                    i.then_inc(cp_ready, 1)

                    def attention_max(i):
                        dve.wait_ge(at_s, i + 1)
                        if i:
                            dve.wait_ge(at_pT, i)
                        causal = cst("causal")
                        v.tensor_tensor(prob[:, 0:1024].rearrange("p (b n) -> p b n", b=4),
                                        MF[:, 0:1024].rearrange("p (b n) -> p b n", b=4),
                                        bc(causal.unsqueeze(1), [P, 4, T]), ALU.add)
                        link(v.tensor_tensor(prob[:, 1024:1536].rearrange("p (b n) -> p b n", b=4),
                                             M[:, 2, :].rearrange("p (b n) -> p b n", b=4),
                                             bc(causal[:, P:T].unsqueeze(1), [P, 4, P]), ALU.add))
                        v.tensor_reduce(st[:, 40:44], prob[:, 0:1024].rearrange("p (b n) -> p b n", b=4), AX, ALU.max, negate=True)
                        v.tensor_reduce(st[:, 44:48], prob[:, 1024:1536].rearrange("p (b n) -> p b n", b=4), AX, ALU.max,
                                        negate=True).then_inc(at_max, 1)

                    def attention_out(i):
                        y, h = i // NKV, i % NKV
                        dve.wait_ge(at_exp, 8 * (i + 1))
                        link(v.reciprocal(st[:, 56:64], st[:, 48:56]))
                        cf = st[:, 64:72].rearrange("p (a g) -> p a g", a=TT)
                        link(v.tensor_tensor(cf, st[:, 56:64].rearrange("p (a g) -> p a g", a=TT),
                                             bgate[:, :, 8 * (y + 1) + 4 * h:8 * (y + 1) + 4 * h + 4], ALU.mult))
                        dve.wait_ge(at_o, i + 1)
                        src = M[:, 3, :].rearrange("p (a g d) -> p a g d", a=TT, g=4)
                        cfb = bc(cf.unsqueeze(3), [P, TT, 4, HD])
                        dst = no4[:, :, 4 * h:4 * h + 4, :]
                        if y == 0:
                            v.tensor_tensor(dst, src, cfb, ALU.mult).then_inc(at_no, 1)
                            dve.wait_ge(at_no, i + 1)
                        else:
                            tmp = att_t.rearrange("p (a g d) -> p a g d", a=TT, g=4)
                            link(v.tensor_tensor(tmp, src, cfb, ALU.mult))
                            v.tensor_tensor(dst, dst, tmp, ALU.add).then_inc(at_no, 1)

                    attention_max(0)
                    branch("lru", 0)
                    branch("lru", 1)
                    lo_of_gated("ret")
                    attention_out(0)
                    attention_max(1)
                    attention_out(1)
                    attention_max(2)
                    branch("ret", 0)
                    branch("ret", 1)
                    attention_out(2)
                    attention_max(3)
                    gate_times("nsa")
                    attention_out(3)
                    dve.wait_ge(co_done, 1)
                    dve.wait_ge(at_no, 4)
                    v.tensor_tensor(nq, nq, MF[:, 0:1024], ALU.add).then_inc(no_cmp, 1)
                    dve.wait_ge(no_cmp, 1)
                    gated("nsa", nq)
                    lo_of_gated("nsa")
                    branch("nsa", 0)
                    dve.wait_ge(nxt["vectors_loaded"], VECTORS_ALL)
                    expand_dt(nxt)
                    for half in range(2):
                        if half:
                            branch("nsa", 1)
                        dve.wait_ge(mhi_done, half + 1)
                        v.tensor_tensor(flat(h_lo[:, 4 * half:4 * half + 4, :]), MF[:, 1024 * half:1024 * half + 1024],
                                        flat(h_hi[:, 4 * half:4 * half + 4, :]).bitcast(f32), ALU.subtract).then_inc(mlo_done, 1)
                    dve.wait_ge(nxt["vecT"], 2)
                    keep_vectors(nxt)
                    dve.wait_ge(chunk_done, ch("out_0b"))
                    dst = x[:, :, 0:512]
                    v.scalar_tensor_tensor(dst, pr("out_0b")[:, :].rearrange("p (a n) -> p a n", a=TT), 0.25, dst,
                                           ALU.mult, ALU.add).then_inc(x_half, 1)
                    for t in range(TT):
                        dve.wait_ge(out_token, t + 1)
                        dst = x[:, t, 512:1024]
                        v.scalar_tensor_tensor(dst, pr("out_1b")[:, 512 * t:512 * t + 512], 0.25, dst,
                                               ALU.mult, ALU.add).then_inc(x_half, 1)
                    mean_square(dve, nxt)

                @block.tensor
                def _(pe):
                    mm = nc.tensor.matmul

                    def tr(dst, src, rows_=P):
                        return nc.tensor.transpose(dst, src, ident[0:rows_, 0:rows_])

                    def split_product(dst, left, right, start, stop):
                        for n, (i, j) in enumerate(((0, 0), (0, 1), (1, 0))):
                            last = mm(dst, left[i], right[j], start=start and n == 0, stop=stop and n == 2, skip_group_check=True)
                        return last

                    def chunk(name, part=2):
                        c = CHUNK[name]
                        _, kt, w = CHUNKS[c]
                        u0 = UNIT_END[c - 1] if c else 0
                        n_units = UNIT_END[c] - u0
                        kind = name.split("_")[0]
                        todo = part if isinstance(part, range) else {
                            0: range(n_units // 2), 1: range(n_units // 2, n_units), 2: range(n_units)}[part]
                        ps = pr(name)
                        if c >= 2 and todo[0] == 0 and name not in ("out_0b", "out_1b"):
                            pe.wait_ge(evacuated[c % 2], c // 2)
                        for n in todo:
                            u = u0 + n
                            _, k0, nk, _ = UNITS[u]
                            pe.wait_ge(lo_done, u + 1)
                            s = u % N_SPLIT
                            for kk in range(nk):
                                k = k0 + kk
                                st_, sp_ = k == 0, k == (KD if kind == "out" else kt) - 1
                                if name == "u_s5":
                                    pe.wait_ge(hlo_done, k + 1)

                                def wt(lo, hi):
                                    return tuple(t[:, s, kk * w + lo:kk * w + hi] for t in (w_hi, w_lo))

                                def ht(lo, hi, pair=(h_hi, h_lo)):
                                    return tuple(t[:, k, lo:hi] for t in pair)

                                if kind == "u" or name in ("gate_s5", "gate_lru"):
                                    for m in range(4):
                                        last = split_product(ps[:, m * T:(m + 1) * T], wt(m * P, (m + 1) * P), ht(0, T), st_ and m % 2 == 0, sp_)
                                elif kind == "glu":
                                    for m in range(4):
                                        last = split_product(ps[:, m * T:(m + 1) * T], wt(m * P, (m + 1) * P), ht(0, T, (ys_hi, ys_lo)), st_ and m % 2 == 0, sp_)
                                else:
                                    pair = (ys_hi, ys_lo) if kind == "branch" else (h_hi, h_lo)
                                    for t in range(TT):
                                        last = split_product(ps[:, 512 * t:512 * t + w], ht(t * P, (t + 1) * P, pair), wt(0, w), st_, sp_)
                            if n == n_units - 1:
                                last.then_inc(chunk_done, 1)
                            else:
                                last.then_inc(unit_used, 1)

                    def compress(m, name):
                        c = CHUNK[name]
                        pe.wait_ge(evacuated[c % 2], c // 2)
                        if m == 0:
                            pe.wait_ge(blk_ready, 1)
                        pe.wait_ge(cw1_loaded, 64 * (m + 1))
                        for k in range(16):
                            last = mm(pr(name)[0:32, 0:256], flat(nqT[:, :, :])[:, (16 * m + k) * 32:(16 * m + k + 1) * 32],
                                      cw1(k // 4)[:, (k % 4) * 256:(k % 4 + 1) * 256], start=k == 0, stop=k == 15)
                        last.then_inc(chunk_done, 1)

                    def hidden_T(m, name):
                        pe.wait_ge(hid_tm_ready, m + 1)
                        for k in range(2):
                            last = tr(pr(name)[:, 512 + 32 * k:544 + 32 * k], hid_tm[:, m, k * P:(k + 1) * P], 32)
                        last.then_inc(hidT_done, 1)

                    def last_chunk():
                        u0 = UNIT_END[CHUNK["out_0b"]]
                        for t in range(TT):
                            for u in range(u0, NU):
                                if t == 0:
                                    pe.wait_ge(lo_done, u + 1)
                                for kk in range(2):
                                    k = UNITS[u][1] + kk
                                    last = split_product(pr("out_1b")[:, 512 * t:512 * t + 512],
                                                         tuple(h[:, k, t * P:(t + 1) * P] for h in (h_hi, h_lo)),
                                                         tuple(w[:, u % N_SPLIT, kk * 512:kk * 512 + 512] for w in (w_hi, w_lo)),
                                                         False, k == KD - 1)
                            last.then_inc(out_token, 1)

                    for k in range(KD):
                        if k % 4 == 0:
                            pe.wait_ge(x_norm, TT * (k // 4 + 1))
                        for t in range(TT):
                            last = tr(M[:, k // 2, (k % 2) * T + t * P:(k % 2) * T + (t + 1) * P], merged[:, t, k * P:(k + 1) * P])
                        if k % 2:
                            last.then_inc(xT_done, 1)
                    chunk("u_s5")
                    pe.wait_ge(hlo_done, KD)
                    pe.wait_ge(b_ready, 2)
                    for f in range(2):
                        for q in range(KB):
                            last = tr(M[:, 2 + f, q * P:(q + 1) * P],
                                      b_exp[:, f, 4 * q:4 * q + 4].rearrange("p s g c -> p (s g c)"))
                    last.then_inc(bT_done, 1)
                    pe.wait_ge(c_ready, 2)
                    for f in range(2):
                        for q in range(KB):
                            last = tr(M[:, f, q * P:(q + 1) * P], c_nat[:, f, q].rearrange("p g n -> p (g n)"))
                    last.then_inc(cT_done, 1)

                    def state_inputs(p):
                        if p == 0:
                            pe.wait_ge(bcT_ready, 2)
                            pe.wait_ge(s5_split, 2)
                        else:
                            pe.wait_ge(bu_used, p)
                        q = p // 2
                        for j in range(2):
                            r = slice(32 * (2 * (p % 2) + j), 32 * (2 * (p % 2) + j) + 32)
                            for f in range(2):
                                last = split_product(M[:, j, f * T:(f + 1) * T], (bT_hi[r, f, q, :], bT_lo[r, f, q, :]),
                                                     (u_hi[r, q, :], u_lo[r, q, :]), True, True)
                        last.then_inc(bu_done, 1)

                    def state_outputs(p):
                        q = p // 2
                        pe.wait_ge(h_done, p + 1)
                        if q >= 2 and p % 2 == 0:
                            pe.wait_ge(y_used, q - 1)
                        for j in range(2):
                            r = slice(32 * (2 * (p % 2) + j), 32 * (2 * (p % 2) + j) + 32)
                            dst = M[r, 2 + q % 2, 0:T]
                            for f in range(2):
                                last = mm(dst, cT[:, f, q, r], s5_h[:, p % 2, f, j, :], start=f == 0, stop=f == 1)
                        last.then_inc(y_done, 1)

                    chunk("cmp")
                    state_inputs(0)
                    chunk("u_lru", 0)
                    pe.wait_ge(cmp_read, 2)
                    for m in range(2):
                        for t in range(TT):
                            at = (2 * m + t) * P
                            last = tr(pr("cmp")[:, at:at + P], cmp_tm[:, t, m * P:(m + 1) * P])
                    last.then_inc(cmpT_done, 1)
                    chunk("u_lru", 1)
                    chunk("ret_v", 0)
                    state_inputs(1)
                    chunk("ret_v", 1)
                    state_outputs(0)
                    chunk("nsa_kv", 0)
                    state_inputs(2)
                    chunk("nsa_kv", 1)
                    state_outputs(1)
                    state_inputs(3)
                    compress(0, "ck")
                    state_outputs(2)
                    chunk("gate_s5", 0)
                    hidden_T(0, "ck")
                    state_inputs(4)
                    chunk("gate_s5", 1)
                    state_outputs(3)
                    compress(1, "cv")
                    state_inputs(5)
                    chunk("gate_lru", 0)
                    hidden_T(1, "cv")
                    chunk("gate_lru", 1)
                    state_outputs(4)
                    chunk("merge_s5_0", 0)
                    state_inputs(6)
                    chunk("merge_s5_0", 1)
                    state_outputs(5)
                    chunk("merge_s5_1", 0)
                    state_inputs(7)
                    chunk("merge_s5_1", 1)
                    state_outputs(6)
                    chunk("ret_q")
                    state_outputs(7)
                    def blocks_T(at, src):
                        for n in range(4):
                            for t in range(TT):
                                last = tr(MF[:, at + n * T + t * P:at + n * T + (t + 1) * P], src[:, (4 * t + n) * P:(4 * t + n + 1) * P])
                        return last

                    chunk("ret_k")
                    pe.wait_ge(y_used, KB)
                    pe.wait_ge(rope_ready, 1)
                    blocks_T(0, merged[:, 0]).then_inc(qkT_done, 1)
                    chunk("nsa_q")
                    pe.wait_ge(xc_ready, 1)
                    pe.wait_ge(wl_loaded, 64)
                    pe.wait_ge(qkT_ready, 1)
                    for f, w in enumerate((wa, wx)):
                        for t in range(KB):
                            last = mm(MF[:, f * 1024 + t * T:f * 1024 + (t + 1) * T], w[:, t, :], xc[:, t, :], start=True, stop=True)
                    last.then_inc(lru_mm, 1)
                    pe.wait_ge(z_lo, 1)
                    chunk("glu_a")
                    pe.wait_ge(rope_ready, 2)
                    pe.wait_ge(lru_act, 2 * KB)
                    blocks_T(1024, merged[:, 1]).then_inc(qkT_done, 1)
                    chunk("glu_b")
                    pe.wait_ge(nrope_ready, 1)
                    pe.wait_ge(qkT_ready, 1)
                    blocks_T(0, kd[:, :, :, :, :, :].rearrange("p a y h u d -> p (a y h u d)")).then_inc(nT_done, 1)
                    chunk("gate_ret")
                    pe.wait_ge(qkT_ready, 2)
                    pe.wait_ge(nT_ready, 1)

                    def ret_scores(h):
                        if h >= 2:
                            pe.wait_ge(rs_ready, h - 1)
                        mm(M[:, h % 2, 0:T], kT[:, h, 0:P], qT[:, h, :], start=True, stop=True)
                        mm(M[:, h % 2, T:T + P], kT[:, h, P:T], qT[:, h, P:T], start=True, stop=True).then_inc(rs_done, 1)

                    def ret_out(h):
                        pe.wait_ge(rs_ready, h + 1)
                        e = slice(h * P, (h + 1) * P)
                        mm(M[:, 2, e], ret_s[:, h % 2, 0:P], ret_v[:, 0, e], start=True, stop=True)
                        mm(M[:, 3, e], ret_s[:, h % 2, P:T], ret_v[:, 0, e], start=True, stop=False)
                        mm(M[:, 3, e], ret_s[:, h % 2, T:T + P], ret_v[:, 1, e], start=False, stop=True).then_inc(ro_done, 1)

                    ret_scores(0)
                    ret_scores(1)
                    pe.wait_ge(yg_lo, 1)
                    chunk("branch_s5_0")
                    pe.wait_ge(nrope_ready, 2)
                    blocks_T(1024, nq).then_inc(nT_done, 1)
                    chunk("branch_s5_1")
                    pe.wait_ge(nT_ready, 2)
                    ret_out(0)
                    ret_out(1)
                    ret_scores(2)
                    ret_scores(3)
                    chunk("merge_lru_0", 0)
                    ret_out(2)
                    ret_out(3)
                    pe.wait_ge(cw_loaded, 32)
                    pe.wait_ge(hid_ready, 1)
                    for k in range(2):
                        mm(M[0:32, 0, 0:HD], hid[:, 0, k, :], cw2[:, 0, k, :], start=k == 0, stop=k == 1)
                    for k in range(2):
                        last = mm(M[:, 0, HD:2 * HD], hid8[:, k].rearrange("p h n -> p (h n)"), cw2[:, 1, k, :], start=k == 0, stop=k == 1)
                    last.then_inc(cw_done, 1)
                    chunk("merge_lru_0", 1)
                    pe.wait_ge(kc_ready, 1)
                    tr(M[:, 1, 0:32], kc[:, :, :].rearrange("p u d -> p (u d)"), 32).then_inc(kcT_done, 1)

                    def compressed_scores(e):
                        r = slice(64 * e, 64 * e + 64)
                        for t in range(TT):
                            for h in range(4):
                                at = t * 64 + h * 16
                                last = mm(M[:, e, at:at + 16], nqT[r, h, t * P:(t + 1) * P], kcT[r, (h // 2) * 16:(h // 2) * 16 + 16],
                                          start=True, stop=True)
                        last.then_inc(cs_done, 1)

                    chunk("merge_lru_1", range(0, 1))
                    pe.wait_ge(vbd_ready, 1)
                    pe.wait_ge(kcT_ready, 1)
                    compressed_scores(0)
                    chunk("merge_lru_1", range(1, 2))
                    pe.wait_ge(yg_ready, 3)
                    blocks_T(1024, flat(gate[:, 0])).then_inc(rnT_done, 1)
                    compressed_scores(1)
                    chunk("merge_lru_1", 1)
                    pe.wait_ge(cp_ready, 1)
                    pe.wait_ge(yr_ready, 1)
                    for t in range(TT):
                        last = tr(M[:, 3, t * P:(t + 1) * P], cmp_p[:, t * P:(t + 1) * P])
                    last.then_inc(cpT_done, 1)

                    def attention_scores(i):
                        h = i % NKV
                        if i:
                            pe.wait_ge(at_pT_ready, i)
                        for e in range(2):
                            r = slice(64 * e, 64 * e + 64)
                            def small_():
                                for n in range(2):
                                    at = (2 * e + n) * P
                                    last_ = mm(M[:, 2, at:at + P], nqT[r, 2 * h + n, 0:P], nkT[r, i, 0:P], start=True, stop=True)
                                return last_
                            if e == 0:
                                small_().then_inc(at_even, 1)
                            for n in range(2):
                                mm(M[:, e, n * T:(n + 1) * T], nqT[r, 2 * h + n, P:T], nkT[r, i, :], start=True, stop=True)
                            if e == 1:
                                pe.wait_ge(at_even, i + 1)
                                last = small_()
                        last.then_inc(at_s, 1)

                    def attention_T(i):
                        pe.wait_ge(at_exp, 8 * (i + 1))
                        for b in range(12):
                            last = tr(MF[:, b * P:(b + 1) * P], prob[:, b * P:(b + 1) * P])
                        last.then_inc(at_pT, 1)

                    def attention_product(i):
                        pe.wait_ge(at_pT_ready, i + 1)
                        if i:
                            pe.wait_ge(at_no, i)
                        for b, g in enumerate((0, 2, 1, 3)):
                            mm(M[:, 3, g * HD:(g + 1) * HD], probT[:, 8 + b, :], nv[:, 0, i, :], start=True, stop=True)
                            mm(M[:, 3, 256 + g * HD:256 + (g + 1) * HD], probT[:, 2 * b, :], nv[:, 0, i, :], start=True, stop=False)
                            last = mm(M[:, 3, 256 + g * HD:256 + (g + 1) * HD], probT[:, 2 * b + 1, :], nv[:, 1, i, :], start=False, stop=True)
                        last.then_inc(at_o, 1)

                    attention_scores(0)
                    pe.wait_ge(yg_lo, 2)
                    chunk("branch_lru_0")
                    chunk("branch_lru_1")
                    attention_T(0)
                    chunk("merge_ret_0", 0)
                    pe.wait_ge(cpT_ready, 1)
                    attention_product(0)
                    attention_scores(1)
                    chunk("merge_ret_0", 1)
                    chunk("merge_ret_1", 0)
                    attention_T(1)
                    chunk("merge_ret_1", 1)
                    attention_product(1)
                    attention_scores(2)
                    pe.wait_ge(yg_lo, 3)
                    chunk("branch_ret_0")
                    chunk("branch_ret_1")
                    attention_T(2)
                    chunk("gate_nsa", 0)
                    attention_product(2)
                    attention_scores(3)
                    chunk("gate_nsa", 1)
                    chunk("merge_nsa_0", 0)
                    attention_T(3)
                    chunk("merge_nsa_0", 1)
                    attention_product(3)
                    pe.wait_ge(at_pT_ready, 4)
                    for t in range(TT):
                        last = mm(M[:, t, :], cmp_pT[:, t * P:(t + 1) * P], vbd[:, :, :].rearrange("p h d -> p (h d)"), start=True, stop=True)
                    last.then_inc(co_done, 1)
                    chunk("merge_nsa_1", 0)
                    pe.wait_ge(yg_ready, 4)
                    blocks_T(1024, flat(gate[:, 1])).then_inc(noT_done, 1)
                    chunk("merge_nsa_1", 1)
                    pe.wait_ge(yg_lo, 4)
                    chunk("branch_nsa_0")
                    chunk("branch_nsa_1", 0)
                    pe.wait_ge(mt_free, 5)
                    blocks_T(0, merged[:, 0]).then_inc(mT_done, 1)
                    chunk("branch_nsa_1", 1)
                    pe.wait_ge(mlo_done, 1)
                    chunk("out_0a")
                    pe.wait_ge(mt_free, 6)
                    blocks_T(1024, merged[:, 1]).then_inc(mT_done, 1)
                    chunk("out_1a")
                    pe.wait_ge(nxt["dt_rows"], 1)
                    turn_vectors(nxt)
                    pe.wait_ge(mlo_done, 2)
                    chunk("out_0b")
                    last_chunk()

            with nc.Block() as block:
                @block.gpsimd
                def _(gp):
                    gp.sem_clear(range(sems[0].num, sems[-1].num + 1))

        with nc.Block() as block:
            @block.sync
            def _(sp):
                for t in range(TT):
                    sp.wait_ge(normed, t + 1)
                    sp.dma_start(out[0, t * P:(t + 1) * P, :], merged[:, t, :]).then_inc(stored, 16)
                sp.wait_ge(stored, 16 * TT)

            @block.vector
            def _(dve):
                for t in range(TT):
                    nc.vector.scalar_tensor_tensor(merged[:, t, :], x[:, t, :], st[:, 2 + t:3 + t], g_row,
                                                   ALU.mult, ALU.mult).then_inc(normed, 1)


_INS = ["x", "norm_g", "w_in", "lru_conv_w", "lru_conv_b", "lru_wa", "lru_ba", "lru_wx", "lru_bx", "lru_lambda",
        "s5_lambda_re", "s5_lambda_im", "s5_b_re", "s5_b_im", "s5_c_re", "s5_c_im", "s5_log_dt", "s5_d",
        "s5_w_glu", "s5_b_glu", "nsa_pos_k", "nsa_pos_v", "nsa_ck_w1", "nsa_ck_w2", "nsa_cv_w1", "nsa_cv_w2",
        "w_branch", "w_out", "final_norm_g"]


def kernel(**inputs):
    import numpy as _np
    import concourse.bacc as _bacc
    from concourse import mybir as _mybir
    from concourse.bass_utils import run_bass_kernel_spmd as _run

    nc = _bacc.Bacc("TRN2", target_bir_lowering=False, num_devices=1)
    arrays = {name: _np.ascontiguousarray(inputs[name]) for name in _INS}
    arrays["constants"] = shape_constants()
    aps = {n: nc.dram_tensor(f"in_{n}", v.shape, _mybir.dt.from_np(v.dtype), kind="ExternalInput").ap()
           for n, v in arrays.items()}
    result = nc.dram_tensor("out", (1, T, D), _mybir.dt.float32, kind="ExternalOutput").ap()
    hybrid_trunk(nc, aps, result)
    r = _run(nc, [{f"in_{n}": v for n, v in arrays.items()}], core_ids=[0])
    return r.results[0]["out"]
```
